# Optimizing a Trainium2 kernel written in Bass

```python
import math
import jax
import jax.numpy as jnp
from jax import lax
import numpy as np
import jax, jax.numpy as jnp

D_MODEL = 1024
BATCH = 1
SEQ = 512
DEPTH = 1

N_MIXERS = 4
QBLOCK = 128
NORM_EPS = 1e-6
NEG_BIG = -1e30
F32 = jnp.float32
DA_HEADS = 8
DA_HEAD_DIM = 64
DA_IN_WIDTH = 3 * DA_HEADS * 2 * DA_HEAD_DIM
NSA_HEADS = 16
NSA_KV_GROUPS = 2
NSA_HEAD_DIM = 64
NSA_QBLOCK = 64
CMP_BLOCK = 32
CMP_STRIDE = 16
CMP_HIDDEN = 256
SEL_BLOCK = 64
N_SELECT = 8
WINDOW = 512
NSA_IN_WIDTH = NSA_HEADS * NSA_HEAD_DIM + 6 * NSA_KV_GROUPS * NSA_HEAD_DIM + 3 * NSA_HEADS
GDN_HEADS = 8
GDN_HEAD_DIM = 128
GDN_CHUNK = 64
GDN_IN_WIDTH = 4 * GDN_HEADS * GDN_HEAD_DIM + 2 * GDN_HEADS
CONV_WIDTH = 4
LRU_WIDTH = D_MODEL
LRU_BLOCKS = 4
LRU_C = 8.0
N_GROUPS = 4
EXPERTS_PER_GROUP = 4
N_EXPERTS = N_GROUPS * EXPERTS_PER_GROUP
TOP_K_IN_GROUP = 2
D_EXPERT = 512


def rmsnorm(x, gain):
    xf = x.astype(F32)
    y = xf * lax.rsqrt(jnp.mean(xf * xf, -1, keepdims=True) + NORM_EPS)
    return (y * gain.astype(F32)).astype(x.dtype)

def l2norm(x):
    xf = x.astype(F32)
    return xf * lax.rsqrt(jnp.sum(xf * xf, -1, keepdims=True) + NORM_EPS)

def alibi_slopes(n):
    return jnp.asarray(2.0 ** (-8.0 * np.arange(1, n + 1) / n), dtype=F32)

def causal_depthwise_conv(x, w):
    k = w.shape[0]
    xp = jnp.pad(x, ((0, 0), (k - 1, 0), (0, 0)))
    return lax.conv_general_dilated(xp, w[:, None, :].astype(x.dtype), window_strides=(1,), padding='VALID',
                                    dimension_numbers=('NWC', 'WIO', 'NWC'), feature_group_count=x.shape[-1])

def diff_attention(x, w_in, q_gain, k_gain, lq1, lk1, lq2, lk2, subln, w_out, lambda_init):
    B, T, _ = x.shape
    H, dh = DA_HEADS, DA_HEAD_DIM
    q, k, v = jnp.split(x @ w_in, [2 * H * dh, 4 * H * dh], axis=-1)
    q = rmsnorm(q.reshape(B, T, H, 2, dh), q_gain) * (dh ** -0.5)
    k = rmsnorm(k.reshape(B, T, H, 2, dh), k_gain)
    v = v.reshape(B, T, H, 2 * dh)
    lam = (jnp.exp(jnp.sum(lq1.astype(F32) * lk1.astype(F32)))
           - jnp.exp(jnp.sum(lq2.astype(F32) * lk2.astype(F32))) + lambda_init)
    slopes = alibi_slopes(H)
    outs = []
    for s in range(0, T, QBLOCK):
        e = s + QBLOCK
        sc = jnp.einsum('bqhcd,bkhcd->bhcqk', q[:, s:e], k[:, :e]).astype(F32)
        dist = (jnp.arange(s, e)[:, None] - jnp.arange(e)[None, :]).astype(F32)
        sc = jnp.where(dist >= 0, sc - slopes[:, None, None, None] * dist, -jnp.inf)
        p = jax.nn.softmax(sc, axis=-1)
        pd = p[:, :, 0] - lam * p[:, :, 1]
        outs.append(jnp.einsum('bhqk,bkhe->bqhe', pd.astype(v.dtype), v[:, :e]))
    o = rmsnorm(jnp.concatenate(outs, axis=1), subln) * (1.0 - lambda_init)
    return o.reshape(B, T, H * 2 * dh) @ w_out

def nsa_attention(x, w_in, q_gain, k_gains, cmp_pos, cmp_w1, cmp_w2, w_out):
    B, T, _ = x.shape
    H, G, dh = NSA_HEADS, NSA_KV_GROUPS, NSA_HEAD_DIM
    P = H // G
    kvw = G * dh
    cuts = np.cumsum([H * dh] + [kvw] * 6).tolist()
    q, kc, vc, ks, vs, kw, vw, gl = jnp.split(x @ w_in, cuts, axis=-1)
    q = (rmsnorm(q.reshape(B, T, H, dh), q_gain) * (dh ** -0.5)).reshape(B, T, G, P, dh)
    gates = jax.nn.sigmoid(gl.reshape(B, T, G, P, 3))
    n_cmp = (T - CMP_BLOCK) // CMP_STRIDE + 1
    cidx = np.arange(n_cmp)[:, None] * CMP_STRIDE + np.arange(CMP_BLOCK)[None, :]

    def compress(t, c):
        tb = t.reshape(B, T, G, dh)[:, cidx] + cmp_pos[c][:, None, :]
        tb = tb.transpose(0, 1, 3, 2, 4).reshape(B, n_cmp, G, CMP_BLOCK * dh)
        return jax.nn.silu(tb @ cmp_w1[c]) @ cmp_w2[c]

    kcmp = rmsnorm(compress(kc, 0), k_gains[0])
    vcmp = compress(vc, 1)
    cmp_end = jnp.asarray(cidx[:, -1])
    n_sel = T // SEL_BLOCK
    k_top = min(N_SELECT, n_sel)

    def to_blocks(t):
        return t.reshape(B, n_sel, SEL_BLOCK, G, dh).transpose(0, 3, 1, 2, 4)

    ksb = to_blocks(rmsnorm(ks.reshape(B, T, G, dh), k_gains[1]))
    vsb = to_blocks(vs)
    cs = np.arange(n_cmp) * CMP_STRIDE
    ss0 = np.arange(n_sel) * SEL_BLOCK
    overlap = jnp.asarray(((cs[:, None] < ss0[None, :] + SEL_BLOCK)
                           & (cs[:, None] + CMP_BLOCK > ss0[None, :])).astype(np.float32))
    kwin = rmsnorm(kw.reshape(B, T, G, dh), k_gains[2])
    vwin = vw.reshape(B, T, G, dh)
    slopes = alibi_slopes(H).reshape(G, P)
    gather = jax.vmap(jax.vmap(lambda blocks, idx: blocks[idx]))
    blk_ids = jnp.arange(n_sel)
    outs = []
    for s in range(0, T, NSA_QBLOCK):
        e = s + NSA_QBLOCK
        qb = q[:, s:e]
        tpos = jnp.arange(s, e)
        dist_c = (tpos[:, None] - cmp_end[None, :]).astype(F32)
        valid_c = dist_c >= 0
        sc = jnp.einsum('bqgpd,bcgd->bgpqc', qb, kcmp).astype(F32) - slopes[:, :, None, None] * dist_c
        p_c = jax.nn.softmax(jnp.where(valid_c, sc, NEG_BIG), -1) * valid_c
        o_cmp = jnp.einsum('bgpqc,bcgd->bqgpd', p_c.astype(vcmp.dtype), vcmp)
        imp = jnp.einsum('bgpqc,cn->bgqn', p_c, overlap)
        qblk = tpos // SEL_BLOCK
        forced = (blk_ids[None, :] == 0) | (blk_ids[None, :] == qblk[:, None])
        future = blk_ids[None, :] > qblk[:, None]
        score = jnp.where(forced, 1e4, jnp.where(future, -1.0, imp))
        _, sel = lax.top_k(score, k_top)
        kg = gather(ksb, sel)
        vg = gather(vsb, sel)
        dist_s = (tpos[None, None, :, None, None]
                  - (sel[..., None] * SEL_BLOCK + jnp.arange(SEL_BLOCK))).astype(F32)
        ssc = (jnp.einsum('bqgpd,bgqksd->bgpqks', qb, kg).astype(F32)
               - slopes[None, :, :, None, None, None] * dist_s[:, :, None])
        ssc = jnp.where(dist_s[:, :, None] >= 0, ssc, -jnp.inf)
        p_s = jax.nn.softmax(ssc.reshape(B, G, P, NSA_QBLOCK, k_top * SEL_BLOCK), -1)
        o_sel = jnp.einsum('bgpqn,bgqnd->bqgpd', p_s.astype(vg.dtype),
                           vg.reshape(B, G, NSA_QBLOCK, k_top * SEL_BLOCK, dh))
        ws = max(0, s - WINDOW + 1)
        dist_w = (tpos[:, None] - jnp.arange(ws, e)[None, :]).astype(F32)
        valid_w = (dist_w >= 0) & (dist_w < WINDOW)
        swc = jnp.einsum('bqgpd,bkgd->bgpqk', qb, kwin[:, ws:e]).astype(F32) - slopes[:, :, None, None] * dist_w
        p_w = jax.nn.softmax(jnp.where(valid_w, swc, -jnp.inf), -1)
        o_win = jnp.einsum('bgpqk,bkgd->bqgpd', p_w.astype(vwin.dtype), vwin[:, ws:e])
        gb = gates[:, s:e]
        outs.append(gb[..., 0:1] * o_cmp + gb[..., 1:2] * o_sel + gb[..., 2:3] * o_win)
    o = jnp.concatenate(outs, axis=1).reshape(B, T, H * dh)
    return o @ w_out

def gated_deltanet(x, w_in, conv_w, a_log, dt_bias, out_gain, w_out):
    B, T, _ = x.shape
    H, dk = GDN_HEADS, GDN_HEAD_DIM
    C = GDN_CHUNK
    n = T // C
    W = H * dk
    qkv, z, b, a = jnp.split(x @ w_in, [3 * W, 4 * W, 4 * W + H], axis=-1)
    qkv = jax.nn.silu(causal_depthwise_conv(qkv, conv_w))
    q, k, v = jnp.split(qkv, 3, axis=-1)
    q = l2norm(q.reshape(B, T, H, dk)) * (dk ** -0.5)
    k = l2norm(k.reshape(B, T, H, dk))
    v = v.reshape(B, T, H, dk).astype(F32)
    beta = jax.nn.sigmoid(b.astype(F32))
    g = -jnp.exp(a_log.astype(F32)) * jax.nn.softplus(a.astype(F32) + dt_bias.astype(F32))

    def chunks(t):
        return jnp.moveaxis(t.reshape(B, n, C, H, *t.shape[3:]), 3, 1)

    q, k, v, beta, g = chunks(q), chunks(k), chunks(v), chunks(beta), chunks(g)
    gc = jnp.cumsum(g, axis=-1)
    tril = jnp.tril(jnp.ones((C, C), bool))
    decay = jnp.exp(jnp.where(tril, gc[..., :, None] - gc[..., None, :], -jnp.inf))
    kb = k * beta[..., None]
    lmat = jnp.einsum('bhnid,bhnjd->bhnij', kb, k) * decay * jnp.tril(jnp.ones((C, C), F32), -1)
    ia = lmat + jnp.eye(C, dtype=F32)
    u = lax.linalg.triangular_solve(ia, v * beta[..., None], left_side=True, lower=True, unit_diagonal=True)
    w = lax.linalg.triangular_solve(ia, kb * jnp.exp(gc)[..., None], left_side=True, lower=True, unit_diagonal=True)
    aqk = jnp.einsum('bhnid,bhnjd->bhnij', q, k) * decay

    def step(S, inp):
        qc, kc, uc, wc, gcc, aq = inp
        v_new = uc - jnp.einsum('bhck,bhkv->bhcv', wc, S)
        o = (jnp.einsum('bhck,bhkv->bhcv', qc * jnp.exp(gcc)[..., None], S)
             + jnp.einsum('bhij,bhjv->bhiv', aq, v_new))
        glast = gcc[..., -1:]
        S = S * jnp.exp(glast)[..., None] + jnp.einsum('bhck,bhcv->bhkv', kc * jnp.exp(glast - gcc)[..., None], v_new)
        return S, o

    xs = (jnp.moveaxis(q, 2, 0), jnp.moveaxis(k, 2, 0), jnp.moveaxis(u, 2, 0),
          jnp.moveaxis(w, 2, 0), jnp.moveaxis(gc, 2, 0), jnp.moveaxis(aqk, 2, 0))
    _, o = lax.scan(step, jnp.zeros((B, H, dk, dk), F32), xs)
    o = o.transpose(1, 0, 3, 2, 4).reshape(B, T, H, dk)
    o = rmsnorm(o, out_gain) * jax.nn.silu(z.reshape(B, T, H, dk).astype(F32))
    return o.astype(x.dtype).reshape(B, T, W) @ w_out

def rg_lru_block(x, w_in, conv_w, conv_b, w_a, b_a, w_x, b_x, lam, w_out):
    B, T, _ = x.shape
    gate, rec = jnp.split(x @ w_in, 2, axis=-1)
    gate = jax.nn.gelu(gate, approximate=True)
    xr = causal_depthwise_conv(rec, conv_w) + conv_b
    xb = xr.reshape(B, T, LRU_BLOCKS, -1)
    r = jax.nn.sigmoid((jnp.einsum('btnc,ncd->btnd', xb, w_a).reshape(B, T, -1) + b_a).astype(F32))
    i = jax.nn.sigmoid((jnp.einsum('btnc,ncd->btnd', xb, w_x).reshape(B, T, -1) + b_x).astype(F32))
    log_a = -LRU_C * r * jax.nn.softplus(-lam.astype(F32))
    a = jnp.exp(log_a)
    bterm = jnp.sqrt(1.0 - jnp.exp(2.0 * log_a)) * (i * xr.astype(F32))
    _, h = lax.associative_scan(lambda c1, c2: (c1[0] * c2[0], c2[0] * c1[1] + c2[1]), (a, bterm), axis=1)
    return (h.astype(x.dtype) * gate) @ w_out

def hier_moe(x, w_group, b_group, w_router, b_router, w_gate, w_up, w_down):
    B, T, D = x.shape
    n_tok = B * T
    xt = x.reshape(n_tok, D)
    logit_g = (xt @ w_group + b_group).astype(F32)
    prob_g = jax.nn.softmax(logit_g, -1)
    g_sel = jnp.argmax(logit_g, -1)
    gate_g = jnp.take_along_axis(prob_g, g_sel[:, None], -1)
    logit_e = (xt @ w_router + b_router).astype(F32).reshape(n_tok, N_GROUPS, EXPERTS_PER_GROUP)
    logit_e = jnp.take_along_axis(logit_e, g_sel[:, None, None], 1)[:, 0]
    top_v, top_i = lax.top_k(jax.nn.softmax(logit_e, -1), TOP_K_IN_GROUP)
    top_v = top_v / jnp.sum(top_v, -1, keepdims=True)
    w_in_group = jnp.sum(jax.nn.one_hot(top_i, EXPERTS_PER_GROUP, dtype=F32) * top_v[..., None], 1) * gate_g
    combine = jax.nn.one_hot(g_sel, N_GROUPS, dtype=F32)[:, :, None] * w_in_group[:, None, :]
    y = jnp.zeros_like(xt)
    for g in range(N_GROUPS):
        e = slice(g * EXPERTS_PER_GROUP, (g + 1) * EXPERTS_PER_GROUP)
        h = jax.nn.silu(jnp.einsum('nd,edf->nef', xt, w_gate[e])) * jnp.einsum('nd,edf->nef', xt, w_up[e])
        h = h * combine[:, g, :, None].astype(h.dtype)
        y = y + jnp.einsum('nef,efd->nd', h, w_down[e])
    return y.reshape(B, T, D)

def first_inputs(seed: int = 0) -> dict:
    key = jax.random.key(seed)
    keys = iter(jax.random.split(key, 48))

    def normal(shape, scale):
        return jax.random.normal(next(keys), shape, F32) * scale

    def gain(shape):
        return 1.0 + normal(shape, 0.02)

    def uniform(shape, lo, hi):
        return jax.random.uniform(next(keys), shape, F32, minval=lo, maxval=hi)

    nA, nB, nC, nD = [len(range(m, DEPTH, N_MIXERS)) for m in range(N_MIXERS)]
    D = D_MODEL
    rs = (2 * DEPTH) ** -0.5
    x = normal((BATCH, SEQ, D), 1.0)
    norm_mix = gain((DEPTH, D))
    norm_ffn = gain((DEPTH, D))
    da_w_in = normal((nA, D, DA_IN_WIDTH), D ** -0.5)
    da_q_norm = gain((nA, DA_HEAD_DIM))
    da_k_norm = gain((nA, DA_HEAD_DIM))
    da_lambda_q1 = normal((nA, DA_HEAD_DIM), 0.1)
    da_lambda_k1 = normal((nA, DA_HEAD_DIM), 0.1)
    da_lambda_q2 = normal((nA, DA_HEAD_DIM), 0.1)
    da_lambda_k2 = normal((nA, DA_HEAD_DIM), 0.1)
    da_subln = gain((nA, 2 * DA_HEAD_DIM))
    da_w_out = normal((nA, DA_HEADS * 2 * DA_HEAD_DIM, D), (DA_HEADS * 2 * DA_HEAD_DIM) ** -0.5 * rs)
    nsa_w_in = normal((nB, D, NSA_IN_WIDTH), D ** -0.5)
    nsa_q_norm = gain((nB, NSA_HEAD_DIM))
    nsa_k_norm = gain((nB, 3, NSA_HEAD_DIM))
    nsa_cmp_pos = normal((nB, 2, CMP_BLOCK, NSA_HEAD_DIM), 0.1)
    nsa_cmp_w1 = normal((nB, 2, CMP_BLOCK * NSA_HEAD_DIM, CMP_HIDDEN), (CMP_BLOCK * NSA_HEAD_DIM) ** -0.5)
    nsa_cmp_w2 = normal((nB, 2, CMP_HIDDEN, NSA_HEAD_DIM), CMP_HIDDEN ** -0.5)
    nsa_w_out = normal((nB, NSA_HEADS * NSA_HEAD_DIM, D), (NSA_HEADS * NSA_HEAD_DIM) ** -0.5 * rs)
    gdn_w_in = normal((nC, D, GDN_IN_WIDTH), D ** -0.5)
    gdn_conv_w = normal((nC, CONV_WIDTH, 3 * GDN_HEADS * GDN_HEAD_DIM), CONV_WIDTH ** -0.5)
    gdn_a_log = jnp.log(uniform((nC, GDN_HEADS), 1.0, 16.0))
    dt = jnp.exp(uniform((nC, GDN_HEADS), math.log(1e-3), math.log(0.1)))
    gdn_dt_bias = dt + jnp.log(-jnp.expm1(-dt))
    gdn_out_norm = gain((nC, GDN_HEAD_DIM))
    gdn_w_out = normal((nC, GDN_HEADS * GDN_HEAD_DIM, D), (GDN_HEADS * GDN_HEAD_DIM) ** -0.5 * rs)
    bw = LRU_WIDTH // LRU_BLOCKS
    lru_w_in = normal((nD, D, 2 * LRU_WIDTH), D ** -0.5)
    lru_conv_w = normal((nD, CONV_WIDTH, LRU_WIDTH), CONV_WIDTH ** -0.5)
    lru_conv_b = normal((nD, LRU_WIDTH), 0.1)
    lru_w_a = normal((nD, LRU_BLOCKS, bw, bw), bw ** -0.5)
    lru_b_a = normal((nD, LRU_WIDTH), 0.1)
    lru_w_x = normal((nD, LRU_BLOCKS, bw, bw), bw ** -0.5)
    lru_b_x = normal((nD, LRU_WIDTH), 0.1)
    a_c = uniform((nD, LRU_WIDTH), 0.9, 0.999)
    a0 = a_c ** (1.0 / LRU_C)
    lru_lambda = jnp.log(a0) - jnp.log1p(-a0)
    lru_w_out = normal((nD, LRU_WIDTH, D), LRU_WIDTH ** -0.5 * rs)
    moe_w_group = normal((DEPTH, D, N_GROUPS), D ** -0.5)
    moe_b_group = normal((DEPTH, N_GROUPS), 0.01)
    moe_w_router = normal((DEPTH, D, N_EXPERTS), D ** -0.5)
    moe_b_router = normal((DEPTH, N_EXPERTS), 0.01)
    moe_w_gate = normal((DEPTH, N_EXPERTS, D, D_EXPERT), D ** -0.5)
    moe_w_up = normal((DEPTH, N_EXPERTS, D, D_EXPERT), D ** -0.5)
    moe_w_down = normal((DEPTH, N_EXPERTS, D_EXPERT, D), D_EXPERT ** -0.5 * rs)
    return {'x': x, 'norm_mix': norm_mix, 'norm_ffn': norm_ffn,
            'da_w_in': da_w_in, 'da_q_norm': da_q_norm, 'da_k_norm': da_k_norm,
            'da_lambda_q1': da_lambda_q1, 'da_lambda_k1': da_lambda_k1,
            'da_lambda_q2': da_lambda_q2, 'da_lambda_k2': da_lambda_k2,
            'da_subln': da_subln, 'da_w_out': da_w_out,
            'nsa_w_in': nsa_w_in, 'nsa_q_norm': nsa_q_norm, 'nsa_k_norm': nsa_k_norm,
            'nsa_cmp_pos': nsa_cmp_pos, 'nsa_cmp_w1': nsa_cmp_w1, 'nsa_cmp_w2': nsa_cmp_w2,
            'nsa_w_out': nsa_w_out,
            'gdn_w_in': gdn_w_in, 'gdn_conv_w': gdn_conv_w, 'gdn_a_log': gdn_a_log,
            'gdn_dt_bias': gdn_dt_bias, 'gdn_out_norm': gdn_out_norm, 'gdn_w_out': gdn_w_out,
            'lru_w_in': lru_w_in, 'lru_conv_w': lru_conv_w, 'lru_conv_b': lru_conv_b,
            'lru_w_a': lru_w_a, 'lru_b_a': lru_b_a, 'lru_w_x': lru_w_x, 'lru_b_x': lru_b_x,
            'lru_lambda': lru_lambda, 'lru_w_out': lru_w_out,
            'moe_w_group': moe_w_group, 'moe_b_group': moe_b_group,
            'moe_w_router': moe_w_router, 'moe_b_router': moe_b_router,
            'moe_w_gate': moe_w_gate, 'moe_w_up': moe_w_up, 'moe_w_down': moe_w_down}

def first_block(x, norm_mix, norm_ffn,
              da_w_in, da_q_norm, da_k_norm, da_lambda_q1, da_lambda_k1, da_lambda_q2, da_lambda_k2,
              da_subln, da_w_out,
              nsa_w_in, nsa_q_norm, nsa_k_norm, nsa_cmp_pos, nsa_cmp_w1, nsa_cmp_w2, nsa_w_out,
              gdn_w_in, gdn_conv_w, gdn_a_log, gdn_dt_bias, gdn_out_norm, gdn_w_out,
              lru_w_in, lru_conv_w, lru_conv_b, lru_w_a, lru_b_a, lru_w_x, lru_b_x, lru_lambda, lru_w_out,
              moe_w_group, moe_b_group, moe_w_router, moe_b_router, moe_w_gate, moe_w_up, moe_w_down):
    for i in range(DEPTH):
        m, j = i % N_MIXERS, i // N_MIXERS
        h = rmsnorm(x, norm_mix[i])
        if m == 0:
            y = diff_attention(h, da_w_in[j], da_q_norm[j], da_k_norm[j], da_lambda_q1[j], da_lambda_k1[j],
                               da_lambda_q2[j], da_lambda_k2[j], da_subln[j], da_w_out[j],
                               0.8 - 0.6 * math.exp(-0.3 * i))
        elif m == 1:
            y = nsa_attention(h, nsa_w_in[j], nsa_q_norm[j], nsa_k_norm[j], nsa_cmp_pos[j],
                              nsa_cmp_w1[j], nsa_cmp_w2[j], nsa_w_out[j])
        elif m == 2:
            y = gated_deltanet(h, gdn_w_in[j], gdn_conv_w[j], gdn_a_log[j], gdn_dt_bias[j],
                               gdn_out_norm[j], gdn_w_out[j])
        else:
            y = rg_lru_block(h, lru_w_in[j], lru_conv_w[j], lru_conv_b[j], lru_w_a[j], lru_b_a[j],
                             lru_w_x[j], lru_b_x[j], lru_lambda[j], lru_w_out[j])
        x = x + y
        x = x + hier_moe(rmsnorm(x, norm_ffn[i]), moe_w_group[i], moe_b_group[i], moe_w_router[i],
                         moe_b_router[i], moe_w_gate[i], moe_w_up[i], moe_w_down[i])
    return x


CTX_LEN = 256
GRID_W = 64
F_WIDTH = D_MODEL // 2
F_GROUPS = 4
F_GROUP_DIM = F_WIDTH // F_GROUPS
HEAD_DIM = 64
NA_WIDTH = D_MODEL - F_WIDTH
NA_HEADS = NA_WIDTH // HEAD_DIM
MIX_WIDTH = F_WIDTH + NA_WIDTH
IN_COLS = 2 * F_WIDTH + 4 * NA_WIDTH
WIN_ROWS_MAX = 8
WIN_COLS = 16
EPS = 1e-6
NEG_INF = -1e30


def _rms_norm(t, g):
    t32 = t.astype(jnp.float32)
    y = t32 * lax.rsqrt(jnp.mean(t32 * t32, axis=-1, keepdims=True) + EPS)
    return (y * g.astype(jnp.float32)).astype(t.dtype)

def _ada(cond, w_ada, b_ada):
    mod = jax.nn.silu(cond) @ w_ada + b_ada
    return jnp.split(mod, 3, axis=-1)

def _split_proj(p):
    f_in = p[..., :F_WIDTH]
    f_gate = p[..., F_WIDTH:2 * F_WIDTH]
    q, k, v, na_gate = jnp.split(p[..., 2 * F_WIDTH:], 4, axis=-1)
    return f_in, f_gate, q, k, v, na_gate

def _heads(t):
    return t.reshape(t.shape[0], t.shape[1], NA_HEADS, HEAD_DIM)

def _fourier(u, w_four):
    b, l, _ = u.shape
    ug = u.reshape(b, l, F_GROUPS, F_GROUP_DIM).astype(jnp.float32)
    y = jnp.real(jnp.fft.fft2(ug, axes=(1, 3))) * ((l * F_GROUP_DIM) ** -0.5)
    y = y.reshape(b, l, F_WIDTH).astype(u.dtype)
    return y @ w_four

def _ctx_attention(qc, kc, vc):
    s = jnp.einsum('bqhd,bkhd->bhqk', qc, kc, preferred_element_type=jnp.float32) * (HEAD_DIM ** -0.5)
    p = jax.nn.softmax(s, axis=-1).astype(vc.dtype)
    o = jnp.einsum('bhqk,bkhd->bqhd', p, vc)
    return o.reshape(o.shape[0], o.shape[1], NA_WIDTH)

def _neighbourhood_attention(q, k, v, kc, vc, rel_bias):
    b, l, h, d = q.shape
    rows = l // GRID_W
    wr = min(WIN_ROWS_MAX, rows)
    r_ar = jnp.arange(rows)
    rs = jnp.clip(r_ar - wr // 2, 0, rows - wr)
    row_idx = rs[:, None] + jnp.arange(wr)[None, :]
    col_ar = jnp.arange(GRID_W)
    cs = jnp.clip(col_ar - WIN_COLS // 2, 0, GRID_W - WIN_COLS)
    in_win = (col_ar[None, :] >= cs[:, None]) & (col_ar[None, :] < cs[:, None] + WIN_COLS)
    mask = jnp.broadcast_to(in_win[:, None, :], (GRID_W, wr, GRID_W)).reshape(GRID_W, wr * GRID_W)
    dr_idx = row_idx - r_ar[:, None] + (WIN_ROWS_MAX - 1)
    dc_idx = jnp.clip(col_ar[None, :] - col_ar[:, None], -(WIN_COLS - 1), WIN_COLS - 1) + (WIN_COLS - 1)
    bias = rel_bias[:, dr_idx[:, None, :, None], dc_idx[None, :, None, :]]
    bias = bias.reshape(h, rows, GRID_W, wr * GRID_W).astype(jnp.float32)
    qg = q.reshape(b, rows, GRID_W, h, d)
    k_rows = k.reshape(b, rows, GRID_W, h, d)[:, row_idx].reshape(b, rows, wr * GRID_W, h, d)
    v_rows = v.reshape(b, rows, GRID_W, h, d)[:, row_idx].reshape(b, rows, wr * GRID_W, h, d)
    scale = HEAD_DIM ** -0.5
    s_loc = jnp.einsum('brqhd,brkhd->bhrqk', qg, k_rows, preferred_element_type=jnp.float32) * scale
    s_loc = jnp.where(mask[None, None, None], s_loc + bias[None], NEG_INF)
    s_ctx = jnp.einsum('brqhd,bkhd->bhrqk', qg, kc, preferred_element_type=jnp.float32) * scale
    p = jax.nn.softmax(jnp.concatenate([s_loc, s_ctx], axis=-1), axis=-1).astype(v.dtype)
    n_loc = wr * GRID_W
    o = (jnp.einsum('bhrqk,brkhd->brqhd', p[..., :n_loc], v_rows)
         + jnp.einsum('bhrqk,bkhd->brqhd', p[..., n_loc:], vc))
    return o.reshape(b, l, NA_WIDTH)

def second_inputs(seed: int = 0) -> dict:
    key = jax.random.key(seed)
    ks = jax.random.split(key, 14)
    f32 = jnp.float32
    n = lambda k, shape: jax.random.normal(k, shape, f32)
    return {
        "x": n(ks[0], (BATCH, SEQ, D_MODEL)),
        "c": n(ks[1], (BATCH, D_MODEL)),
        "ctx": n(ks[2], (BATCH, CTX_LEN, D_MODEL)),
        "c_ctx": n(ks[3], (D_MODEL,)),
        "norm_g": 1.0 + 0.02 * n(ks[4], (DEPTH, D_MODEL)),
        "w_ada": n(ks[5], (DEPTH, D_MODEL, 3 * D_MODEL)) * D_MODEL ** -0.5,
        "b_ada": 0.02 * n(ks[6], (DEPTH, 3 * D_MODEL)),
        "w_in": n(ks[7], (DEPTH, D_MODEL, IN_COLS)) * D_MODEL ** -0.5,
        "w_four": n(ks[8], (DEPTH, F_WIDTH, F_WIDTH)) * F_WIDTH ** -0.5,
        "q_norm_g": 1.0 + 0.02 * n(ks[9], (DEPTH, HEAD_DIM)),
        "k_norm_g": 1.0 + 0.02 * n(ks[10], (DEPTH, HEAD_DIM)),
        "rel_bias": 0.02 * n(ks[11], (DEPTH, NA_HEADS, 2 * WIN_ROWS_MAX - 1, 2 * WIN_COLS - 1)),
        "w_out": n(ks[12], (DEPTH, MIX_WIDTH, D_MODEL)) * MIX_WIDTH ** -0.5,
    }

def second_block(x, c, ctx, c_ctx, norm_g, w_ada, b_ada, w_in, w_four, q_norm_g, k_norm_g, rel_bias, w_out):
    for l in range(DEPTH):
        last = l == DEPTH - 1
        sh_x, sc_x, g_x = [t[:, None, :] for t in _ada(c, w_ada[l], b_ada[l])]
        sh_c, sc_c, g_c = _ada(c_ctx, w_ada[l], b_ada[l])
        xn = _rms_norm(x, norm_g[l]) * (1.0 + sc_x) + sh_x
        cn = _rms_norm(ctx, norm_g[l]) * (1.0 + sc_c) + sh_c
        fx_in, fx_gate, qx, kx, vx, nx_gate = _split_proj(xn @ w_in[l])
        fc_in, fc_gate, qc, kc, vc, nc_gate = _split_proj(cn @ w_in[l])
        qx = _rms_norm(_heads(qx), q_norm_g[l])
        kx = _rms_norm(_heads(kx), k_norm_g[l])
        vx = _heads(vx)
        qc = _rms_norm(_heads(qc), q_norm_g[l])
        kc = _rms_norm(_heads(kc), k_norm_g[l])
        vc = _heads(vc)
        f_out = _fourier(fx_in, w_four[l]) * jax.nn.silu(fx_gate)
        na_out = _neighbourhood_attention(qx, kx, vx, kc, vc, rel_bias[l]) * jax.nn.silu(nx_gate)
        x_new = x + g_x * (jnp.concatenate([f_out, na_out], axis=-1) @ w_out[l])
        if not last:
            fc_out = _fourier(fc_in, w_four[l]) * jax.nn.silu(fc_gate)
            nc_out = _ctx_attention(qc, kc, vc) * jax.nn.silu(nc_gate)
            ctx = ctx + g_c * (jnp.concatenate([fc_out, nc_out], axis=-1) @ w_out[l])
        x = x_new
    return x


def setup_inputs(seed=0):
    out = dict(first_inputs(seed))
    for name, value in second_inputs(seed + 1).items():
        if name != "x":
            out[name + "_2"] = value
    return out


def reference(
    x, norm_mix, norm_ffn, da_w_in, da_q_norm, da_k_norm, da_lambda_q1, da_lambda_k1,
    da_lambda_q2, da_lambda_k2, da_subln, da_w_out, nsa_w_in, nsa_q_norm, nsa_k_norm,
    nsa_cmp_pos, nsa_cmp_w1, nsa_cmp_w2, nsa_w_out, gdn_w_in, gdn_conv_w, gdn_a_log,
    gdn_dt_bias, gdn_out_norm, gdn_w_out, lru_w_in, lru_conv_w, lru_conv_b, lru_w_a, lru_b_a,
    lru_w_x, lru_b_x, lru_lambda, lru_w_out, moe_w_group, moe_b_group, moe_w_router,
    moe_b_router, moe_w_gate, moe_w_up, moe_w_down, c_2, ctx_2, c_ctx_2, norm_g_2, w_ada_2,
    b_ada_2, w_in_2, w_four_2, q_norm_g_2, k_norm_g_2, rel_bias_2, w_out_2,
):
    x = first_block(
        x, norm_mix, norm_ffn, da_w_in, da_q_norm, da_k_norm, da_lambda_q1, da_lambda_k1,
        da_lambda_q2, da_lambda_k2, da_subln, da_w_out, nsa_w_in, nsa_q_norm, nsa_k_norm,
        nsa_cmp_pos, nsa_cmp_w1, nsa_cmp_w2, nsa_w_out, gdn_w_in, gdn_conv_w, gdn_a_log,
        gdn_dt_bias, gdn_out_norm, gdn_w_out, lru_w_in, lru_conv_w, lru_conv_b, lru_w_a,
        lru_b_a, lru_w_x, lru_b_x, lru_lambda, lru_w_out, moe_w_group, moe_b_group,
        moe_w_router, moe_b_router, moe_w_gate, moe_w_up, moe_w_down,
    )
    return second_block(
        x, c_2, ctx_2, c_ctx_2, norm_g_2, w_ada_2, b_ada_2, w_in_2, w_four_2, q_norm_g_2,
        k_norm_g_2, rel_bias_2, w_out_2,
    )


_drawn_inputs = setup_inputs


def setup_inputs(seed=0):
    import zlib

    import numpy as np

    out = dict(_drawn_inputs(seed))
    spreads = {}
    factors = {'norm_ffn': 2.993,
     'da_q_norm': 4.668,
     'da_k_norm': 3.983,
     'da_lambda_q1': 2.874,
     'da_lambda_k2': 7.724,
     'da_subln': 3.412,
     'moe_b_group': 4.564,
     'moe_b_router': 8.0,
     'ctx_2': 2.855,
     'norm_g_2': 7.559,
     'b_ada_2': 3.702,
     'q_norm_g_2': 8.0,
     'k_norm_g_2': 8.0,
     'rel_bias_2': 40.174}
    for name, (base, spread) in spreads.items():
        noise = np.random.default_rng([zlib.crc32(name.encode()), seed]).standard_normal(out[name].shape)
        drawn = base * np.exp(spread * noise) if base else spread * noise
        out[name] = jnp.asarray(drawn.astype(out[name].dtype))
    for name, factor in factors.items():
        out[name] = (out[name] * factor).astype(out[name].dtype)
    return out
```

```python
from contextlib import ExitStack

import numpy as np

import concourse.bass as bass
from concourse import mybir

ALU = mybir.AluOpType
ACT = mybir.ActivationFunctionType
AX = mybir.AxisListType
F32 = mybir.dt.float32
I32 = mybir.dt.int32
U32 = mybir.dt.uint32

P = 128
SEQ, D = 512, 1024
TT = SEQ // P
KD = D // P
EPS = 1e-6

HEADS, DH = 8, 64
CH = 512
QK_CHUNKS = 4
LAMBDA_INIT = 0.2
BIG = 1e30

GROUPS, PER_GROUP = 4, 4
EXPERTS = GROUPS * PER_GROUP
F = 512
FC = F // P
SPILL = 7
ROWS = (EXPERTS + SPILL) * P

CTX = 256
CT = CTX // P
GRID = 64
ROWS_G = SEQ // GRID
H2 = 8
W2 = 512
QC, KC = 16, 32
KEY_COL = [0, 8, 24, 32]
SHIFT = [16, 8, 8, 0]
MASK = [0, 1, 1, 2]
REL_W = 63
PARTS = {"f_in": 0, "f_gate": 1, "q": 2, "k": 3, "v": 4, "na_gate": 5}

SLOTS = 6
W_IN, W_OUT, W_MOE = 0, 6, 8


def kernel_program(nc, A, out):
    with ExitStack() as ctx:
        build(nc, ctx, A, out)


def attention_steps(s):
    todo = []
    if s < TT * HEADS:
        todo.append(("scores", s))
    if 1 <= s <= TT * HEADS:
        todo.append(("pd", s - 1))
    if 2 <= s < TT * HEADS + 2:
        todo.append(("pdT", s - 2))
    if 3 <= s < TT * HEADS + 3:
        todo.append(("pv", s - 3))
    for name, at in (("o_raw0", 7), ("o_raw1", 11), ("o_mean", 12), ("o_norm", 13), ("oT", 14),
                     ("w_out", 15), ("x_add", 16)):
        t, rest = divmod(s - at, HEADS)
        if 0 <= t < TT and rest == 0:
            todo.append((name, t))
    return todo


ATTENTION_STEPS = HEADS * TT + 9

PROJ2 = ([("ck", t) for t in range(CT)] + [("cv", t) for t in range(CT)]
         + [(part, t) for part in ("k", "v", "q", "u", "ng", "fg") for t in range(TT)])
QK2 = [item for item in PROJ2 if item[0] in ("ck", "k", "q")]
PAIRS = TT * H2 // 2


def mixer_steps(s):
    todo = []
    if s < PAIRS:
        todo.append(("scores", s))
    if s % 2 == 0 and s < 16:
        todo.append(("fourier", s // 2))
    if 2 <= s < PAIRS + 2:
        todo.append(("pv", s - 2))
    if 1 <= s <= PAIRS:
        todo.append(("pT", s - 1))
    c, late = divmod(s - 6, 4)
    if 0 <= c < TT and late == 0:
        todo.append(("oT", c))
    return todo


MIXER_STEPS = PAIRS + 4


def build(nc, ctx, A, out):
    def sb(name, shape, dt=F32):
        return ctx.enter_context(nc.sbuf_tensor(name, shape, dt))

    def sem(name):
        return ctx.enter_context(nc.semaphore(name))

    x = sb("x", [P, TT, D])
    buf_a = sb("buf_a", [P, 4096])
    buf_b = sb("buf_b", [P, 4096])
    buf_c = sb("buf_c", [P, 4096])
    buf_d = sb("buf_d", [P, 4096])
    ring = sb("ring", [P, SLOTS, 4096])
    s_buf = sb("s_buf", [P, 2, 2, 512])
    pd = sb("pd", [P, 2, 512])
    pT = sb("pT", [P, 2, 512])
    o_sb = sb("o_sb", [P, D])
    zeros = sb("zeros", [P, P])
    ident = sb("ident", [P, P])
    tri = sb("tri", [P, P])
    ones = sb("ones", [P, P])
    g_x = sb("g_x", [P, D])
    dist = g_x[:, 0:512]
    gain1 = sb("gain1", [P, KD])
    gain2 = sb("gain2", [P, KD])
    qk_gain = sb("qk_gain", [P, 2])
    sub_gain = sb("sub_gain", [P, 1])
    lam = sb("lam", [P, 4])
    w_rt = sb("w_rt", [P, KD, 20])
    b_rt = sb("b_rt", [P, 20])
    ssq = sb("ssq", [P, 8])
    ms = sb("ms", [P, 8])
    rstd = sb("rstd", [P, 8])
    qk_st = sb("qk_st", [P, 2, 3, 8])
    half = sb("half", [P, 8])
    den = sb("den", [P, 2, 2])
    nmx = sb("nmx", [P, 2, 2])
    ratio = sb("ratio", [P, 2, 2])
    rden = sb("rden", [P, 2, 8])
    o_st = sb("o_st", [P, 3, 8])
    logit = sb("logit", [P, TT, 20])
    g_pick = sb("g_pick", [P, TT, GROUPS])
    g_exp = sb("g_exp", [P, TT, GROUPS])
    in_group = sb("in_group", [P, TT, PER_GROUP])
    e_pick = sb("e_pick", [P, 2, TT, PER_GROUP])
    r_a = sb("r_a", [P, TT, EXPERTS])
    r_b = sb("r_b", [P, TT, 4])
    r_c = sb("r_c", [P, TT, 4])
    r_m = sb("r_m", [P, 6, TT])
    picks = sb("picks", [P, 2, TT, EXPERTS])
    sel = sb("sel", [P, TT, EXPERTS])
    place = sb("place", [P, TT + 1, EXPERTS])
    full_tiles = sb("full_tiles", [P, 4, EXPERTS])
    weight = sb("weight", [P, 2, TT])
    row_f = sb("row_f", [P, 2, TT])
    iota16 = sb("iota16", [P, 16])
    prio = sb("prio", [P, 4])
    row_i = sb("row_i", [P, 2, TT], I32)
    tok_i = sb("tok_i", [P, TT], I32)
    spill_i = sb("spill_i", [P, SPILL + 1], I32)
    idx = sb("idx", [P, 2], I32)

    norm_g = sb("norm_g", [P, KD])
    mod_g = sb("mod_g", [P, 2, KD])
    mod_sh = sb("mod_sh", [P, 2, KD])
    qk_gain2 = sb("qk_gain2", [P, 2])
    cond = sb("cond", [P, KD, 2])
    mask = sb("mask", [P, 3, KC])
    chan = sb("chan", [P, 2, P])
    cssq = sb("cssq", [P, 3, CT])

    lam_in = s_buf[:, 0, 0, 0:4 * DH].rearrange("p (n d) -> p n d", n=4)
    lam_pr = s_buf[:, 0, 1, 0:2 * DH].rearrange("p (n d) -> p n d", n=2)
    xs = buf_a[:, :].rearrange("p (t d) -> p t d", t=TT)
    v = xs
    hT = buf_b[:, :].rearrange("p (k n) -> p k n", k=KD)
    oT = hT
    qT = buf_c[:, :].rearrange("p (h n) -> p h n", h=HEADS)
    kT = buf_d[:, :].rearrange("p (h n) -> p h n", h=HEADS)
    xs2 = buf_c[:, :].rearrange("p (t d) -> p t d", t=TT)
    xT2 = buf_d[:, :].rearrange("p (k n) -> p k n", k=KD)
    xg = buf_a[:, 0:2048].rearrange("p (b d) -> p b d", b=2)
    xgT = buf_a[:, 2048:4096].rearrange("p (b k n) -> p b k n", b=2, k=KD)
    sg = buf_b[:, 0:1024].rearrange("p (b f) -> p b f", b=2)
    hidT = buf_b[:, 1024:2048].rearrange("p (b f) -> p b f", b=2)
    y_sb = buf_b[:, 2048:4096].rearrange("p (b d) -> p b d", b=2)
    yg = buf_a[:, :].rearrange("p (b d) -> p b d", b=4)
    mod_row = buf_c[0:2, 0:3 * D]
    b_ada = buf_c[0:2, 3 * D:4 * D]
    q2T = buf_c[:, 0:2048].rearrange("p (g n) -> p g n", g=4)
    k2T = buf_c[:, 2048:4096].rearrange("p (g n) -> p g n", g=4)
    cx = buf_d[:, 0:2048].rearrange("p (t d) -> p t d", t=CT)
    cxT = buf_d[:, 2048:4096].rearrange("p (k n) -> p k n", k=KD)
    u = buf_d[:, 0:2048].rearrange("p (t n) -> p t n", t=TT)
    yT = u
    fgT = buf_d[:, 2048:4096].rearrange("p (f n) -> p f n", f=4)
    xs3 = xs
    x3T = hT
    v_win = buf_a[:, :].rearrange("p (i n) -> p i n", i=8)
    mixT = hT
    ckT = ring[:, 5, 0:1024].rearrange("p (g n) -> p g n", g=4)
    cv = ring[:, 5, 1024:2048].rearrange("p (t n) -> p t n", t=CT)
    ngT = ring[:, 5, 2048:4096].rearrange("p (f n) -> p f n", f=4)
    rel = ring[:, 1, 0:8 * 8 * 48].rearrange("p (r h n) -> p r h n", r=8, h=8)
    bias = [ring[:, 0, 0:2048], ring[:, 0, 2048:4096], ring[:, 3, 2048:4096]]
    seqT = ring[:, 1, :].rearrange("p (g a n) -> p g a n", g=4, a=2)

    xn_d = nc.dram_tensor("xn_d", (SEQ, D), F32).ap()
    ids_d = nc.dram_tensor("ids_d", (ROWS, 1), I32).ap()
    y_d = nc.dram_tensor("y_d", (ROWS, D), F32).ap()
    v_d = nc.dram_tensor("v_d", (SEQ, W2), F32).ap()

    psum = ctx.enter_context(nc.psum_tensor("psum", [P, 8, 512], F32))
    SC = [psum[:, 0:2, :], psum[:, 2:4, :]]
    TP = [psum[:, 4, :], psum[:, 5, :]]
    MM = [psum[:, 6, :], psum[:, 7, :]]

    full = {c: [sem(f"{c}_full{i}") for i in range(2)] for c in ("sc", "tp", "mm")}
    free = {c: [sem(f"{c}_free{i}") for i in range(2)] for c in ("sc", "tp", "mm")}
    bufs = {"sc": SC, "tp": TP, "mm": MM}

    turn = {}
    count = {"sc": 0, "tp": 0, "mm": 0}

    def book(c, *key):
        turn[(c, *key)] = count[c]
        count[c] += 1

    for k in range(KD):
        book("tp", "hT", k)
    for i in range(6 * TT):
        book("mm", "proj", i)
    for i in range(QK_CHUNKS * TT):
        book("tp", "qkT", i)
    for s in range(ATTENTION_STEPS):
        for name, m in attention_steps(s):
            if name == "scores":
                book("sc", "scores", m)
            elif name == "pdT":
                book("tp", "pdT", m)
            elif name == "pv" and m % 4 == 0:
                book("mm", "o", m // 4)
            elif name == "oT":
                book("tp", "oT", 2 * m)
                book("tp", "oT", 2 * m + 1)
            elif name == "w_out":
                book("sc", "w_out", m)
    for k in range(KD):
        book("tp", "xT2", k)
    book("mm", "router")
    book("mm", "places")
    tp0, sc0 = count["tp"], count["sc"]

    def turn_x(e):
        return tp0 if e == 0 else tp0 + 3 * e - 1

    def turn_hid(e):
        return tp0 + 3 * e + (4 if e < EXPERTS - 1 else 2)

    def turn_gu(e):
        return sc0 if e == 0 else sc0 + 2 * e - 1

    def turn_dn(e):
        return sc0 + 2 * e + (2 if e < EXPERTS - 1 else 1)

    count["tp"] += 3 * EXPERTS
    count["sc"] += 2 * EXPERTS

    for c in range(6):
        book("mm", "ada", c)
    book("tp", "mod")
    for c in range(2):
        book("mm", "g_x", c)
    for k in range(0, KD, 2):
        book("tp", "cxT", k)
    for i, item in enumerate(PROJ2):
        if item == ("k", 0):
            for k in range(KD):
                book("tp", "x3T", k)
        book("mm", *item)
        if i >= 1 and PROJ2[i - 1] in QK2:
            book("tp", "qkT2", QK2.index(PROJ2[i - 1]))
    for s in range(MIXER_STEPS):
        for name, m in mixer_steps(s):
            if name == "scores":
                book("sc", "scores2", m)
            elif name == "fourier":
                book("sc", "fourier", m)
            elif name == "pT":
                book("tp", "pT2", 2 * m)
                book("tp", "pT2", 2 * m + 1)
            elif name == "pv" and m % 4 == 0:
                book("mm", "o2", m // 4)
            elif name == "oT":
                book("tp", "oT2", m)
    for t in range(TT):
        book("sc", "out", t)

    slot_of, loads = {}, [10, 10, 9, 9, 9, 9]
    for name, i in (("ada0", 2), ("ada1", 3), ("ada2", 4), ("ada3", 5), ("ada4", 0), ("ada5", 1),
                    ("k", 2), ("v", 3), ("q", 4), ("f_in", 2), ("na_gate", 3), ("f_gate", 4),
                    ("dft", 2), ("w_four", 3), ("w_out0", 4), ("w_out1", 2)):
        loads[i] += 1
        slot_of[name] = (i, 16 * loads[i])

    def buf(c, n):
        return bufs[c][n % 2]

    def claim(eng, c, n, more=0):
        if n >= 2:
            eng.wait_ge(free[c][n % 2], more + n // 2)

    def filled(eng, c, n, more=0):
        eng.wait_ge(full[c][n % 2], more + (n // 2 + 1))

    def drained(eng, c, n, more=0):
        eng.wait_ge(free[c][n % 2], more + (n // 2 + 1))

    def fill(ins, c, n):
        ins.then_inc(full[c][n % 2], 1)

    def drain(ins, c, n):
        ins.then_inc(free[c][n % 2], 1)

    x_loaded = [sem(f"x_loaded{t}") for t in range(TT)]
    early_loaded, late_loaded = sem("early_loaded"), sem("late_loaded")
    w_landed = [sem(f"w_landed{i}") for i in range(SLOTS)]
    pool_consts = sem("pool_consts")
    dve_done, act_done, pool_done = sem("dve_done"), sem("act_done"), sem("pool_done")
    ssq_ready = sem("ssq_ready")
    ms_ready = sem("ms_ready")
    rstd_ready = sem("rstd_ready")
    xs_ready = sem("xs_ready")
    gains_scaled = sem("gains_scaled")
    sq_ready = sem("sq_ready")
    qk_ms_ready = sem("qk_ms_ready")
    qk_rstd_ready = sem("qk_rstd_ready")
    lam_sum, lam_exp = sem("lam_sum"), sem("lam_exp")
    nmx_ready = sem("nmx_ready")
    exp_ready = sem("exp_ready")
    pd_ready = sem("pd_ready")
    o_sq_ready = sem("o_sq_ready")
    o_ms_ready, o_rstd_ready = sem("o_ms_ready"), sem("o_rstd_ready")
    o_norm_ready = sem("o_norm_ready")
    xs2_ready = sem("xs2_ready")
    w_rt_ready = sem("w_rt_ready")
    ge_in, ge_out = sem("ge_in"), sem("ge_out")
    sel_ready = sem("sel_ready")
    rows_ready = sem("rows_ready")
    y_zeroed = sem("y_zeroed")
    xn_stored, ids_zeroed, ids_stored = sem("xn_stored"), sem("ids_zeroed"), sem("ids_stored")
    idx_loaded = [sem(f"idx_loaded{b}") for b in range(2)]
    xg_ready = [sem(f"xg_ready{b}") for b in range(2)]
    sg_ready = sem("sg_ready")
    y_stored = [sem(f"y_stored{b}") for b in range(2)]
    yg_ready = [sem(f"yg_ready{i}") for i in range(8)]
    x2_ready = sem("x2_ready")
    out_stored = sem("out_stored")
    spill_ready = sem("spill_ready")
    spill_pe, spill_dve, spill_act = sem("spill_pe"), sem("spill_dve"), sem("spill_act")
    spill_w, spill_idx, spill_x, spill_y = sem("spill_w"), sem("spill_idx"), sem("spill_x"), sem("spill_y")
    second_loaded = sem("second_loaded")
    ctx_loaded = [sem(f"ctx_loaded{t}") for t in range(CT)]
    b_ada_loaded = sem("b_ada_loaded")
    cond_ready = sem("cond_ready")
    mod_ready = sem("mod_ready")
    c_ssq_ready, c_ms_ready, c_rstd_ready = sem("c_ssq_ready"), sem("c_ms_ready"), sem("c_rstd_ready")
    cx_ready = sem("cx_ready")
    xs3_ready = sem("xs3_ready")
    v_stored = [sem(f"v_stored{b}") for b in range(2)]
    v_win_loaded = sem("v_win_loaded")
    rel_loaded = sem("rel_loaded")
    bias_ready = sem("bias_ready")
    neg_max = sem("neg_max")
    o2_ready = sem("o2_ready")
    out_ready = sem("out_ready")

    def spill_count(eng):
        eng.wait_ge(spill_ready, 1)
        return eng.value_load(spill_i[0:1, SPILL:SPILL + 1], min_val=0, max_val=SPILL)

    block = ctx.enter_context(nc.Block())

    @block.sync
    def _(sp):
        def load(i, src, k=KD):
            dst = ring[:, i % SLOTS, :].rearrange("p (k n) -> p k n", k=k)
            sp.dma_start(dst, src).then_inc(w_landed[i % SLOTS], 16)

        for t in range(TT):
            sp.dma_start(x[:, t, :], A["x"][0, t * P:(t + 1) * P, :]).then_inc(x_loaded[t], 16)
        w_in = A["da_w_in"][0].rearrange("(k p) n -> p k n", p=P)
        for c in range(6):
            load(W_IN + c, w_in[:, :, c * CH:(c + 1) * CH])
        w_out = A["da_w_out"][0].rearrange("(k p) n -> p k n", p=P)
        for c in range(2):
            filled(sp, "mm", turn["mm", "proj", (c + 1) * TT - 1])
            load(W_OUT + c, w_out[:, :, c * CH:(c + 1) * CH])

        def load_expert(e, first):
            for m, (name, k) in enumerate((("moe_w_gate", KD), ("moe_w_up", KD), ("moe_w_down", FC))):
                yield m
                src = A[name][0, e] if isinstance(e, int) else A[name][0, bass.ds(e, 1)].rearrange("a r n -> (a r) n")
                load(first + m, src.rearrange("(k p) n -> p k n", p=P), k)

        for m in load_expert(0, W_MOE):
            filled(sp, "mm", turn["mm", "proj", (m + 3) * TT - 1])
        for m in load_expert(1, W_MOE + 3):
            if m == 0:
                filled(sp, "mm", turn["mm", "proj", 6 * TT - 1])
            else:
                filled(sp, "sc", turn["sc", "w_out", TT - 1])
        for m in load_expert(2, W_MOE + 6):
            filled(sp, "sc", turn_gu(0) if m < 2 else turn_dn(0))
        with sp.Fori(0, (EXPERTS - 4) // 2) as j:
            for b in (3, 4):
                for m in load_expert(2 * j + b, W_MOE + 3 * b):
                    filled(sp, "sc", turn_gu(b - 2) if m < 2 else turn_dn(b - 2), 2 * j)
        for m in load_expert(EXPERTS - 1, W_MOE + 3 * (EXPERTS - 1)):
            filled(sp, "sc", turn_gu(EXPERTS - 3) if m < 2 else turn_dn(EXPERTS - 3))

        spills = spill_count(sp)
        with sp.If(spills > 0):
            with sp.Fori(0, SPILL) as o:
                with sp.If(spills > o):
                    e = sp.value_load(spill_i[0:1, bass.ds(o, 1)], min_val=0, max_val=EXPERTS - 1)
                    for m, (name, k, dst) in enumerate((("moe_w_gate", KD, buf_c), ("moe_w_up", KD, buf_d),
                                                        ("moe_w_down", FC, buf_c))):
                        if m == 0:
                            sp.wait_ge(spill_pe, 4 * o + 1)
                        if m == 2:
                            sp.wait_ge(spill_pe, 4 * o + 3)
                        src = A[name][0, bass.ds(e, 1)].rearrange("a r n -> (a r) n")
                        sp.dma_start(dst[:, :].rearrange("p (k n) -> p k n", k=k),
                                     src.rearrange("(k p) n -> p k n", p=P)).then_inc(spill_w, 16)

        def load2(name, src, k=KD):
            i, _ = slot_of[name]
            sp.dma_start(ring[:, i, 0:k * 512].rearrange("p (k n) -> p k n", k=k), src).then_inc(w_landed[i], 16)

        w_ada = A["w_ada_2"][0].rearrange("(k p) n -> p k n", p=P)
        for c in range(6):
            e = EXPERTS - 2 + c // 3
            filled(sp, "sc", turn_gu(e) if c % 3 < 2 else turn_dn(e))
            load2(f"ada{c}", w_ada[:, :, c * 512:(c + 1) * 512])
        w_in2 = A["w_in_2"][0].rearrange("(k p) n -> p k n", p=P)
        for c, name in enumerate(("k", "v", "q", "f_in", "na_gate", "f_gate")):
            if c < 3:
                filled(sp, "mm", turn["mm", "ada", c])
            else:
                filled(sp, "mm", turn["mm", ("k", "v", "q")[c - 3], TT - 1])
            load2(name, w_in2[:, :, PARTS[name] * W2:(PARTS[name] + 1) * W2])
            if name == "k":
                filled(sp, "mm", turn["mm", "ada", 5])
                rel_in = A["rel_pad"]
                for r in range(ROWS_G):
                    sp.dma_start(rel[r * QC:(r + 1) * QC].rearrange("p r h n -> p (r h) n"),
                                 bass.AP(tensor=rel_in.tensor, offset=(ROWS_G - 1 - r) * H2 * REL_W,
                                         ap=[[1, QC], [REL_W, ROWS_G * H2], [1, 48]])).then_inc(rel_loaded, 16)
        filled(sp, "mm", turn["mm", "u", TT - 1])
        load2("dft", A["dft"].rearrange("a (k p) n -> p (a k) n", p=P))
        filled(sp, "mm", turn["mm", "ng", TT - 1])
        load2("w_four", A["w_four_2"][0].rearrange("(k p) n -> p k n", p=P), 4)
        for t in range(2):
            sp.wait_ge(v_stored[t], 32)
        v_rows = v_d.rearrange("(r w) n -> r w n", w=GRID)
        for c in range(TT):
            for half_c in range(2):
                for r in range(4):
                    sp.dma_start(v_win[r * KC:(r + 1) * KC, 2 * c + half_c, :],
                                 v_rows[4 * half_c + r, KEY_COL[c]:KEY_COL[c] + KC, :]).then_inc(v_win_loaded, 16)
        w_out2 = A["w_out_2"][0].rearrange("(k p) n -> p k n", p=P)
        filled(sp, "mm", turn["mm", "fg", TT - 1])
        load2("w_out0", w_out2[:, :, 0:512])
        filled(sp, "sc", turn["sc", "fourier", 3])
        load2("w_out1", w_out2[:, :, 512:1024])

    @block.tensor
    def _(pe):
        mm, transpose = nc.tensor.matmul, nc.tensor.transpose

        def landed(i, more=0):
            pe.wait_ge(w_landed[i % SLOTS], more * 16 + 16 * (i // SLOTS + 1))

        def slot(i, k=KD):
            return ring[:, i % SLOTS, :].rearrange("p (k n) -> p k n", k=k)

        def transposes(n, blocks):
            for g, block_in in enumerate(blocks):
                last = transpose(buf("tp", n)[:, g * P:(g + 1) * P], block_in, ident[:])
            fill(last, "tp", n)

        pe.wait_ge(pool_consts, 1)
        pe.wait_ge(xs_ready, TT)
        for k in range(KD):
            n = turn["tp", "hT", k]
            claim(pe, "tp", n)
            transposes(n, [xs[:, t, k * P:(k + 1) * P] for t in range(TT)])

        for i in range(6 * TT):
            c, t = divmod(i, TT)
            n = turn["mm", "proj", i]
            if t == 0:
                landed(W_IN + c)
            claim(pe, "mm", n)
            for k in range(KD):
                if i == 0:
                    drained(pe, "tp", turn["tp", "hT", k])
                last = mm(buf("mm", n), hT[:, k, t * P:(t + 1) * P], slot(W_IN + c)[:, k, :],
                          start=(k == 0), stop=(k == KD - 1))
            fill(last, "mm", n)
            if 1 <= i <= QK_CHUNKS * TT:
                drained(pe, "mm", turn["mm", "proj", i - 1])
                n = turn["tp", "qkT", i - 1]
                claim(pe, "tp", n)
                transposes(n, [pd[:, (i - 1) % 2, g * P:(g + 1) * P] for g in range(4)])

        for s in range(ATTENTION_STEPS):
            for name, m in attention_steps(s):
                t, h = divmod(m, HEADS)
                if name == "scores":
                    n = turn["sc", "scores", m]
                    if m == 0:
                        drained(pe, "tp", turn["tp", "qkT", QK_CHUNKS * TT - 2])
                        drained(pe, "tp", turn["tp", "qkT", QK_CHUNKS * TT - 1])
                    claim(pe, "sc", n)
                    for c in range(2):
                        rows = slice(c * DH, (c + 1) * DH)
                        last = mm(buf("sc", n)[:, c, 0:(t + 1) * P], qT[rows, h, t * P:(t + 1) * P],
                                  kT[rows, h, 0:(t + 1) * P], start=True, stop=True)
                    fill(last, "sc", n)
                elif name == "pdT":
                    n = turn["tp", "pdT", m]
                    pe.wait_ge(pd_ready, m + 1)
                    claim(pe, "tp", n)
                    transposes(n, [pd[:, m % 2, g * P:(g + 1) * P] for g in range(t + 1)])
                elif name == "pv":
                    n = turn["mm", "o", m // 4]
                    if m == 0:
                        drained(pe, "mm", turn["mm", "proj", 6 * TT - 2])
                        drained(pe, "mm", turn["mm", "proj", 6 * TT - 1])
                    if m % 4 == 0:
                        claim(pe, "mm", n)
                    drained(pe, "tp", turn["tp", "pdT", m])
                    for g in range(t + 1):
                        last = mm(buf("mm", n)[:, (h % 4) * P:(h % 4 + 1) * P], pT[:, m % 2, g * P:(g + 1) * P],
                                  v[:, g, h * P:(h + 1) * P], start=(g == 0), stop=(g == t))
                    if m % 4 == 3:
                        fill(last, "mm", n)
                elif name == "oT":
                    t = m
                    pe.wait_ge(o_norm_ready, t + 1)
                    for b in range(2):
                        n = turn["tp", "oT", 2 * t + b]
                        claim(pe, "tp", n)
                        transposes(n, [o_sb[:, g * P:(g + 1) * P] for g in range(4 * b, 4 * b + 4)])
                elif name == "w_out":
                    t = m
                    n = turn["sc", "w_out", t]
                    claim(pe, "sc", n)
                    drained(pe, "tp", turn["tp", "oT", 2 * t])
                    drained(pe, "tp", turn["tp", "oT", 2 * t + 1])
                    for c in range(2):
                        if t == 0:
                            landed(W_OUT + c)
                        for k in range(KD):
                            last = mm(buf("sc", n)[:, c, :], oT[:, k, t * P:(t + 1) * P], slot(W_OUT + c)[:, k, :],
                                      start=(k == 0), stop=(k == KD - 1))
                    fill(last, "sc", n)

        pe.wait_ge(xs2_ready, TT)
        for k in range(KD):
            n = turn["tp", "xT2", k]
            claim(pe, "tp", n)
            transposes(n, [xs2[:, t, k * P:(k + 1) * P] for t in range(TT)])
        n = turn["mm", "router"]
        claim(pe, "mm", n)
        pe.wait_ge(w_rt_ready, 1)
        drained(pe, "tp", turn["tp", "xT2", KD - 2])
        drained(pe, "tp", turn["tp", "xT2", KD - 1])
        for t in range(TT):
            for k in range(KD):
                last = mm(buf("mm", n)[:, t * 20:(t + 1) * 20], xT2[:, k, t * P:(t + 1) * P], w_rt[:, k, :],
                          start=(k == 0), stop=(k == KD - 1))
        fill(last, "mm", n)
        n = turn["mm", "places"]
        claim(pe, "mm", n)
        pe.wait_ge(sel_ready, 1)
        pe.wait_ge(pool_consts, 3)
        for t in range(TT + 1):
            for i in range(min(t + 1, TT)):
                last = mm(buf("mm", n)[:, t * 16:(t + 1) * 16], tri[:] if i == t else ones[:], sel[:, i, :],
                          start=(i == 0), stop=(i == min(t, TT - 1)))
        fill(last, "mm", n)

        def x_transposes(b, n, gathered, more=0):
            pe.wait_ge(xg_ready[b], gathered)
            for half_row in range(2):
                claim(pe, "tp", n + half_row, more)
                transposes(n + half_row, [xg[:, b, g * P:(g + 1) * P] for g in range(4 * half_row, 4 * half_row + 4)])

        def gate_up(b, n, n_x, i, more_sc=0, more_x=0, more_w=0):
            claim(pe, "sc", n, more_sc)
            drained(pe, "tp", n_x, more_x)
            drained(pe, "tp", n_x + 1, more_x)
            for m in range(2):
                landed(i + m, more_w)
                for k in range(KD):
                    last = mm(buf("sc", n)[:, m, :], xgT[:, b, k, :], slot(i + m)[:, k, :],
                              start=(k == 0), stop=(k == KD - 1))
            fill(last, "sc", n)

        def hid_transposes(b, n, n_gu, more=0, more_gu=0):
            drained(pe, "sc", n_gu, more_gu)
            claim(pe, "tp", n, more)
            transposes(n, [sg[:, b, g * P:(g + 1) * P] for g in range(FC)])

        def down(b, n, n_hid, i, more_sc=0, more_hid=0, more_w=0):
            claim(pe, "sc", n, more_sc)
            drained(pe, "tp", n_hid, more_hid)
            landed(i, more_w)
            for m in range(2):
                for f in range(FC):
                    last = mm(buf("sc", n)[:, m, :], hidT[:, b, f * P:(f + 1) * P],
                              slot(i, FC)[:, f, m * CH:(m + 1) * CH], start=(f == 0), stop=(f == FC - 1))
            fill(last, "sc", n)

        x_transposes(0, turn_x(0), 16)
        gate_up(0, turn_gu(0), turn_x(0), W_MOE)
        x_transposes(1, turn_x(1), 16)
        hid_transposes(0, turn_hid(0), turn_gu(0))
        with pe.Fori(0, EXPERTS // 2 - 1) as j:
            for e in (1, 2):
                gate_up(e % 2, turn_gu(e), turn_x(e), W_MOE + 3 * e, 2 * j, 3 * j, j)
                x_transposes((e + 1) % 2, turn_x(e + 1), 16 * j + 16 * ((e + 1) // 2 + 1), 3 * j)
                down((e - 1) % 2, turn_dn(e - 1), turn_hid(e - 1), W_MOE + 3 * (e - 1) + 2, 2 * j, 3 * j, j)
                hid_transposes(e % 2, turn_hid(e), turn_gu(e), 3 * j, 2 * j)
        e = EXPERTS - 1
        gate_up(1, turn_gu(e), turn_x(e), W_MOE + 3 * e)
        down(0, turn_dn(e - 1), turn_hid(e - 1), W_MOE + 3 * (e - 1) + 2)
        hid_transposes(1, turn_hid(e), turn_gu(e))
        down(1, turn_dn(e), turn_hid(e), W_MOE + 3 * e + 2)

        spills = spill_count(pe)
        with pe.If(spills > 0):
            for n in (turn_hid(EXPERTS - 2), turn_hid(EXPERTS - 1)):
                drained(pe, "tp", n)
            for n in (turn_dn(EXPERTS - 2), turn_dn(EXPERTS - 1)):
                drained(pe, "sc", n)
            pe.sem_inc(spill_pe, 1)
            with pe.Fori(0, SPILL) as o:
                with pe.If(spills > o):
                    pe.wait_ge(spill_act, 3 * o + 1)
                    pe.wait_ge(spill_x, 16 * o + 16)
                    for g in range(KD):
                        last = transpose(TP[g // 4][:, g % 4 * P:(g % 4 + 1) * P], xg[:, 0, g * P:(g + 1) * P], ident[:])
                    last.then_inc(spill_pe, 1)
                    pe.wait_ge(spill_dve, 2 * o + 1)
                    pe.wait_ge(spill_w, 48 * o + 32)
                    for m, w in enumerate((buf_c, buf_d)):
                        for k in range(KD):
                            last = mm(SC[0][:, m, :], xgT[:, 0, k, :], w[:, k * 512:(k + 1) * 512],
                                      start=(k == 0), stop=(k == KD - 1))
                    last.then_inc(spill_pe, 1)
                    pe.wait_ge(spill_dve, 2 * o + 2)
                    for g in range(FC):
                        last = transpose(TP[0][:, g * P:(g + 1) * P], sg[:, 0, g * P:(g + 1) * P], ident[:])
                    last.then_inc(spill_pe, 1)
                    pe.wait_ge(spill_act, 3 * o + 3)
                    pe.wait_ge(spill_w, 48 * o + 48)
                    for m in range(2):
                        for f in range(FC):
                            last = mm(SC[1][:, m, :], hidT[:, 0, f * P:(f + 1) * P],
                                      buf_c[:, f * D + m * CH:f * D + (m + 1) * CH], start=(f == 0), stop=(f == FC - 1))
                    last.then_inc(spill_pe, 1)

        def chunk2(name, k=KD):
            i, landings = slot_of[name]
            pe.wait_ge(w_landed[i], landings)
            return ring[:, i, 0:k * 512].rearrange("p (k n) -> p k n", k=k)

        pe.wait_ge(cond_ready, 1)
        for c in range(6):
            n = turn["mm", "ada", c]
            w = chunk2(f"ada{c}")
            claim(pe, "mm", n)
            for k in range(KD):
                last = mm(buf("mm", n)[0:2, :], cond[:, k, :], w[:, k, :], start=(k == 0), stop=(k == KD - 1))
            fill(last, "mm", n)
        n = turn["tp", "mod"]
        claim(pe, "tp", n)
        drained(pe, "mm", turn["mm", "ada", 4])
        drained(pe, "mm", turn["mm", "ada", 5])
        for k in range(2 * KD):
            last = transpose(buf("tp", n)[:, 2 * k:2 * k + 2], mod_row[:, k * P:(k + 1) * P], ident[0:2, 0:2])
        fill(last, "tp", n)
        for c in range(2):
            n = turn["mm", "g_x", c]
            claim(pe, "mm", n)
            fill(mm(buf("mm", n), ones[0:1, :], mod_row[0:1, 2 * D + c * 512:2 * D + (c + 1) * 512],
                    start=True, stop=True), "mm", n)
        pe.wait_ge(cx_ready, CT)
        for k in range(0, KD, 2):
            n = turn["tp", "cxT", k]
            claim(pe, "tp", n)
            transposes(n, [cx[:, t, kk * P:(kk + 1) * P] for kk in (k, k + 1) for t in range(CT)])
        drained(pe, "tp", turn["tp", "cxT", KD - 4])
        drained(pe, "tp", turn["tp", "cxT", KD - 2])
        source = {"ck": "k", "cv": "v", "k": "k", "v": "v", "q": "q", "u": "f_in", "ng": "na_gate", "fg": "f_gate"}
        for i, (what, t) in enumerate(PROJ2):
            if (what, t) == ("k", 0):
                pe.wait_ge(xs3_ready, TT)
                for k in range(KD):
                    n = turn["tp", "x3T", k]
                    claim(pe, "tp", n)
                    transposes(n, [xs3[:, tt, k * P:(k + 1) * P] for tt in range(TT)])
                drained(pe, "tp", turn["tp", "x3T", KD - 2])
                drained(pe, "tp", turn["tp", "x3T", KD - 1])
            n = turn["mm", what, t]
            claim(pe, "mm", n)
            w = chunk2(source[what])
            for k in range(KD):
                tile = slice(t * P, (t + 1) * P)
                if what in ("ck", "cv"):
                    left, right = cxT[:, k, tile], w[:, k, :]
                elif what in ("ng", "fg"):
                    left, right = w[:, k, tile], x3T[:, k, :]
                else:
                    left, right = x3T[:, k, tile], w[:, k, :]
                last = mm(buf("mm", n), left, right, start=(k == 0), stop=(k == KD - 1))
            fill(last, "mm", n)
            if i >= 1 and PROJ2[i - 1] in QK2:
                j = QK2.index(PROJ2[i - 1])
                drained(pe, "mm", turn["mm", *QK2[j]])
                n = turn["tp", "qkT2", j]
                claim(pe, "tp", n)
                transposes(n, [pd[:, j % 2, g * P:(g + 1) * P] for g in range(4)])

        drained(pe, "tp", turn["tp", "qkT2", len(QK2) - 2])
        drained(pe, "tp", turn["tp", "qkT2", len(QK2) - 1])
        for s in range(MIXER_STEPS):
            for name, m in mixer_steps(s):
                c, g = divmod(m, 4)
                if name == "scores":
                    n = turn["sc", "scores2", m]
                    claim(pe, "sc", n)
                    for hh in range(2):
                        rows = slice(hh * DH, (hh + 1) * DH)
                        q = q2T[rows, g, c * P:(c + 1) * P]
                        k = k2T[rows, g, :].rearrange("p (r w) -> p r w", w=GRID)[:, :, KEY_COL[c]:KEY_COL[c] + KC]
                        mm(buf("sc", n)[:, hh, 0:256], q, k, start=True, stop=True)
                        last = mm(buf("sc", n)[:, hh, 256:512], q, ckT[rows, g, :], start=True, stop=True)
                    fill(last, "sc", n)
                elif name == "fourier":
                    n = turn["sc", "fourier", m]
                    claim(pe, "sc", n)
                    if m < 4:
                        w = chunk2("dft")
                        if m == 0:
                            drained(pe, "mm", turn["mm", "u", TT - 2])
                            drained(pe, "mm", turn["mm", "u", TT - 1])
                        for a in range(2):
                            for t in range(TT):
                                last = mm(buf("sc", n)[:, a, :], u[:, t, m * P:(m + 1) * P], w[:, 4 * a + t, :],
                                          start=(t == 0), stop=(t == TT - 1))
                    elif m < 6:
                        if m == 4:
                            drained(pe, "sc", turn["sc", "fourier", 2])
                            drained(pe, "sc", turn["sc", "fourier", 3])
                        for b in range(2):
                            for a in range(2):
                                last = mm(buf("sc", n)[:, b, :], chan[:, a, :], seqT[:, 2 * (m - 4) + b, a, :],
                                          start=(a == 0), stop=(a == 1))
                    else:
                        w = chunk2("w_four", 4)
                        if m == 6:
                            drained(pe, "sc", turn["sc", "fourier", 4])
                            drained(pe, "sc", turn["sc", "fourier", 5])
                        for b in range(2):
                            f = 2 * (m - 6) + b
                            for k in range(4):
                                last = mm(buf("sc", n)[:, b, :], w[:, k, f * P:(f + 1) * P], yT[:, k, :],
                                          start=(k == 0), stop=(k == 3))
                    fill(last, "sc", n)
                elif name == "pT":
                    drained(pe, "sc", turn["sc", "scores2", m])
                    for hh in range(2):
                        n = turn["tp", "pT2", 2 * m + hh]
                        claim(pe, "tp", n)
                        transposes(n, [s_buf[:, m % 2, hh, b * P:(b + 1) * P] for b in range(4)])
                elif name == "pv":
                    n = turn["mm", "o2", c]
                    if m == 0:
                        pe.wait_ge(v_win_loaded, 16 * 32)
                    if g == 0:
                        claim(pe, "mm", n)
                    for hh in range(2):
                        cols = slice((2 * g + hh) * DH, (2 * g + hh + 1) * DH)
                        drained(pe, "tp", turn["tp", "pT2", 2 * m + hh])
                        for b in range(4):
                            values = v_win[:, 2 * c + b, cols] if b < 2 else cv[:, b - 2, cols]
                            last = mm(buf("mm", n)[:, cols], pT[:, hh, b * P:(b + 1) * P], values,
                                      start=(b == 0), stop=(b == 3))
                    if g == 3:
                        fill(last, "mm", n)
                elif name == "oT":
                    n = turn["tp", "oT2", m]
                    drained(pe, "mm", turn["mm", "o2", m])
                    claim(pe, "tp", n)
                    transposes(n, [o_sb[:, b * P:(b + 1) * P] for b in range(4)])

        drained(pe, "tp", turn["tp", "oT2", TT - 1])
        for t in range(TT):
            n = turn["sc", "out", t]
            claim(pe, "sc", n)
            for a in range(2):
                w = chunk2(f"w_out{a}")
                for k in range(KD):
                    last = mm(buf("sc", n)[:, a, :], mixT[:, k, t * P:(t + 1) * P], w[:, k, :],
                              start=(k == 0), stop=(k == KD - 1))
            fill(last, "sc", n)

    @block.scalar
    def _(act):
        S = nc.scalar
        with nc.allow_non_contiguous_dma(reason="small vectors laid along partitions"):
            act.dma_start(gain1[:], A["norm_mix"][0].rearrange("(k p) -> p k", p=P)).then_inc(early_loaded, 16)
            for n, name in enumerate(("da_q_norm", "da_k_norm")):
                for c in range(2):
                    act.dma_start(qk_gain[c * DH:(c + 1) * DH, n:n + 1],
                                  A[name].rearrange("a d -> d a")).then_inc(early_loaded, 16)
            act.dma_start(gain2[:], A["norm_ffn"][0].rearrange("(k p) -> p k", p=P)).then_inc(late_loaded, 16)
            act.dma_start(sub_gain[:], A["da_subln"].rearrange("a d -> d a")).then_inc(late_loaded, 16)
            for n, name in enumerate(("da_lambda_q1", "da_lambda_q2", "da_lambda_k1", "da_lambda_k2")):
                act.dma_start(lam_in[:, n, :], A[name].broadcast_to([P, DH])).then_inc(late_loaded, 16)
            act.dma_start(w_rt[:, :, 0:GROUPS], A["moe_w_group"][0].rearrange("(k p) g -> p k g", p=P)).then_inc(late_loaded, 16)
            act.dma_start(w_rt[:, :, GROUPS:20], A["moe_w_router"][0].rearrange("(k p) g -> p k g", p=P)).then_inc(late_loaded, 16)
            act.dma_start(b_rt[:, 0:GROUPS], A["moe_b_group"].broadcast_to([P, GROUPS])).then_inc(late_loaded, 16)
            act.dma_start(b_rt[:, GROUPS:20], A["moe_b_router"].broadcast_to([P, EXPERTS])).then_inc(late_loaded, 16)
            act.dma_start(norm_g[:], A["norm_g_2"][0].rearrange("(k p) -> p k", p=P)).then_inc(second_loaded, 16)
            for n, name in enumerate(("q_norm_g_2", "k_norm_g_2")):
                for c in range(2):
                    act.dma_start(qk_gain2[c * DH:(c + 1) * DH, n:n + 1],
                                  A[name].rearrange("a d -> d a")).then_inc(second_loaded, 16)
            act.dma_start(cond[:, :, 0], A["c_2"][0].rearrange("(k p) -> p k", p=P)).then_inc(second_loaded, 16)
            act.dma_start(cond[:, :, 1], A["c_ctx_2"].rearrange("(k p) -> p k", p=P)).then_inc(second_loaded, 16)
            act.dma_start(mask[:], A["mask"]).then_inc(second_loaded, 16)
            act.dma_start(chan[:], A["chan"]).then_inc(second_loaded, 16)

        for t in range(TT):
            act.wait_ge(x_loaded[t], 16)
            S.activation(xs[:, t, :], x[:, t, :], ACT.Square, accum_out=ssq[:, t:t + 1]).then_inc(ssq_ready, 1)
        act.wait_ge(early_loaded, 5 * 16)
        for k in range(0, KD, 2):
            n = turn["tp", "hT", k]
            filled(act, "tp", n)
            drain(S.activation(hT[:, k, :], buf("tp", n), ACT.Copy, scale=gain1[:, k:k + 1]), "tp", n)

        for i in range(6 * TT):
            c, t = divmod(i, TT)
            n = turn["mm", "proj", i]
            filled(act, "mm", n)
            if c < QK_CHUNKS:
                if i >= 2:
                    act.wait_ge(qk_ms_ready, i - 1)
                S.activation(pT[:, i % 2, :], buf("mm", n), ACT.Square).then_inc(sq_ready, 1)
            else:
                drain(S.copy(v[:, t, (c - QK_CHUNKS) * CH:(c - QK_CHUNKS + 1) * CH], buf("mm", n)), "mm", n)
            if 1 <= i <= QK_CHUNKS * TT:
                c, t = divmod(i - 1, TT)
                n = turn["tp", "qkT", i - 1]
                filled(act, "tp", n)
                if i == 1:
                    act.wait_ge(gains_scaled, 1)
                dst, g = (qT, 0) if c < 2 else (kT, 1)
                drain(S.activation(dst[:, 4 * (c % 2):4 * (c % 2) + 4, t * P:(t + 1) * P],
                                   buf("tp", n).rearrange("p (h n) -> p h n", h=4), ACT.Copy,
                                   scale=qk_gain[:, g:g + 1]), "tp", n)

        act.wait_ge(lam_sum, 1)
        S.activation(lam[:, 2:4], lam[:, 0:2], ACT.Exp).then_inc(lam_exp, 1)
        for s in range(ATTENTION_STEPS):
            for name, m in attention_steps(s):
                t, h = divmod(m, HEADS)
                if name == "scores":
                    act.wait_ge(nmx_ready, m + 1)
                    for c in range(2):
                        sc = s_buf[:, m % 2, c, 0:(t + 1) * P]
                        last = S.activation(sc, sc, ACT.Exp, bias=nmx[:, m % 2, c:c + 1],
                                            accum_out=den[:, m % 2, c:c + 1])
                    last.then_inc(exp_ready, 1)
                elif name == "pdT":
                    n = turn["tp", "pdT", m]
                    filled(act, "tp", n)
                    drain(S.copy(pT[:, m % 2, 0:(t + 1) * P], buf("tp", n)[:, 0:(t + 1) * P]), "tp", n)
                elif name == "o_raw1":
                    drained(act, "mm", turn["mm", "o", 2 * m + 1])
                    S.activation(oT[:, :, m * P:(m + 1) * P], o_sb[:].rearrange("p (h e) -> p h e", h=HEADS),
                                 ACT.Square).then_inc(o_sq_ready, 1)
                elif name == "oT":
                    t = m
                    act.wait_ge(gains_scaled, 2)
                    for b in range(2):
                        n = turn["tp", "oT", 2 * t + b]
                        filled(act, "tp", n)
                        drain(S.activation(oT[:, 4 * b:4 * b + 4, t * P:(t + 1) * P],
                                           buf("tp", n).rearrange("p (h n) -> p h n", h=4), ACT.Copy,
                                           scale=sub_gain[:, 0:1]), "tp", n)

        for t in range(TT):
            drained(act, "sc", turn["sc", "w_out", t])
            S.activation(xs2[:, t, :], x[:, t, :], ACT.Square, accum_out=ssq[:, 4 + t:5 + t]).then_inc(ssq_ready, 1)
        for k in range(0, KD, 2):
            n = turn["tp", "xT2", k]
            filled(act, "tp", n)
            drain(S.copy(xT2[:, k, :], buf("tp", n)), "tp", n)
        act.wait_ge(ge_in, 1)
        S.activation(g_exp[:], g_exp[:], ACT.Exp).then_inc(ge_out, 1)
        act.wait_ge(ge_in, 2)
        S.activation(in_group[:], in_group[:], ACT.Exp).then_inc(ge_out, 1)

        def silu(b, n, n_hid, more=0, more_hid=0):
            filled(act, "sc", n, more)
            if n_hid is not None:
                filled(act, "tp", n_hid, more_hid)
            S.activation(sg[:, b, :], buf("sc", n)[:, 0, :], ACT.Silu).then_inc(sg_ready, 1)

        def hid_copy(b, n, more=0):
            filled(act, "tp", n, more)
            drain(S.copy(hidT[:, b, :], buf("tp", n)), "tp", n)

        def y_copy(b, n, e, stored, more=0):
            filled(act, "sc", n, more)
            if stored is not None:
                act.wait_ge(y_stored[b], stored)
            drain(S.copy(y_sb[:, b, :].rearrange("p (m n) -> p m n", m=2), buf("sc", n)), "sc", n)
            drained(act, "sc", n, more)
            dst = y_d[e * P:(e + 1) * P, :] if isinstance(e, int) else y_d[bass.ds(e * P, P), :]
            act.dma_start(dst, y_sb[:, b, :]).then_inc(y_stored[b], 16)

        silu(0, turn_gu(0), None)
        hid_copy(0, turn_hid(0))
        silu(1, turn_gu(1), None)
        y_copy(0, turn_dn(0), 0, None)
        hid_copy(1, turn_hid(1))
        silu(0, turn_gu(2), turn_hid(0))
        y_copy(1, turn_dn(1), 1, None)
        hid_copy(0, turn_hid(2))
        with act.Fori(0, (EXPERTS - 4) // 2) as j:
            for e in (3, 4):
                silu(e % 2, turn_gu(e), turn_hid(e - 2), 2 * j, 3 * j)
                y_copy((e - 1) % 2, turn_dn(e - 1), 2 * j + (e - 1), 16 * j + 16 * ((e - 1) // 2), 2 * j)
                hid_copy(e % 2, turn_hid(e), 3 * j)
        e = EXPERTS - 1
        silu(1, turn_gu(e), turn_hid(e - 2))
        y_copy(0, turn_dn(e - 1), e - 1, 16 * ((e - 1) // 2))
        hid_copy(1, turn_hid(e))
        y_copy(1, turn_dn(e), e, 16 * (e // 2))

        spills = spill_count(act)
        with act.If(spills > 0):
            act.wait_ge(y_stored[0], 16 * EXPERTS // 2)
            act.sem_inc(spill_y, 16)
            act.sem_inc(spill_act, 1)
            with act.Fori(0, SPILL) as o:
                with act.If(spills > o):
                    act.wait_ge(spill_pe, 4 * o + 3)
                    S.activation(sg[:, 0, :], SC[0][:, 0, :], ACT.Silu).then_inc(spill_act, 1)
                    act.wait_ge(spill_pe, 4 * o + 4)
                    S.copy(hidT[:, 0, :], TP[0]).then_inc(spill_act, 1)
                    act.wait_ge(spill_pe, 4 * o + 5)
                    act.wait_ge(spill_y, 16 * o + 16)
                    S.copy(y_sb[:, 0, :].rearrange("p (m n) -> p m n", m=2), SC[1]).then_inc(spill_act, 1)
                    act.wait_ge(spill_act, 3 * o + 4)
                    act.dma_start(y_d[bass.ds(o * P + EXPERTS * P, P), :], y_sb[:, 0, :]).then_inc(spill_y, 16)

        act.wait_ge(second_loaded, 9 * 16)
        S.activation(cond[:], cond[:], ACT.Silu).then_inc(cond_ready, 1)
        for t in range(CT):
            act.wait_ge(ctx_loaded[t], 16)
            S.activation(buf_d[:, 2048 + t * D:2048 + (t + 1) * D], cx[:, t, :], ACT.Square,
                         accum_out=cssq[:, 0, t:t + 1]).then_inc(c_ssq_ready, 1)
        for c in range(2):
            n = turn["mm", "g_x", c]
            filled(act, "mm", n)
            drain(S.copy(g_x[:, c * 512:(c + 1) * 512], buf("mm", n)), "mm", n)
        act.wait_ge(mod_ready, 1)
        for k in range(0, KD, 2):
            n = turn["tp", "cxT", k]
            filled(act, "tp", n)
            for kk in range(2):
                last = S.activation(cxT[:, k + kk, :], buf("tp", n)[:, kk * CTX:(kk + 1) * CTX], ACT.Identity,
                                    bias=mod_sh[:, 1, k + kk:k + kk + 1], scale=mod_g[:, 1, k + kk:k + kk + 1])
            drain(last, "tp", n)
        qk_from = QK_CHUNKS * TT

        def qk_squares(j):
            n = turn["mm", *QK2[j]]
            filled(act, "mm", n)
            if j >= 2:
                act.wait_ge(qk_ms_ready, qk_from + j - 1)
            S.activation(pT[:, j % 2, :], buf("mm", n), ACT.Square).then_inc(sq_ready, 1)

        for i, (what, t) in enumerate(PROJ2):
            n = turn["mm", what, t]
            if (what, t) == ("k", 0):
                for tt in range(TT):
                    act.wait_ge(x2_ready, tt + 1)
                    if tt >= 2:
                        act.wait_ge(ssq_ready, 8 + tt - 1)
                    S.activation(s_buf[:, tt % 2].rearrange("p a n -> p (a n)"), x[:, tt, :], ACT.Square,
                                 accum_out=ssq[:, tt:tt + 1]).then_inc(ssq_ready, 1)
                for k in range(0, KD, 2):
                    nk = turn["tp", "x3T", k]
                    filled(act, "tp", nk)
                    drain(S.activation(x3T[:, k, :], buf("tp", nk), ACT.Identity, bias=mod_sh[:, 0, k:k + 1],
                                       scale=mod_g[:, 0, k:k + 1]), "tp", nk)
            if (what, t) in QK2:
                qk_squares(QK2.index((what, t)))
            else:
                filled(act, "mm", n)
                if what == "cv":
                    drain(S.copy(cv[:, t, :], buf("mm", n)), "mm", n)
                elif what == "v":
                    if t >= 2:
                        act.wait_ge(v_stored[t % 2], 16)
                    drain(S.copy(o_sb[:, (t % 2) * 512:(t % 2 + 1) * 512], buf("mm", n)), "mm", n)
                    drained(act, "mm", n)
                    act.dma_start(v_d[t * P:(t + 1) * P, :], o_sb[:, (t % 2) * 512:(t % 2 + 1) * 512]).then_inc(v_stored[t % 2], 16)
                elif what == "u":
                    drain(S.copy(u[:, t, :], buf("mm", n)), "mm", n)
                else:
                    dst = ngT if what == "ng" else fgT
                    drain(S.activation(dst[:, t, :], buf("mm", n), ACT.Silu), "mm", n)
            if i >= 1 and PROJ2[i - 1] in QK2:
                j = QK2.index(PROJ2[i - 1])
                what, t = QK2[j]
                n = turn["tp", "qkT2", j]
                filled(act, "tp", n)
                if what == "q":
                    for r in range(2):
                        dst = q2T.rearrange("p g (c r w) -> p g c r w", c=TT, r=ROWS_G)[:, :, :, 2 * t + r, :]
                        src = buf("tp", n).rearrange("p (g r c w) -> p g r c w", g=4, r=2, c=TT)[:, :, r, :, ::-1]
                        last = S.activation(dst, src, ACT.Copy, scale=qk_gain2[:, 0:1])
                    drain(last, "tp", n)
                else:
                    dst = ckT if what == "ck" else k2T
                    drain(S.activation(dst[:, :, t * P:(t + 1) * P], buf("tp", n).rearrange("p (g n) -> p g n", g=4),
                                       ACT.Copy, scale=qk_gain2[:, 1:2]), "tp", n)

        for s in range(MIXER_STEPS):
            for name, m in mixer_steps(s):
                if name == "scores":
                    n = turn["sc", "scores2", m]
                    act.wait_ge(neg_max, m + 1)
                    if m >= 2:
                        filled(act, "tp", turn["tp", "pT2", 2 * (m - 2) + 1])
                    for hh in range(2):
                        last = S.activation(s_buf[:, m % 2, hh, :], buf("sc", n)[:, hh, :], ACT.Exp,
                                            bias=nmx[:, m % 2, hh:hh + 1],
                                            accum_out=rden[:, (m // 4) % 2, 2 * (m % 4) + hh:2 * (m % 4) + hh + 1])
                    drain(last, "sc", n)
                elif name == "fourier" and m < 6:
                    n = turn["sc", "fourier", m]
                    filled(act, "sc", n)
                    if m == 0:
                        act.wait_ge(bias_ready, 3)
                    dst = seqT[:, m, :, :] if m < 4 else yT[:, 2 * (m - 4):2 * (m - 4) + 2, :]
                    drain(S.copy(dst, buf("sc", n)), "sc", n)
                elif name == "pT":
                    for hh in range(2):
                        n = turn["tp", "pT2", 2 * m + hh]
                        filled(act, "tp", n)
                        drain(S.copy(pT[:, hh, :], buf("tp", n)), "tp", n)

    @block.vector
    def _(dve):
        V = nc.vector
        links = [0]

        def link(ins):
            links[0] += 1
            ins.then_inc(dve_done, 1)
            dve.wait_ge(dve_done, links[0])

        for t in range(TT):
            dve.wait_ge(ssq_ready, t + 1)
            V.tensor_scalar(ms[:, t:t + 1], ssq[:, t:t + 1], 1.0 / D, EPS, ALU.mult, ALU.add).then_inc(ms_ready, 1)
            dve.wait_ge(rstd_ready, t + 1)
            V.tensor_scalar(xs[:, t, :], x[:, t, :], rstd[:, t:t + 1], None, ALU.mult).then_inc(xs_ready, 1)
        dve.wait_ge(early_loaded, 5 * 16)
        V.tensor_scalar(qk_gain[:, 0:1], qk_gain[:, 0:1], DH ** -0.5, None, ALU.mult).then_inc(gains_scaled, 1)
        for k in range(1, KD, 2):
            n = turn["tp", "hT", k]
            filled(dve, "tp", n)
            drain(V.tensor_scalar(hT[:, k, :], buf("tp", n), gain1[:, k:k + 1], None, ALU.mult), "tp", n)

        for i in range(QK_CHUNKS * TT):
            b = i % 2
            dve.wait_ge(sq_ready, i + 1)
            link(V.tensor_reduce(qk_st[:, b, 0, :], pT[:, b, :].rearrange("p (g d) -> p g d", d=DH), AX.X, ALU.add))
            V.tensor_scalar(qk_st[:, b, 1, :], qk_st[:, b, 0, :], 1.0 / DH, EPS, ALU.mult, ALU.add).then_inc(qk_ms_ready, 1)
            dve.wait_ge(qk_rstd_ready, i + 1)
            n = turn["mm", "proj", i]
            filled(dve, "mm", n)
            if i >= 2:
                filled(dve, "tp", turn["tp", "qkT", i - 2])
            drain(V.tensor_tensor(pd[:, b, :].rearrange("p (g d) -> p g d", d=DH),
                                  buf("mm", n).rearrange("p (g d) -> p g d", d=DH),
                                  qk_st[:, b, 2, :].unsqueeze(2).to_broadcast([P, 8, DH]), ALU.mult), "mm", n)

        dve.wait_ge(late_loaded, 10 * 16)
        V.tensor_scalar(sub_gain[:], sub_gain[:], 1.0 - LAMBDA_INIT, None, ALU.mult).then_inc(gains_scaled, 1)
        link(V.tensor_tensor(lam_pr[:], lam_in[:, 0:2, :], lam_in[:, 2:4, :], ALU.mult))
        V.tensor_reduce(lam[:, 0:2], lam_pr[:], AX.X, ALU.add).then_inc(lam_sum, 1)
        V.tensor_tensor(w_rt[:], w_rt[:], gain2[:].unsqueeze(2).to_broadcast([P, KD, 20]), ALU.mult).then_inc(w_rt_ready, 1)
        dve.wait_ge(lam_exp, 1)
        link(V.tensor_tensor(lam[:, 0:1], lam[:, 3:4], lam[:, 2:3], ALU.subtract))
        link(V.tensor_scalar(lam[:, 1:2], lam[:, 0:1], LAMBDA_INIT, None, ALU.subtract))
        neg_lambda = lam[:, 1:2]
        dve.wait_ge(pool_consts, 2)

        for s in range(ATTENTION_STEPS):
            for name, m in attention_steps(s):
                t, h = divmod(m, HEADS)
                b = m % 2
                w = (t + 1) * P
                if name == "scores":
                    n = turn["sc", "scores", m]
                    filled(dve, "sc", n)
                    if m >= 2:
                        dve.wait_ge(pd_ready, m - 1)
                    drain(V.scalar_tensor_tensor(out=s_buf[:, b, :, 0:w],
                                                 in0=dist[:, 512 - w:512].unsqueeze(1).to_broadcast([P, 2, w]),
                                                 scalar=2.0 ** -(h + 1), in1=buf("sc", n)[:, :, 0:w],
                                                 op0=ALU.mult, op1=ALU.add), "sc", n)
                    drained(dve, "sc", n)
                    V.tensor_reduce(nmx[:, b, :], s_buf[:, b, :, 0:w], AX.X, ALU.max, negate=True).then_inc(nmx_ready, 1)
                elif name == "pd":
                    dve.wait_ge(exp_ready, m + 1)
                    V.reciprocal(rden[:, t % 2, h:h + 1], den[:, b, 0:1])
                    link(V.reciprocal(ratio[:, b, 0:1], den[:, b, 1:2]))
                    link(V.scalar_tensor_tensor(out=ratio[:, b, 1:2], in0=den[:, b, 0:1], scalar=neg_lambda,
                                                in1=ratio[:, b, 0:1], op0=ALU.mult, op1=ALU.mult))
                    if m >= 2:
                        filled(dve, "tp", turn["tp", "pdT", m - 2])
                    V.scalar_tensor_tensor(out=pd[:, b, 0:w], in0=s_buf[:, b, 1, 0:w], scalar=ratio[:, b, 1:2],
                                           in1=s_buf[:, b, 0, 0:w], op0=ALU.mult, op1=ALU.add).then_inc(pd_ready, 1)
                elif name in ("o_raw0", "o_raw1"):
                    t, g = m, int(name[-1])
                    if t > 0 and g == 0:
                        filled(dve, "tp", turn["tp", "oT", 2 * t - 1])
                    n = turn["mm", "o", 2 * t + g]
                    filled(dve, "mm", n)
                    drain(V.tensor_tensor(o_sb[:, g * 512:(g + 1) * 512].rearrange("p (h e) -> p h e", h=4),
                                          buf("mm", n).rearrange("p (h e) -> p h e", h=4),
                                          rden[:, t % 2, 4 * g:4 * g + 4].unsqueeze(2).to_broadcast([P, 4, P]),
                                          ALU.mult), "mm", n)
                elif name == "o_mean":
                    dve.wait_ge(o_sq_ready, m + 1)
                    link(V.tensor_reduce(o_st[:, 0, :], oT[:, :, m * P:(m + 1) * P], AX.X, ALU.add))
                    V.tensor_scalar(o_st[:, 1, :], o_st[:, 0, :], 1.0 / P, EPS, ALU.mult, ALU.add).then_inc(o_ms_ready, 1)
                elif name == "o_norm":
                    dve.wait_ge(o_rstd_ready, m + 1)
                    o3 = o_sb[:].rearrange("p (h e) -> p h e", h=HEADS)
                    V.tensor_tensor(o3, o3, o_st[:, 2, :].unsqueeze(2).to_broadcast([P, HEADS, P]),
                                    ALU.mult).then_inc(o_norm_ready, 1)
                elif name == "x_add":
                    n = turn["sc", "w_out", m]
                    filled(dve, "sc", n)
                    xt = x[:, m, :].rearrange("p (c n) -> p c n", c=2)
                    drain(V.tensor_tensor(xt, xt, buf("sc", n), ALU.add), "sc", n)

        for t in range(TT):
            dve.wait_ge(ssq_ready, 4 + t + 1)
            V.tensor_scalar(ms[:, 4 + t:5 + t], ssq[:, 4 + t:5 + t], 1.0 / D, EPS, ALU.mult, ALU.add).then_inc(ms_ready, 1)
        for t in range(TT):
            dve.wait_ge(rstd_ready, 4 + t + 1)
            V.tensor_scalar(xs2[:, t, :], x[:, t, :], rstd[:, 4 + t:5 + t], None, ALU.mult).then_inc(xs2_ready, 1)
        for k in range(1, KD, 2):
            n = turn["tp", "xT2", k]
            filled(dve, "tp", n)
            drain(V.tensor_copy(xT2[:, k, :], buf("tp", n)), "tp", n)

        def wide(ap, k):
            return ap.unsqueeze(2).to_broadcast([P, TT, k])

        n = turn["mm", "router"]
        filled(dve, "mm", n)
        drain(V.tensor_tensor(logit[:], buf("mm", n)[:, 0:TT * 20].rearrange("p (t e) -> p t e", t=TT),
                              b_rt[:].unsqueeze(1).to_broadcast([P, TT, 20]), ALU.add), "mm", n)
        drained(dve, "mm", n)
        dve.wait_ge(pool_consts, 3)

        def first_of_max(out_ap, values, top, k=4):
            link(V.tensor_tensor(r_b[:], values, wide(top, k), ALU.is_equal))
            link(V.tensor_tensor(r_c[:], r_b[:], prio[:].unsqueeze(1).to_broadcast([P, TT, k]), ALU.mult))
            link(V.tensor_reduce(r_m[:, 5, :], r_c[:], AX.X, ALU.max))
            link(V.tensor_tensor(out_ap, r_c[:], wide(r_m[:, 5, :], k), ALU.is_equal))

        groups = logit[:, :, 0:GROUPS]
        link(V.tensor_reduce(r_m[:, 0, :], groups, AX.X, ALU.max))
        V.tensor_tensor(g_exp[:], groups, wide(r_m[:, 0, :], GROUPS), ALU.subtract).then_inc(ge_in, 1)
        first_of_max(g_pick[:], groups, r_m[:, 0, :])
        link(V.tensor_tensor(r_a[:].rearrange("p t (g e) -> p t g e", g=GROUPS),
                             logit[:, :, GROUPS:20].rearrange("p t (g e) -> p t g e", g=GROUPS),
                             g_pick[:].unsqueeze(3).to_broadcast([P, TT, GROUPS, PER_GROUP]), ALU.mult))
        link(V.tensor_reduce(in_group[:], r_a[:].rearrange("p t (g e) -> p t e g", g=GROUPS), AX.X, ALU.add))
        link(V.tensor_reduce(r_m[:, 1, :], in_group[:], AX.X, ALU.max))
        V.tensor_tensor(in_group[:], in_group[:], wide(r_m[:, 1, :], PER_GROUP), ALU.subtract).then_inc(ge_in, 1)
        dve.wait_ge(ge_out, 2)
        link(V.tensor_reduce(r_m[:, 1, :], in_group[:], AX.X, ALU.max))
        first_of_max(e_pick[:, 0], in_group[:], r_m[:, 1, :])
        link(V.scalar_tensor_tensor(out=in_group[:], in0=e_pick[:, 0], scalar=-4.0, in1=in_group[:],
                                    op0=ALU.mult, op1=ALU.add))
        link(V.tensor_reduce(r_m[:, 2, :], in_group[:], AX.X, ALU.max))
        first_of_max(e_pick[:, 1], in_group[:], r_m[:, 2, :])
        for c in range(2):
            last = V.tensor_tensor(picks[:, c].rearrange("p t (g e) -> p t g e", g=GROUPS),
                                   g_pick[:].unsqueeze(3).to_broadcast([P, TT, GROUPS, PER_GROUP]),
                                   e_pick[:, c].unsqueeze(2).to_broadcast([P, TT, GROUPS, PER_GROUP]), ALU.mult)
        link(last)
        V.tensor_tensor(sel[:], picks[:, 0], picks[:, 1], ALU.add).then_inc(sel_ready, 1)
        link(V.tensor_reduce(r_m[:, 3, :], g_exp[:], AX.X, ALU.add))
        link(V.tensor_tensor(r_m[:, 4, :], r_m[:, 1, :], r_m[:, 2, :], ALU.add))
        link(V.tensor_tensor(r_m[:, 3, :], r_m[:, 3, :], r_m[:, 4, :], ALU.mult))
        link(V.reciprocal(r_m[:, 4, :], r_m[:, 3, :]))
        V.tensor_tensor(weight[:, 0, :], r_m[:, 1, :], r_m[:, 4, :], ALU.mult)
        V.tensor_tensor(weight[:, 1, :], r_m[:, 2, :], r_m[:, 4, :], ALU.mult)
        n = turn["mm", "places"]
        filled(dve, "mm", n)
        drain(V.tensor_copy(place[:], buf("mm", n)[:, 0:(TT + 1) * 16].rearrange("p (t e) -> p t e", e=16)), "mm", n)
        drained(dve, "mm", n)
        length = place[:, TT, :]
        tiles, upto = full_tiles[:, 0, :], full_tiles[:, 1, :]
        link(V.tensor_scalar(tiles, length, float(P), None, ALU.is_gt))
        for q in (2, 3):
            link(V.scalar_tensor_tensor(out=tiles, in0=length, scalar=float(q * P), in1=tiles, op0=ALU.is_gt, op1=ALU.add))
        link(V.tensor_tensor_scan(upto, ones[:, 0:16], tiles, 0.0, ALU.mult, ALU.add))
        before = s_buf[:, 0, 0, 0:SPILL * EXPERTS].rearrange("p (o e) -> p o e", o=SPILL)
        spill_f = s_buf[:, 0, 1, 0:SPILL + 1]
        link(V.tensor_tensor(before, upto.unsqueeze(1).to_broadcast([P, SPILL, EXPERTS]),
                             iota16[:, 0:SPILL].unsqueeze(2).to_broadcast([P, SPILL, EXPERTS]), ALU.is_le))
        V.tensor_reduce(spill_f[:, 0:SPILL], before, AX.X, ALU.add)
        link(V.tensor_copy(spill_f[:, SPILL:SPILL + 1], upto[:, EXPERTS - 1:EXPERTS]))
        link(V.tensor_scalar(spill_f, spill_f, float(EXPERTS - 1), None, ALU.min))
        V.tensor_copy(spill_i[:], spill_f).then_inc(spill_ready, 1)
        spill_base, step_back = full_tiles[:, 2, :], full_tiles[:, 3, :]
        link(V.tensor_tensor(spill_base, upto, tiles, ALU.subtract))
        link(V.tensor_scalar(spill_base, spill_base, float(P), float((EXPERTS - 1) * P), ALU.mult, ALU.add))
        link(V.scalar_tensor_tensor(out=step_back, in0=iota16[:], scalar=float(P), in1=spill_base,
                                    op0=ALU.mult, op1=ALU.subtract))
        link(V.tensor_scalar(r_a[:], place[:, 0:TT, :], float(P), None, ALU.is_lt))
        link(V.tensor_tensor(r_a[:], r_a[:], step_back.unsqueeze(1).to_broadcast([P, TT, EXPERTS]), ALU.mult))
        link(V.tensor_tensor(r_a[:], r_a[:], spill_base.unsqueeze(1).to_broadcast([P, TT, EXPERTS]), ALU.add))
        link(V.tensor_tensor(r_a[:], r_a[:], place[:, 0:TT, :], ALU.add))
        for c in range(2):
            link(V.tensor_tensor(picks[:, c], picks[:, c], r_a[:], ALU.mult))
            link(V.tensor_reduce(row_f[:, c, :], picks[:, c], AX.X, ALU.add))
        V.tensor_copy(row_i[:], row_f[:]).then_inc(rows_ready, 1)

        def x_copy(b, n, more=0):
            for half_row in range(2):
                filled(dve, "tp", n + half_row, more)
                drain(V.tensor_tensor(xgT[:, b, 4 * half_row:4 * half_row + 4, :],
                                      buf("tp", n + half_row).rearrange("p (k n) -> p k n", k=4),
                                      gain2[:, 4 * half_row:4 * half_row + 4].unsqueeze(2).to_broadcast([P, 4, P]),
                                      ALU.mult), "tp", n + half_row)

        def hidden(b, n, n_sg, more=0):
            dve.wait_ge(sg_ready, n_sg)
            filled(dve, "sc", n, more)
            drain(V.tensor_tensor(sg[:, b, :], sg[:, b, :], buf("sc", n)[:, 1, :], ALU.mult), "sc", n)

        x_copy(0, turn_x(0))
        hidden(0, turn_gu(0), 1)
        x_copy(1, turn_x(1))
        with dve.Fori(0, EXPERTS // 2 - 1) as j:
            for e in (1, 2):
                hidden(e % 2, turn_gu(e), 2 * j + (e + 1), 2 * j)
                x_copy((e + 1) % 2, turn_x(e + 1), 3 * j)
        e = EXPERTS - 1
        hidden(1, turn_gu(e), e + 1)

        spills = spill_count(dve)
        with dve.If(spills > 0):
            with dve.Fori(0, SPILL) as o:
                with dve.If(spills > o):
                    dve.wait_ge(spill_pe, 4 * o + 2)
                    for half_row in range(2):
                        last = V.tensor_tensor(xgT[:, 0, 4 * half_row:4 * half_row + 4, :],
                                               TP[half_row].rearrange("p (k n) -> p k n", k=4),
                                               gain2[:, 4 * half_row:4 * half_row + 4].unsqueeze(2).to_broadcast([P, 4, P]),
                                               ALU.mult)
                    last.then_inc(spill_dve, 1)
                    dve.wait_ge(spill_act, 3 * o + 2)
                    V.tensor_tensor(sg[:, 0, :], sg[:, 0, :], SC[0][:, 1, :], ALU.mult).then_inc(spill_dve, 1)

        def add_rows(t):
            for c in range(2):
                dve.wait_ge(yg_ready[(2 * t + c) % 4], 16 * ((2 * t + c) // 4 + 1))
                ins = V.scalar_tensor_tensor(out=x[:, t, :], in0=yg[:, (2 * t + c) % 4, :], scalar=weight[:, c, t:t + 1],
                                             in1=x[:, t, :], op0=ALU.mult, op1=ALU.add)
                if c == 0:
                    link(ins)
            ins.then_inc(x2_ready, 1)

        for c in range(6):
            n = turn["mm", "ada", c]
            filled(dve, "mm", n)
            if c % 2 == 0:
                dve.wait_ge(b_ada_loaded, 16 * (c // 2 + 1))
            drain(V.tensor_tensor(mod_row[:, c * 512:(c + 1) * 512], buf("mm", n)[0:2, :],
                                  b_ada[:, (c % 2) * 512:(c % 2 + 1) * 512], ALU.add), "mm", n)
        dve.wait_ge(second_loaded, 9 * 16)
        V.tensor_scalar(qk_gain2[:, 0:1], qk_gain2[:, 0:1], DH ** -0.5, None, ALU.mult)
        n = turn["tp", "mod"]
        filled(dve, "tp", n)
        modT = buf("tp", n)[:, 0:4 * KD].rearrange("p (a k b) -> p a b k", a=2, k=KD)
        V.tensor_copy(mod_sh[:], modT[:, 0])
        drain(V.tensor_copy(mod_g[:], modT[:, 1]), "tp", n)
        drained(dve, "tp", n)
        V.scalar_tensor_tensor(out=mod_g[:], in0=mod_g[:], scalar=1.0, in1=norm_g[:].unsqueeze(1).to_broadcast([P, 2, KD]),
                               op0=ALU.add, op1=ALU.mult).then_inc(mod_ready, 1)
        dve.wait_ge(mod_ready, 1)
        for t in range(CT):
            dve.wait_ge(c_ssq_ready, t + 1)
            V.tensor_scalar(cssq[:, 1, t:t + 1], cssq[:, 0, t:t + 1], 1.0 / D, EPS, ALU.mult, ALU.add).then_inc(c_ms_ready, 1)
            dve.wait_ge(c_rstd_ready, t + 1)
            V.tensor_scalar(cx[:, t, :], cx[:, t, :], cssq[:, 2, t:t + 1], None, ALU.mult).then_inc(cx_ready, 1)

        qk_from = QK_CHUNKS * TT
        for j, item in enumerate(QK2):
            if item == ("k", 0):
                for t in range(TT):
                    add_rows(t)
                for t in range(TT):
                    dve.wait_ge(ssq_ready, 8 + t + 1)
                    V.tensor_scalar(ms[:, t:t + 1], ssq[:, t:t + 1], 1.0 / D, EPS, ALU.mult, ALU.add).then_inc(ms_ready, 1)
                for t in range(TT):
                    dve.wait_ge(rstd_ready, 8 + t + 1)
                    V.tensor_scalar(xs3[:, t, :], x[:, t, :], rstd[:, t:t + 1], None, ALU.mult).then_inc(xs3_ready, 1)
                for k in range(1, KD, 2):
                    n = turn["tp", "x3T", k]
                    filled(dve, "tp", n)
                    drain(V.tensor_scalar(x3T[:, k, :], buf("tp", n), mod_g[:, 0, k:k + 1], mod_sh[:, 0, k:k + 1],
                                          ALU.mult, ALU.add), "tp", n)
            b = j % 2
            dve.wait_ge(sq_ready, qk_from + j + 1)
            link(V.tensor_reduce(qk_st[:, b, 0, :], pT[:, b, :].rearrange("p (g d) -> p g d", d=DH), AX.X, ALU.add))
            V.tensor_scalar(qk_st[:, b, 1, :], qk_st[:, b, 0, :], 1.0 / DH, EPS, ALU.mult, ALU.add).then_inc(qk_ms_ready, 1)
            dve.wait_ge(qk_rstd_ready, qk_from + j + 1)
            n = turn["mm", *item]
            filled(dve, "mm", n)
            if j >= 2:
                filled(dve, "tp", turn["tp", "qkT2", j - 2])
            drain(V.tensor_tensor(pd[:, b, :].rearrange("p (g d) -> p g d", d=DH),
                                  buf("mm", n).rearrange("p (g d) -> p g d", d=DH),
                                  qk_st[:, b, 2, :].unsqueeze(2).to_broadcast([P, 8, DH]), ALU.mult), "mm", n)

        for s in range(MIXER_STEPS):
            for name, m in mixer_steps(s):
                c, g = divmod(m, 4)
                if name == "scores":
                    n = turn["sc", "scores2", m]
                    filled(dve, "sc", n)
                    dve.wait_ge(bias_ready, MASK[c] + 1)
                    local = buf("sc", n)[:, :, 0:256]
                    link(V.tensor_tensor(local, local, bias[MASK[c]].rearrange("p (h n) -> p h n", h=H2)[:, 2 * g:2 * g + 2, :],
                                         ALU.add))
                    V.tensor_reduce(nmx[:, m % 2, :], buf("sc", n), AX.X, ALU.max, negate=True).then_inc(neg_max, 1)
                elif name == "fourier" and m >= 6:
                    n = turn["sc", "fourier", m]
                    filled(dve, "sc", n)
                    drain(V.tensor_tensor(mixT[:, 2 * (m - 6):2 * (m - 6) + 2, :], buf("sc", n),
                                          fgT[:, 2 * (m - 6):2 * (m - 6) + 2, :], ALU.mult), "sc", n)
                elif name == "pv" and g == 3:
                    n = turn["mm", "o2", c]
                    drained(dve, "sc", turn["sc", "scores2", m])
                    link(V.reciprocal(rden[:, c % 2, :], rden[:, c % 2, :]))
                    filled(dve, "mm", n)
                    if c > 0:
                        filled(dve, "tp", turn["tp", "oT2", c - 1])
                    drain(V.tensor_tensor(o_sb[:, 0:512].rearrange("p (h d) -> p h d", h=H2),
                                          buf("mm", n).rearrange("p (h d) -> p h d", h=H2),
                                          rden[:, c % 2, :].unsqueeze(2).to_broadcast([P, H2, DH]), ALU.mult), "mm", n)
                elif name == "oT":
                    n = turn["tp", "oT2", m]
                    filled(dve, "tp", n)
                    cols = slice(m * QC, (m + 1) * QC)
                    grid = lambda ap: ap.rearrange("p f (r w) -> p f r w", w=GRID)[:, :, :, cols]
                    drain(V.tensor_tensor(grid(mixT[:, 4:8, :]), buf("tp", n).rearrange("p (f r w) -> p f r w", f=4, r=ROWS_G)[:, :, :, ::-1],
                                          grid(ngT[:, :, :]), ALU.mult), "tp", n)

        for t in range(TT):
            n = turn["sc", "out", t]
            filled(dve, "sc", n)
            gated = o_sb[:] if t % 2 == 0 else pd[:, :, :].rearrange("p a n -> p (a n)")
            if t >= 2:
                dve.wait_ge(out_ready, t - 1)
            drain(V.tensor_tensor(gated.rearrange("p (a n) -> p a n", a=2), buf("sc", n),
                                  g_x[:].rearrange("p (a n) -> p a n", a=2), ALU.mult), "sc", n)
            drained(dve, "sc", n)
            V.tensor_tensor(x[:, t, :], x[:, t, :], gated, ALU.add).then_inc(out_ready, 1)

    @block.gpsimd
    def _(pool):
        G = nc.gpsimd
        links = [0]

        def link(ins):
            links[0] += 1
            ins.then_inc(pool_done, 1)
            pool.wait_ge(pool_done, links[0])

        link(G.memset(half[:], -0.5))
        link(G.memset(ones[:], 1.0))
        G.affine_select(out=ident[:], in_=ones[:], compare_op=ALU.is_equal, fill=0.0, base=0,
                        pattern=[[1, P]], channel_multiplier=-1).then_inc(pool_consts, 1)

        def power(dst, src, width, signal):
            G.tensor_tensor(dst, src, half[:, 0:width], ALU.pow).then_inc(signal, 1)

        for t in range(TT):
            pool.wait_ge(ms_ready, t + 1)
            power(rstd[:, t:t + 1], ms[:, t:t + 1], 1, rstd_ready)
        link(G.iota(dist, pattern=[[1, 512]], base=P - 512, channel_multiplier=-1,
                    allow_small_or_imprecise_dtypes=True))
        G.affine_select(out=dist, in_=dist, compare_op=ALU.is_ge, fill=-BIG, base=512 - P,
                        pattern=[[-1, 512]], channel_multiplier=1).then_inc(pool_consts, 1)
        G.affine_select(out=tri[:], in_=ones[:], compare_op=ALU.is_gt, fill=0.0, base=0,
                        pattern=[[1, P]], channel_multiplier=-1)
        G.iota(iota16[:], pattern=[[1, 16]], base=0, channel_multiplier=0, allow_small_or_imprecise_dtypes=True)
        G.iota(prio[:], pattern=[[-1, 4]], base=4, channel_multiplier=0, allow_small_or_imprecise_dtypes=True)
        link(G.memset(zeros[:], 0.0))
        G.iota(tok_i[:], pattern=[[P, TT]], base=0, channel_multiplier=1).then_inc(pool_consts, 1)
        pool.wait_ge(pool_consts, 3)
        pool.dma_start(ids_d.rearrange("(p c) a -> p (c a)", p=P), zeros[:, 0:ROWS // P].bitcast(I32)).then_inc(ids_zeroed, 16)
        pool.dma_start(y_d[EXPERTS * P:ROWS, :].rearrange("(p s) (c n) -> p (s c) n", p=P, n=P),
                       zeros[:].unsqueeze(1).to_broadcast([P, SPILL * KD, P])).then_inc(y_zeroed, 16)
        for i in range(QK_CHUNKS * TT):
            pool.wait_ge(qk_ms_ready, i + 1)
            power(qk_st[:, i % 2, 2, :], qk_st[:, i % 2, 1, :], 8, qk_rstd_ready)
        for t in range(TT):
            pool.wait_ge(o_ms_ready, t + 1)
            power(o_st[:, 2, :], o_st[:, 1, :], 8, o_rstd_ready)
        for t in range(TT, 2 * TT):
            pool.wait_ge(ms_ready, t + 1)
            power(rstd[:, t:t + 1], ms[:, t:t + 1], 1, rstd_ready)
        for t in range(TT):
            pool.wait_ge(xs2_ready, t + 1)
            pool.dma_start(xn_d[t * P:(t + 1) * P, :], xs2[:, t, :]).then_inc(xn_stored, 16)
        pool.wait_ge(rows_ready, 1)
        pool.wait_ge(ids_zeroed, 16)
        for c in range(2):
            for t in range(TT):
                pool.indirect_dma_start(out=ids_d, out_offset=bass.IndirectOffsetOnAxis(ap=row_i[:, c, t:t + 1], axis=0),
                                        in_=tok_i[:, t:t + 1], in_offset=None).then_inc(ids_stored, 16)
        pool.wait_ge(ids_stored, 8 * 16)
        pool.wait_ge(xn_stored, TT * 16)

        for e in range(EXPERTS):
            b = e % 2
            if e >= 2:
                filled(pool, "tp", turn_x(e - 2) + 1)
            pool.dma_start(idx[:, b:b + 1], ids_d[e * P:(e + 1) * P, :]).then_inc(idx_loaded[b], 16)
            pool.wait_ge(idx_loaded[b], 16 * (e // 2 + 1))
            pool.indirect_dma_start(out=xg[:, b, :], out_offset=None, in_=xn_d,
                                    in_offset=bass.IndirectOffsetOnAxis(ap=idx[:, b:b + 1], axis=0)
                                    ).then_inc(xg_ready[b], 16)
        spills = spill_count(pool)
        for o in range(SPILL):
            with pool.If(spills > o):
                pool.wait_ge(spill_pe, 4 * o + 1)
                pool.dma_start(idx[:, 0:1], ids_d[(EXPERTS + o) * P:(EXPERTS + o + 1) * P, :]).then_inc(spill_idx, 16)
                pool.wait_ge(spill_idx, 16 * (o + 1))
                pool.indirect_dma_start(out=xg[:, 0, :], out_offset=None, in_=xn_d,
                                        in_offset=bass.IndirectOffsetOnAxis(ap=idx[:, 0:1], axis=0)
                                        ).then_inc(spill_x, 16)
                pool.wait_ge(spill_y, 16 * (o + 2))
        filled(pool, "sc", turn_gu(0))
        for t in range(CT):
            pool.dma_start(cx[:, t, :], A["ctx_2"][0, t * P:(t + 1) * P, :]).then_inc(ctx_loaded[t], 16)
        for c in range(3):
            if c > 0:
                drained(pool, "mm", turn["mm", "ada", 2 * c - 1])
            pool.dma_start(b_ada, A["b_ada_2"][:, c * D:(c + 1) * D].broadcast_to([2, D])).then_inc(b_ada_loaded, 16)
        for t in range(CT):
            pool.wait_ge(c_ms_ready, t + 1)
            power(cssq[:, 2, t:t + 1], cssq[:, 1, t:t + 1], 1, c_rstd_ready)
        for j in range(CT):
            pool.wait_ge(qk_ms_ready, QK_CHUNKS * TT + j + 1)
            power(qk_st[:, j % 2, 2, :], qk_st[:, j % 2, 1, :], 8, qk_rstd_ready)
        pool.wait_ge(y_zeroed, 16)
        pool.wait_ge(y_stored[0], 16 * EXPERTS // 2)
        pool.wait_ge(y_stored[1], 16 * EXPERTS // 2)
        for i in range(2 * TT):
            t, c = divmod(i, 2)
            if i >= 4:
                pool.wait_ge(x2_ready, (i - 4) // 2 + 1)
            pool.indirect_dma_start(out=yg[:, i % 4, :], out_offset=None, in_=y_d,
                                    in_offset=bass.IndirectOffsetOnAxis(ap=row_i[:, c, t:t + 1], axis=0)
                                    ).then_inc(yg_ready[i % 4], 16)
        for t in range(TT):
            pool.wait_ge(ms_ready, 8 + t + 1)
            power(rstd[:, t:t + 1], ms[:, t:t + 1], 1, rstd_ready)
        def bias_table(i):
            shift = (16, 8, 0)[i]
            G.tensor_tensor(bias[i].rearrange("p (h r n) -> p r h n", h=H2, r=ROWS_G), rel[:, :, :, shift:shift + KC],
                            mask[:, i, :].unsqueeze(1).unsqueeze(1).to_broadcast([P, ROWS_G, H2, KC]),
                            ALU.add).then_inc(bias_ready, 1)

        for j in range(CT, len(QK2)):
            pool.wait_ge(qk_ms_ready, QK_CHUNKS * TT + j + 1)
            power(qk_st[:, j % 2, 2, :], qk_st[:, j % 2, 1, :], 8, qk_rstd_ready)
            if j == len(QK2) - 1:
                pool.wait_ge(rel_loaded, 16 * ROWS_G)
                bias_table(0)
                bias_table(1)
                filled(pool, "mm", turn["mm", "ng", TT - 1])
                bias_table(2)
        for t in range(TT):
            pool.wait_ge(out_ready, t + 1)
            pool.dma_start(out[0, t * P:(t + 1) * P, :], x[:, t, :]).then_inc(out_stored, 16)
        pool.wait_ge(out_stored, TT * 16)


_NAMES = ["x", "norm_mix", "norm_ffn", "da_w_in", "da_q_norm", "da_k_norm", "da_lambda_q1", "da_lambda_k1",
          "da_lambda_q2", "da_lambda_k2", "da_subln", "da_w_out", "moe_w_group", "moe_b_group", "moe_w_router",
          "moe_b_router", "moe_w_gate", "moe_w_up", "moe_w_down", "c_2", "ctx_2", "c_ctx_2", "norm_g_2",
          "w_ada_2", "b_ada_2", "w_in_2", "w_four_2", "q_norm_g_2", "k_norm_g_2", "w_out_2"]


def _shape_constants():
    n = np.arange(SEQ)
    angle = 2 * np.pi * ((n[:, None] * n[None, :]) % SEQ) / SEQ
    dft = np.stack([np.cos(angle), np.sin(angle)]).astype(np.float32)
    m = np.arange(P)
    angle = 2 * np.pi * ((m[:, None] * m[None, :]) % P) / P
    scale = (SEQ * P) ** -0.5
    chan = np.stack([np.cos(angle) * scale, -np.sin(angle) * scale], axis=1).astype(np.float32)
    mask = np.zeros((P, 3, KC), np.float32)
    for tile in (0, 1, 3):
        q = tile * QC + QC - 1 - np.arange(P) % QC
        first = np.clip(q - QC // 2, 0, GRID - QC)[:, None]
        key = KEY_COL[tile] + np.arange(KC)[None, :]
        mask[:, MASK[tile], :] = np.where((key >= first) & (key < first + QC), 0.0, -BIG)
    return {"dft": dft, "chan": chan, "mask": mask}


def kernel(**inputs):
    import numpy as _np
    import concourse.bacc as _bacc
    from concourse import mybir as _mybir
    from concourse.bass_utils import run_bass_kernel_spmd as _run

    nc = _bacc.Bacc("TRN2", target_bir_lowering=False, num_devices=1)
    arrays, A = {}, {}
    for name in _NAMES:
        a = _np.ascontiguousarray(inputs[name])
        arrays[f"in_{name}"] = a
        A[name] = nc.dram_tensor(f"in_{name}", a.shape, _mybir.dt.from_np(a.dtype), kind="ExternalInput").ap()
    rel = _np.ascontiguousarray(inputs["rel_bias_2"])[0]
    rel_pad = _np.zeros((rel.shape[1], H2, REL_W), rel.dtype)
    rel_pad[:, :, 16:16 + rel.shape[2]] = rel.transpose(1, 0, 2)
    for name, a in {"rel_pad": rel_pad, **_shape_constants()}.items():
        arrays[f"in_{name}"] = a
        A[name] = nc.dram_tensor(f"in_{name}", a.shape, _mybir.dt.from_np(a.dtype), kind="ExternalInput").ap()
    out = nc.dram_tensor("out_0", (1, SEQ, D), F32, kind="ExternalOutput").ap()
    kernel_program(nc, A, out)
    r = _run(nc, [arrays], core_ids=[0])
    return r.results[0]["out_0"]
```

```python
from contextlib import ExitStack

import numpy as np

import concourse.bass as bass
from concourse import mybir

ALU = mybir.AluOpType
ACT = mybir.ActivationFunctionType
AX = mybir.AxisListType
F32 = mybir.dt.float32
I32 = mybir.dt.int32
U32 = mybir.dt.uint32

P = 128
SEQ, D = 512, 1024
TT = SEQ // P
KD = D // P
LAST = SEQ - P
EPS = 1e-6

HEADS, DH = 8, 64
CH = 512
QK_CHUNKS = 4
LAMBDA_INIT = 0.2
BIG = 1e30

GROUPS, PER_GROUP = 4, 4
EXPERTS = GROUPS * PER_GROUP
F = 512
FC = F // P
SPILL = 7
ROWS = (EXPERTS + SPILL) * P

CTX = 256
CT = CTX // P
GRID = 64
ROWS_G = SEQ // GRID
H2 = 8
W2 = 512
QC, KC = 16, 32
KEY_COL = [0, 8, 24, 32]
SHIFT = [16, 8, 8, 0]
MASK = [0, 1, 1, 2]
REL_W = 63
FREQ = SEQ // 2 + 1
PARTS = {"f_in": 0, "f_gate": 1, "q": 2, "k": 3, "v": 4, "na_gate": 5}

SLOTS = 6
W_IN, W_OUT, W_MOE = 0, 8, 10

ADA_CHUNKS = 6
ADA_AFTER = [9, 13, 17, 20, 22, 23]
ADA_OPS = [16, 32, 48, 64, 72, 80]


def kernel_program(nc, A, out):
    with ExitStack() as ctx:
        build(nc, ctx, A, out)


def attention_steps(s):
    todo = []
    if s < TT * HEADS:
        todo.append(("scores", s))
    if 1 <= s <= TT * HEADS:
        todo.append(("pd", s - 1))
    if 2 <= s < TT * HEADS + 2:
        todo.append(("pdT", s - 2))
    if 16 <= s < TT * HEADS + 16:
        todo.append(("w_out", s - 16))
    if 3 <= s < TT * HEADS + 3:
        todo.append(("pv", s - 3))
    for name, at in (("o_raw0", 6), ("o_raw1", 10), ("o_mean", 11), ("o_norm", 12), ("oT", 14),
                     ("x_add0", 19), ("x_add1", 23)):
        t, rest = divmod(s - at, HEADS)
        if 0 <= t < TT and rest == 0:
            todo.append((name, t))
    if s == HEADS * TT + 8:
        todo.append(("norm2", 0))
    if HEADS * TT + 11 <= s < HEADS * TT + 15:
        todo.append(("xT2", s - HEADS * TT - 11))
    return todo


ATTENTION_STEPS = HEADS * TT + 16

PROJ2 = ([("cv", t) for t in range(CT)] + [("ck", t) for t in range(CT)]
         + [(part, t) for part in ("k", "v", "q", "u", "ng", "fg") for t in range(TT)])
QK2 = [item for item in PROJ2 if item[0] in ("ck", "k", "q")]
PAIRS = TT * H2 // 2


FOURIER_AT = [0, 1, 2, 4, 5, 6, 8, 9]
OUT_AT = [11, 13, 15, 16]


def mixer_steps(s):
    todo = []
    if s < PAIRS:
        todo.append(("scores", s))
    if s in FOURIER_AT:
        todo.append(("fourier", FOURIER_AT.index(s)))
    if s in OUT_AT:
        todo.append(("out_f", OUT_AT.index(s)))
    if 2 <= s < PAIRS + 2:
        todo.append(("pv", s - 2))
    if 1 <= s <= PAIRS:
        todo.append(("pT", s - 1))
    c, late = divmod(s - 6, 4)
    if 0 <= c < TT and late == 0:
        todo.append(("oT", c))
    return todo


MIXER_STEPS = PAIRS + 4


def build(nc, ctx, A, out):
    def sb(name, shape, dt=F32):
        return ctx.enter_context(nc.sbuf_tensor(name, shape, dt))

    def sem(name):
        return ctx.enter_context(nc.semaphore(name))

    x = sb("x", [P, TT, D])
    buf_a = sb("buf_a", [P, 4096])
    buf_b = sb("buf_b", [P, 4096])
    buf_c = sb("buf_c", [P, 4096])
    buf_d = sb("buf_d", [P, 4096])
    ring = sb("ring", [P, SLOTS, 4096])
    s_buf = sb("s_buf", [P, 2, 2, 512])
    pd = sb("pd", [P, 2, 512])
    pT = sb("pT", [P, 2, 512])
    o_sb = sb("o_sb", [P, D])
    ident = sb("ident", [P, P])
    tri = sb("tri", [P, P])
    ones = sb("ones", [P, P])
    g_x = sb("g_x", [P, D])
    dist = g_x[:, 0:512]
    gain1 = sb("gain1", [P, KD])
    gain2 = sb("gain2", [P, KD])
    qk_gain = sb("qk_gain", [P, 2])
    sub_gain = sb("sub_gain", [P, 1])
    lam = sb("lam", [P, 4])
    w_rt = sb("w_rt", [P, KD, 20])
    b_rt = sb("b_rt", [P, 20])
    ssq = sb("ssq", [P, 8])
    ms = sb("ms", [P, 8])
    rstd = sb("rstd", [P, 8])
    qk_st = sb("qk_st", [P, 2, 3, 8])
    half = sb("half", [P, 8])
    den = sb("den", [P, 2, 2])
    nmx = sb("nmx", [P, 2, 2])
    ratio = sb("ratio", [P, 2, 2])
    rden = sb("rden", [P, 2, 8])
    o_st = sb("o_st", [P, 3, 8])
    logit = sb("logit", [P, TT, 20])
    g_pick = sb("g_pick", [P, TT, GROUPS])
    g_exp = sb("g_exp", [P, TT, GROUPS])
    in_group = sb("in_group", [P, TT, PER_GROUP])
    e_pick = sb("e_pick", [P, 2, TT, PER_GROUP])
    r_a = sb("r_a", [P, TT, EXPERTS])
    r_b = sb("r_b", [P, TT, 4])
    r_c = sb("r_c", [P, TT, 4])
    r_m = sb("r_m", [P, 6, TT])
    picks = sb("picks", [P, 2, TT, EXPERTS])
    sel_pad = sb("sel_pad", [P, 2 * TT + 1, EXPERTS])
    place = sb("place", [P, TT + 1, EXPERTS])
    full_tiles = sb("full_tiles", [P, 4, EXPERTS])
    weight = sb("weight", [P, 2, TT])
    row_f = sb("row_f", [P, 2, TT])
    iota16 = sb("iota16", [P, 16])
    prio = sb("prio", [P, 4])
    row_i = sb("row_i", [P, 2, TT], I32)
    tok_i = sb("tok_i", [P, TT], I32)
    spill_i = sb("spill_i", [P, SPILL + 1], I32)
    place_f = sb("place_f", [P, 2, TT])
    tok_f = sb("tok_f", [P, TT])
    idx = sb("idx", [P, EXPERTS + 1], I32)

    norm_g = sb("norm_g", [P, KD])
    mod_g = sb("mod_g", [P, 2, KD])
    mod_sh = sb("mod_sh", [P, 2, KD])
    qk_gain2 = sb("qk_gain2", [P, 2])
    b_ada = sb("b_ada", [P, 3 * KD])
    gate_col = sb("gate_col", [P, KD])
    cond = sb("cond", [P, KD, 2])
    mask = sb("mask", [P, 3, KC])
    chan = sb("chan", [P, 2, P])
    cssq = sb("cssq", [P, 3, CT])

    ada_acc = s_buf[:, 0]
    zeros = s_buf[:, 1, 1, P:2 * P]
    sel = sel_pad[:, TT:2 * TT, :]
    logit_T = pT[0:20, 0, :]
    slots_iota = s_buf[:, 1, 0, 0:P]
    slot_pick = pd[:, :, :].rearrange("p a (b n) -> p (a b) n", n=P)
    lam_in = s_buf[:, 1, 0, 0:4 * DH].rearrange("p (n d) -> p n d", n=4)
    lam_pr = s_buf[:, 1, 1, 0:2 * DH].rearrange("p (n d) -> p n d", n=2)
    xs = buf_a[:, :].rearrange("p (t d) -> p t d", t=TT)
    v = xs
    hT = buf_b[:, :].rearrange("p (k n) -> p k n", k=KD)
    oT = hT
    qT = buf_c[:, :].rearrange("p (h n) -> p h n", h=HEADS)
    kT = buf_d[:, :].rearrange("p (h n) -> p h n", h=HEADS)
    xs2 = buf_c[:, :].rearrange("p (t d) -> p t d", t=TT)
    xT2 = buf_d[:, :].rearrange("p (k n) -> p k n", k=KD)
    xg = buf_a[:, 0:2048].rearrange("p (b d) -> p b d", b=2)
    xgT = buf_a[:, 2048:4096].rearrange("p (b k n) -> p b k n", b=2, k=KD)
    sg = buf_b[:, 0:1024].rearrange("p (b f) -> p b f", b=2)
    hidT = buf_b[:, 1024:2048].rearrange("p (b f) -> p b f", b=2)
    y_sb = buf_b[:, 2048:4096].rearrange("p (b d) -> p b d", b=2)
    yg = buf_a[:, :].rearrange("p (b d) -> p b d", b=4)
    gate_diag = o_sb[:].rearrange("p (k n) -> p k n", k=KD)
    q2T = buf_c[:, 0:2048].rearrange("p (g n) -> p g n", g=4)
    k2T = buf_c[:, 2048:4096].rearrange("p (g n) -> p g n", g=4)
    cx = buf_d[:, 0:2048].rearrange("p (t d) -> p t d", t=CT)
    cxT = buf_d[:, 2048:4096].rearrange("p (k n) -> p k n", k=KD)
    u = buf_d[:, 0:2048].rearrange("p (t n) -> p t n", t=TT)
    yT = u
    fgT = buf_d[:, 2048:4096].rearrange("p (f n) -> p f n", f=4)
    xs3 = xs
    x3T = hT
    v_win = buf_a[:, :].rearrange("p (i n) -> p i n", i=8)
    mixT = hT
    ckT = ring[:, 1, 0:1024].rearrange("p (g n) -> p g n", g=4)
    cv = ring[:, 1, 1024:2048].rearrange("p (t n) -> p t n", t=CT)
    ngT = ring[:, 1, 2048:4096].rearrange("p (f n) -> p f n", f=4)
    rel = ring[:, 2, 0:8 * 8 * 48].rearrange("p (r h n) -> p r h n", r=8, h=8)
    bias = [ring[:, 3, 0:2048], ring[:, 3, 2048:4096], ring[:, 5, 2048:4096]]
    seqT = ring[:, 2, :].rearrange("p (g a n) -> p g a n", g=4, a=2)

    xn_d = nc.dram_tensor("xn_d", (SEQ, D), F32).ap()
    ids_d = nc.dram_tensor("ids_d", (ROWS, 1), I32).ap()
    y_d = nc.dram_tensor("y_d", (ROWS, D), F32).ap()
    v_d = nc.dram_tensor("v_d", (SEQ, W2), F32).ap()

    psum = ctx.enter_context(nc.psum_tensor("psum", [P, 8, 512], F32))
    SC = [psum[:, 0:2, :], psum[:, 2:4, :]]
    TP = [psum[:, 4, :], psum[:, 5, :]]
    MM = [psum[:, 6, :], psum[:, 7, :]]

    full = {c: [sem(f"{c}_full{i}") for i in range(2)] for c in ("sc", "tp", "mm")}
    free = {c: [sem(f"{c}_free{i}") for i in range(2)] for c in ("sc", "tp", "mm")}
    bufs = {"sc": SC, "tp": TP, "mm": MM}

    turn = {}
    count = {"sc": 0, "tp": 0, "mm": 0}

    def book(c, *key):
        turn[(c, *key)] = count[c]
        count[c] += 1

    for b in range(2):
        book("tp", "hT", b)
    for i in range(6 * TT):
        book("mm", "proj", i)
    for i in range(6 * TT):
        if i < TT - 1:
            book("tp", "hT", 2 * i + 2)
            book("tp", "hT", 2 * i + 3)
        if 1 <= i <= QK_CHUNKS * TT:
            book("tp", "qkT", i - 1)
        if i in ADA_AFTER:
            book("tp", "ada", ADA_AFTER.index(i))
    for s in range(ATTENTION_STEPS):
        for name, m in attention_steps(s):
            if name == "scores":
                book("sc", "scores", m)
            elif name == "pdT":
                book("tp", "pdT", m)
            elif name == "pv" and m % 4 == 0:
                book("mm", "o", m // 4)
            elif name == "oT":
                book("tp", "oT", 2 * m)
                book("tp", "oT", 2 * m + 1)
            elif name == "w_out" and m % 4 == 0:
                book("mm", "w_out", m // 4)
            elif name == "xT2":
                book("tp", "xT2", 2 * m)
                book("tp", "xT2", 2 * m + 1)
    for b in range(2):
        book("tp", "xT2_last", b)
    book("mm", "router_T")
    book("mm", "router")
    for c in range(2):
        book("mm", "g_x", c)
    book("mm", "places")
    book("mm", "ids")
    tp0, sc0 = count["tp"], count["sc"]

    def turn_x(e):
        return tp0 if e == 0 else tp0 + 3 * e - 1

    def turn_hid(e):
        return tp0 + 3 * e + (4 if e < EXPERTS - 1 else 2 + KD // 2)

    def turn_gu(e):
        return sc0 if e == 0 else sc0 + 2 * e - 1

    def turn_dn(e):
        return sc0 + 2 * e + (2 if e < EXPERTS - 1 else 1)

    count["tp"] += 3 * EXPERTS - 1
    count["sc"] += 2 * EXPERTS

    for k in range(0, KD, 2):
        book("tp", "cxT", k)
    count["tp"] += 1
    for i, item in enumerate(PROJ2):
        if item == ("k", 0):
            for k in range(KD):
                book("tp", "x3T", k)
        book("mm", *item)
        if i >= 1 and PROJ2[i - 1] in QK2:
            book("tp", "qkT2", QK2.index(PROJ2[i - 1]))
    for s in range(MIXER_STEPS):
        for name, m in mixer_steps(s):
            if name == "scores":
                book("sc", "scores2", m)
            elif name == "fourier":
                book("sc", "fourier", m)
            elif name == "out_f":
                book("sc", "out_f", m)
            elif name == "pT":
                book("tp", "pT2", 2 * m)
                book("tp", "pT2", 2 * m + 1)
            elif name == "pv" and m % 4 == 0:
                book("mm", "o2", m // 4)
            elif name == "oT":
                book("tp", "oT2", m)
    for t in range(TT):
        book("sc", "out", t)

    slot_of, loads = {}, [9, 9, 10, 10, 9, 9]
    for name, i in (("k", 4), ("v", 5), ("q", 0), ("f_in", 4), ("na_gate", 5), ("f_gate", 0),
                    ("dft", 4), ("w_four", 5), ("w_out0", 0), ("w_out1", 4)):
        loads[i] += 1
        slot_of[name] = (i, 16 * loads[i])

    def buf(c, n):
        return bufs[c][n % 2]

    def claim(eng, c, n, more=0):
        if n >= 2:
            eng.wait_ge(free[c][n % 2], more + n // 2)

    def filled(eng, c, n, more=0):
        eng.wait_ge(full[c][n % 2], more + (n // 2 + 1))

    def drained(eng, c, n, more=0):
        eng.wait_ge(free[c][n % 2], more + (n // 2 + 1))

    def fill(ins, c, n):
        ins.then_inc(full[c][n % 2], 1)

    def drain(ins, c, n):
        ins.then_inc(free[c][n % 2], 1)

    x_loaded = [sem(f"x_loaded{t}") for t in range(TT)]
    gain_loaded = sem("gain_loaded")
    early_loaded, late_loaded = sem("early_loaded"), sem("late_loaded")
    w_landed = [sem(f"w_landed{i}") for i in range(SLOTS)]
    pool_consts = sem("pool_consts")
    dve_done, act_done, pool_done = sem("dve_done"), sem("act_done"), sem("pool_done")
    ssq_ready = sem("ssq_ready")
    ms_ready = sem("ms_ready")
    rstd_ready = sem("rstd_ready")
    xs_ready = sem("xs_ready")
    gains_scaled = sem("gains_scaled")
    sq_ready = sem("sq_ready")
    qk_ms_ready = sem("qk_ms_ready")
    qk_rstd_ready = sem("qk_rstd_ready")
    lam_sum, lam_exp = sem("lam_sum"), sem("lam_exp")
    nmx_ready = sem("nmx_ready")
    exp_ready = sem("exp_ready")
    pd_ready = sem("pd_ready")
    o_sq_ready = sem("o_sq_ready")
    o_ms_ready, o_rstd_ready = sem("o_ms_ready"), sem("o_rstd_ready")
    o_norm_ready = sem("o_norm_ready")
    xs2_ready = sem("xs2_ready")
    w_rt_ready = sem("w_rt_ready")
    ge_in, ge_out = sem("ge_in"), sem("ge_out")
    sel_ready = sem("sel_ready")
    rows_ready = sem("rows_ready")
    y_zeroed = sem("y_zeroed")
    xn_stored, ids_zeroed, ids_stored = sem("xn_stored"), sem("ids_zeroed"), sem("ids_stored")
    iota_ready = sem("iota_ready")
    pick_ready = sem("pick_ready")
    xg_ready = [sem(f"xg_ready{b}") for b in range(2)]
    sg_ready = sem("sg_ready")
    y_stored = [sem(f"y_stored{b}") for b in range(2)]
    yg_ready = [sem(f"yg_ready{i}") for i in range(8)]
    x2_ready = sem("x2_ready")
    out_stored = sem("out_stored")
    spill_ready = sem("spill_ready")
    spill_pe, spill_dve, spill_act = sem("spill_pe"), sem("spill_dve"), sem("spill_act")
    spill_w, spill_idx, spill_x, spill_y = sem("spill_w"), sem("spill_idx"), sem("spill_x"), sem("spill_y")
    second_loaded = sem("second_loaded")
    ctx_loaded = [sem(f"ctx_loaded{t}") for t in range(CT)]
    spills_done = sem("spills_done")
    ada_landed = [sem(f"ada_landed{b}") for b in range(2)]
    ada_step = sem("ada_step")
    gate_ready = sem("gate_ready")
    cond_ready = sem("cond_ready")
    mod_ready = sem("mod_ready")
    c_ssq_ready, c_ms_ready, c_rstd_ready = sem("c_ssq_ready"), sem("c_ms_ready"), sem("c_rstd_ready")
    cx_ready = sem("cx_ready")
    xs3_ready = sem("xs3_ready")
    v_stored = [sem(f"v_stored{b}") for b in range(2)]
    v_win_loaded = sem("v_win_loaded")
    rel_loaded = sem("rel_loaded")
    bias_ready = sem("bias_ready")
    neg_max = sem("neg_max")
    out_f_added = sem("out_f_added")
    out_ready = sem("out_ready")

    def spill_count(eng):
        eng.wait_ge(spill_ready, 1)
        return eng.value_load(spill_i[0:1, SPILL:SPILL + 1], min_val=0, max_val=SPILL)

    block = ctx.enter_context(nc.Block())

    @block.sync
    def _(sp):
        def load(i, src, k=KD):
            dst = ring[:, i % SLOTS, :].rearrange("p (k n) -> p k n", k=k)
            sp.dma_start(dst, src).then_inc(w_landed[i % SLOTS], 16)

        w_in = A["da_w_in"][0].rearrange("(k p) n -> p k n", p=P)
        for t in range(TT):
            sp.dma_start(x[:, t, :], A["x"][0, t * P:(t + 1) * P, :]).then_inc(x_loaded[t], 16)
            if t == 0:
                load(W_IN, w_in[:, :, 0:CH])
        for c in range(1, 6):
            load(W_IN + c, w_in[:, :, c * CH:(c + 1) * CH])
        w_out = A["da_w_out"][0].rearrange("(k p) n -> p k n", p=P)
        w_ada = A["w_ada_2"][0].rearrange("(k p) n -> p k n", p=P)

        def load_ada(c):
            if c >= 2:
                sp.wait_ge(ada_step, ADA_OPS[c - 2])
            else:
                filled(sp, "mm", turn["mm", "proj", (c + 1) * TT - 1])
            sp.dma_start(ring[:, c % 2, :].rearrange("p (k n) -> p k n", k=KD),
                         w_ada[:, :, c * 512:(c + 1) * 512]).then_inc(ada_landed[c % 2], 16)

        load_ada(0)
        load_ada(1)
        load_ada(2)
        for c in range(2):
            filled(sp, "mm", turn["mm", "proj", (c + 3) * TT - 1])
            load(W_OUT + c, w_out[:, :, c * CH:(c + 1) * CH])
            load_ada(3 + c)

        def load_expert(e, first):
            for m, (name, k) in enumerate((("moe_w_gate", KD), ("moe_w_up", KD), ("moe_w_down", FC))):
                yield m
                src = A[name][0, e] if isinstance(e, int) else A[name][0, bass.ds(e, 1)].rearrange("a r n -> (a r) n")
                load(first + m, src.rearrange("(k p) n -> p k n", p=P), k)

        for m in load_expert(0, W_MOE):
            if m == 0:
                filled(sp, "mm", turn["mm", "proj", 5 * TT - 1])
            elif m == 1:
                load_ada(5)
                filled(sp, "mm", turn["mm", "proj", 6 * TT - 1])
            else:
                sp.wait_ge(ada_step, ADA_OPS[4])
        for m in load_expert(1, W_MOE + 3):
            if m == 0:
                sp.wait_ge(ada_step, ADA_OPS[5])
            else:
                filled(sp, "mm", turn["mm", "w_out", 2 * TT - 3 + m])
        for m in load_expert(2, W_MOE + 6):
            filled(sp, "sc", turn_gu(0) if m < 2 else turn_dn(0))
        with sp.Fori(0, (EXPERTS - 4) // 2) as j:
            for b in (3, 4):
                for m in load_expert(2 * j + b, W_MOE + 3 * b):
                    filled(sp, "sc", turn_gu(b - 2) if m < 2 else turn_dn(b - 2), 2 * j)
        for m in load_expert(EXPERTS - 1, W_MOE + 3 * (EXPERTS - 1)):
            filled(sp, "sc", turn_gu(EXPERTS - 3) if m < 2 else turn_dn(EXPERTS - 3))

        spills = spill_count(sp)
        with sp.If(spills > 0):
            with sp.Fori(0, SPILL) as o:
                with sp.If(spills > o):
                    e = sp.value_load(spill_i[0:1, bass.ds(o, 1)], min_val=0, max_val=EXPERTS - 1)
                    for m, (name, k, dst) in enumerate((("moe_w_gate", KD, ring[:, 1, :]),
                                                        ("moe_w_up", KD, ring[:, 2, :]),
                                                        ("moe_w_down", FC, ring[:, 1, :]))):
                        if m == 0:
                            sp.wait_ge(spill_pe, 4 * o + 1)
                        if m == 2:
                            sp.wait_ge(spill_pe, 4 * o + 3)
                        src = A[name][0, bass.ds(e, 1)].rearrange("a r n -> (a r) n")
                        sp.dma_start(dst.rearrange("p (k n) -> p k n", k=k),
                                     src.rearrange("(k p) n -> p k n", p=P)).then_inc(spill_w, 16)

        def load2(name, src, k=KD, n=512):
            i, _ = slot_of[name]
            sp.dma_start(ring[:, i, 0:k * n].rearrange("p (k n) -> p k n", k=k), src).then_inc(w_landed[i], 16)

        w_in2 = A["w_in_2"][0].rearrange("(k p) n -> p k n", p=P)
        for c, name in enumerate(("k", "v", "q", "f_in", "na_gate", "f_gate")):
            if c < 3:
                filled(sp, "sc", turn_gu(EXPERTS - 2) if c < 2 else turn_dn(EXPERTS - 2))
            else:
                filled(sp, "mm", turn["mm", ("k", "v", "q")[c - 3], TT - 1])
            load2(name, w_in2[:, :, PARTS[name] * W2:(PARTS[name] + 1) * W2])
            if name == "q":
                filled(sp, "sc", turn_gu(EXPERTS - 1))
                rel_in = A["rel_pad"]
                for r in range(ROWS_G):
                    sp.dma_start(rel[r * QC:(r + 1) * QC].rearrange("p r h n -> p (r h) n"),
                                 bass.AP(tensor=rel_in.tensor, offset=(ROWS_G - 1 - r) * H2 * REL_W,
                                         ap=[[1, QC], [REL_W, ROWS_G * H2], [1, 48]])).then_inc(rel_loaded, 16)
        filled(sp, "mm", turn["mm", "u", TT - 1])
        load2("dft", A["dft"].rearrange("a (k p) n -> p (a k) n", p=P), n=FREQ)
        filled(sp, "mm", turn["mm", "ng", TT - 1])
        load2("w_four", A["w_four_2"][0].rearrange("(k p) n -> p k n", p=P), 4)
        for t in range(2):
            sp.wait_ge(v_stored[t], 32)
        v_rows = v_d.rearrange("(r w) n -> r w n", w=GRID)
        for c in range(TT):
            for half_c in range(2):
                for r in range(4):
                    sp.dma_start(v_win[r * KC:(r + 1) * KC, 2 * c + half_c, :],
                                 v_rows[4 * half_c + r, KEY_COL[c]:KEY_COL[c] + KC, :]).then_inc(v_win_loaded, 16)
        w_out2 = A["w_out_2"][0].rearrange("(k p) n -> p k n", p=P)
        filled(sp, "mm", turn["mm", "fg", TT - 1])
        load2("w_out0", w_out2[:, :, 0:512])
        filled(sp, "sc", turn["sc", "fourier", 3])
        load2("w_out1", w_out2[:, :, 512:1024])
        for t in range(TT):
            sp.wait_ge(out_ready, t + 1)
            sp.dma_start(out[0, t * P:(t + 1) * P, :], x[:, t, :]).then_inc(out_stored, 16)
        sp.wait_ge(out_stored, TT * 16)

    @block.tensor
    def _(pe):
        mm, transpose = nc.tensor.matmul, nc.tensor.transpose

        def landed(i, more=0):
            others = 1 if i >= SLOTS and i % SLOTS < 2 else 0
            pe.wait_ge(w_landed[i % SLOTS], more * 16 + 16 * (i // SLOTS + 1 - others))

        def slot(i, k=KD):
            return ring[:, i % SLOTS, :].rearrange("p (k n) -> p k n", k=k)

        def transposes(n, blocks):
            for g, block_in in enumerate(blocks):
                last = transpose(buf("tp", n)[:, g * P:(g + 1) * P], block_in, ident[:])
            fill(last, "tp", n)

        def h_transposes(t):
            pe.wait_ge(xs_ready, t + 1)
            for b in range(2):
                n = turn["tp", "hT", 2 * t + b]
                claim(pe, "tp", n)
                transposes(n, [xs[:, t, k * P:(k + 1) * P] for k in range(4 * b, 4 * b + 4)])

        pe.wait_ge(pool_consts, 1)
        h_transposes(0)

        for i in range(6 * TT):
            c, t = divmod(i, TT)
            n = turn["mm", "proj", i]
            if t == 0:
                landed(W_IN + c)
            claim(pe, "mm", n)
            for k in range(KD):
                if i < TT and k % 4 == 0:
                    drained(pe, "tp", turn["tp", "hT", 2 * i + k // 4])
                last = mm(buf("mm", n), hT[:, k, t * P:(t + 1) * P], slot(W_IN + c)[:, k, :],
                          start=(k == 0), stop=(k == KD - 1))
                if i < TT - 1 and k == 5:
                    h_transposes(t + 1)
            fill(last, "mm", n)
            if 1 <= i <= QK_CHUNKS * TT:
                drained(pe, "mm", turn["mm", "proj", i - 1])
                n = turn["tp", "qkT", i - 1]
                claim(pe, "tp", n)
                transposes(n, [pd[:, (i - 1) % 2, g * P:(g + 1) * P] for g in range(4)])
            if i in ADA_AFTER:
                c = ADA_AFTER.index(i)
                n = turn["tp", "ada", c]
                claim(pe, "tp", n)
                pe.wait_ge(ada_step, ADA_OPS[c])
                for g in range(4):
                    for b in range(2):
                        col = g if c >= 4 else 4 * b + g
                        last = mm(buf("tp", n)[:, col:col + 1], ada_acc[:, b, g * P:(g + 1) * P], ones[:, 0:1],
                                  start=(c < 4 or b == 0), stop=(c < 4 or b == 1))
                fill(last, "tp", n)

        for s in range(ATTENTION_STEPS):
            for name, m in attention_steps(s):
                t, h = divmod(m, HEADS)
                if name == "scores":
                    n = turn["sc", "scores", m]
                    if m == 0:
                        drained(pe, "tp", turn["tp", "qkT", QK_CHUNKS * TT - 2])
                        drained(pe, "tp", turn["tp", "qkT", QK_CHUNKS * TT - 1])
                    claim(pe, "sc", n)
                    for c in range(2):
                        rows = slice(c * DH, (c + 1) * DH)
                        last = mm(buf("sc", n)[:, c, 0:(t + 1) * P], qT[rows, h, t * P:(t + 1) * P],
                                  kT[rows, h, 0:(t + 1) * P], start=True, stop=True)
                    fill(last, "sc", n)
                elif name == "pdT":
                    n = turn["tp", "pdT", m]
                    pe.wait_ge(pd_ready, m + 1)
                    claim(pe, "tp", n)
                    transposes(n, [pd[:, m % 2, g * P:(g + 1) * P] for g in range(t + 1)])
                elif name == "pv":
                    n = turn["mm", "o", m // 4]
                    if m == 0:
                        drained(pe, "mm", turn["mm", "proj", 6 * TT - 2])
                        drained(pe, "mm", turn["mm", "proj", 6 * TT - 1])
                    if m % 4 == 0:
                        claim(pe, "mm", n)
                    drained(pe, "tp", turn["tp", "pdT", m])
                    for g in range(t + 1):
                        last = mm(buf("mm", n)[:, (h % 4) * P:(h % 4 + 1) * P], pT[:, m % 2, g * P:(g + 1) * P],
                                  v[:, g, h * P:(h + 1) * P], start=(g == 0), stop=(g == t))
                    if m % 4 == 3:
                        fill(last, "mm", n)
                elif name == "oT":
                    t = m
                    pe.wait_ge(o_norm_ready, t + 1)
                    for b in range(2):
                        n = turn["tp", "oT", 2 * t + b]
                        claim(pe, "tp", n)
                        transposes(n, [o_sb[:, g * P:(g + 1) * P] for g in range(4 * b, 4 * b + 4)])
                elif name == "w_out":
                    t, c, piece = m // 8, m // 4 % 2, m % 4
                    n = turn["mm", "w_out", m // 4]
                    if piece == 0:
                        claim(pe, "mm", n)
                    if m == 0 or m == 4:
                        landed(W_OUT + c)
                    if c == 0 and piece == 0:
                        drained(pe, "tp", turn["tp", "oT", 2 * t])
                        drained(pe, "tp", turn["tp", "oT", 2 * t + 1])
                    for k in (2 * piece, 2 * piece + 1):
                        last = mm(buf("mm", n), oT[:, k, t * P:(t + 1) * P], slot(W_OUT + c)[:, k, :],
                                  start=(k == 0), stop=(k == KD - 1))
                    if piece == 3:
                        fill(last, "mm", n)
                elif name == "xT2":
                    pe.wait_ge(xs2_ready, TT - 1)
                    for k in (2 * m, 2 * m + 1):
                        n = turn["tp", "xT2", k]
                        claim(pe, "tp", n)
                        transposes(n, [xs2[:, t, k * P:(k + 1) * P] for t in range(TT - 1)])

        pe.wait_ge(w_rt_ready, 1)
        n_r = turn["mm", "router_T"]
        claim(pe, "mm", n_r)
        for k in range(KD):
            drained(pe, "tp", turn["tp", "xT2", k])
            mm(buf("mm", n_r)[0:20, 0:LAST], w_rt[:, k, :], xT2[:, k, 0:LAST], start=(k == 0), stop=(k == KD - 1))
        pe.wait_ge(xs2_ready, TT)
        for b in range(2):
            n = turn["tp", "xT2_last", b]
            claim(pe, "tp", n)
            transposes(n, [xs2[:, TT - 1, k * P:(k + 1) * P] for k in range(4 * b, 4 * b + 4)])
        for k in range(KD):
            drained(pe, "tp", turn["tp", "xT2_last", k // 4])
            last = mm(buf("mm", n_r)[0:20, LAST:SEQ], w_rt[:, k, :], xT2[:, k, LAST:SEQ], start=(k == 0), stop=(k == KD - 1))
        fill(last, "mm", n_r)
        n = turn["mm", "router"]
        claim(pe, "mm", n)
        drained(pe, "mm", n_r)
        for t in range(TT):
            last = transpose(buf("mm", n)[:, t * 20:(t + 1) * 20], logit_T[:, t * P:(t + 1) * P], ident[0:20, 0:20])
        fill(last, "mm", n)
        pe.wait_ge(gate_ready, 1)
        for c in range(2):
            n = turn["mm", "g_x", c]
            claim(pe, "mm", n)
            fill(mm(buf("mm", n), ones[:], o_sb[:, c * 512:(c + 1) * 512], start=True, stop=True), "mm", n)
        n = turn["mm", "places"]
        claim(pe, "mm", n)
        pe.wait_ge(sel_ready, 1)
        pe.wait_ge(pool_consts, 3)
        for i in range(TT + 1):
            last = mm(buf("mm", n)[:, 0:(TT + 1) * 16], tri[:] if i == 0 else ones[:],
                      sel_pad[:, TT - i:2 * TT + 1 - i, :], start=(i == 0), stop=(i == TT))
        fill(last, "mm", n)
        n = turn["mm", "ids"]
        claim(pe, "mm", n)
        for i in range(2 * TT):
            pe.wait_ge(pick_ready, i + 1)
            last = mm(buf("mm", n)[:, 0:EXPERTS], slot_pick[:, i, :], picks[:, i // TT, i % TT, :],
                      start=(i == 0), stop=(i == 2 * TT - 1))
        fill(last, "mm", n)

        def x_transposes(b, n, gathered, more=0):
            pe.wait_ge(xg_ready[b], gathered)
            for half_row in range(2):
                claim(pe, "tp", n + half_row, more)
                transposes(n + half_row, [xg[:, b, g * P:(g + 1) * P] for g in range(4 * half_row, 4 * half_row + 4)])

        def gate_up(b, n, n_x, i, more_sc=0, more_x=0, more_w=0):
            claim(pe, "sc", n, more_sc)
            drained(pe, "tp", n_x, more_x)
            drained(pe, "tp", n_x + 1, more_x)
            for m in range(2):
                landed(i + m, more_w)
                for k in range(KD):
                    last = mm(buf("sc", n)[:, m, :], xgT[:, b, k, :], slot(i + m)[:, k, :],
                              start=(k == 0), stop=(k == KD - 1))
            fill(last, "sc", n)

        def hid_transposes(b, n, n_gu, more=0, more_gu=0):
            drained(pe, "sc", n_gu, more_gu)
            claim(pe, "tp", n, more)
            transposes(n, [sg[:, b, g * P:(g + 1) * P] for g in range(FC)])

        def down(b, n, n_hid, i, more_sc=0, more_hid=0, more_w=0):
            claim(pe, "sc", n, more_sc)
            drained(pe, "tp", n_hid, more_hid)
            landed(i, more_w)
            for m in range(2):
                for f in range(FC):
                    last = mm(buf("sc", n)[:, m, :], hidT[:, b, f * P:(f + 1) * P],
                              slot(i, FC)[:, f, m * CH:(m + 1) * CH], start=(f == 0), stop=(f == FC - 1))
            fill(last, "sc", n)

        x_transposes(0, turn_x(0), 16)
        gate_up(0, turn_gu(0), turn_x(0), W_MOE)
        x_transposes(1, turn_x(1), 16)
        hid_transposes(0, turn_hid(0), turn_gu(0))
        with pe.Fori(0, EXPERTS // 2 - 1) as j:
            for e in (1, 2):
                gate_up(e % 2, turn_gu(e), turn_x(e), W_MOE + 3 * e, 2 * j, 3 * j, j)
                x_transposes((e + 1) % 2, turn_x(e + 1), 16 * j + 16 * ((e + 1) // 2 + 1), 3 * j)
                down((e - 1) % 2, turn_dn(e - 1), turn_hid(e - 1), W_MOE + 3 * (e - 1) + 2, 2 * j, 3 * j, j)
                hid_transposes(e % 2, turn_hid(e), turn_gu(e), 3 * j, 2 * j)
        e = EXPERTS - 1
        gate_up(1, turn_gu(e), turn_x(e), W_MOE + 3 * e)
        pe.wait_ge(cx_ready, CT)
        for k in range(0, KD, 2):
            n = turn["tp", "cxT", k]
            claim(pe, "tp", n)
            transposes(n, [cx[:, t, kk * P:(kk + 1) * P] for kk in (k, k + 1) for t in range(CT)])
        down(0, turn_dn(e - 1), turn_hid(e - 1), W_MOE + 3 * (e - 1) + 2)
        hid_transposes(1, turn_hid(e), turn_gu(e))
        down(1, turn_dn(e), turn_hid(e), W_MOE + 3 * e + 2)

        spills = spill_count(pe)
        with pe.If(spills > 0):
            drained(pe, "tp", turn["tp", "cxT", KD - 2])
            drained(pe, "tp", turn_hid(EXPERTS - 1))
            for n in (turn_dn(EXPERTS - 2), turn_dn(EXPERTS - 1)):
                drained(pe, "sc", n)
            pe.sem_inc(spill_pe, 1)
            with pe.Fori(0, SPILL) as o:
                with pe.If(spills > o):
                    pe.wait_ge(spill_act, 3 * o + 1)
                    pe.wait_ge(spill_x, 16 * o + 16)
                    for g in range(KD):
                        last = transpose(TP[g // 4][:, g % 4 * P:(g % 4 + 1) * P], xg[:, 0, g * P:(g + 1) * P], ident[:])
                    last.then_inc(spill_pe, 1)
                    pe.wait_ge(spill_dve, 2 * o + 1)
                    pe.wait_ge(spill_w, 48 * o + 32)
                    for m, w in enumerate((ring[:, 1, :], ring[:, 2, :])):
                        for k in range(KD):
                            last = mm(SC[0][:, m, :], xgT[:, 0, k, :], w[:, k * 512:(k + 1) * 512],
                                      start=(k == 0), stop=(k == KD - 1))
                    last.then_inc(spill_pe, 1)
                    pe.wait_ge(spill_dve, 2 * o + 2)
                    for g in range(FC):
                        last = transpose(TP[0][:, g * P:(g + 1) * P], sg[:, 0, g * P:(g + 1) * P], ident[:])
                    last.then_inc(spill_pe, 1)
                    pe.wait_ge(spill_act, 3 * o + 3)
                    pe.wait_ge(spill_w, 48 * o + 48)
                    for m in range(2):
                        for f in range(FC):
                            last = mm(SC[1][:, m, :], hidT[:, 0, f * P:(f + 1) * P],
                                      ring[:, 1, f * D + m * CH:f * D + (m + 1) * CH], start=(f == 0), stop=(f == FC - 1))
                    last.then_inc(spill_pe, 1)
            pe.wait_ge(spills_done, 1)

        def chunk2(name, k=KD, n=512):
            i, landings = slot_of[name]
            pe.wait_ge(w_landed[i], landings)
            return ring[:, i, 0:k * n].rearrange("p (k n) -> p k n", k=k)

        drained(pe, "tp", turn["tp", "cxT", KD - 4])
        drained(pe, "tp", turn["tp", "cxT", KD - 2])
        source = {"ck": "k", "cv": "v", "k": "k", "v": "v", "q": "q", "u": "f_in", "ng": "na_gate", "fg": "f_gate"}
        for i, (what, t) in enumerate(PROJ2):
            if (what, t) == ("k", 0):
                pe.wait_ge(xs3_ready, TT)
                for k in range(KD):
                    n = turn["tp", "x3T", k]
                    claim(pe, "tp", n)
                    transposes(n, [xs3[:, tt, k * P:(k + 1) * P] for tt in range(TT)])
                drained(pe, "tp", turn["tp", "x3T", KD - 2])
                drained(pe, "tp", turn["tp", "x3T", KD - 1])
            n = turn["mm", what, t]
            claim(pe, "mm", n)
            w = chunk2(source[what])
            for k in range(KD):
                tile = slice(t * P, (t + 1) * P)
                if what in ("ck", "cv"):
                    left, right = cxT[:, k, tile], w[:, k, :]
                elif what in ("ng", "fg"):
                    left, right = w[:, k, tile], x3T[:, k, :]
                else:
                    left, right = x3T[:, k, tile], w[:, k, :]
                last = mm(buf("mm", n), left, right, start=(k == 0), stop=(k == KD - 1))
            fill(last, "mm", n)
            if i >= 1 and PROJ2[i - 1] in QK2:
                j = QK2.index(PROJ2[i - 1])
                drained(pe, "mm", turn["mm", *QK2[j]])
                n = turn["tp", "qkT2", j]
                claim(pe, "tp", n)
                transposes(n, [pd[:, j % 2, g * P:(g + 1) * P] for g in range(4)])

        def out_products(n, t, first):
            claim(pe, "sc", n)
            for a in range(2):
                w = chunk2(f"w_out{a}")
                for k in range(first, first + 4):
                    last = mm(buf("sc", n)[:, a, :], mixT[:, k, t * P:(t + 1) * P], w[:, k, :],
                              start=(k == first), stop=(k == first + 3))
            fill(last, "sc", n)

        drained(pe, "tp", turn["tp", "qkT2", len(QK2) - 2])
        drained(pe, "tp", turn["tp", "qkT2", len(QK2) - 1])
        for s in range(MIXER_STEPS):
            for name, m in mixer_steps(s):
                c, g = divmod(m, 4)
                if name == "scores":
                    n = turn["sc", "scores2", m]
                    claim(pe, "sc", n)
                    for hh in range(2):
                        rows = slice(hh * DH, (hh + 1) * DH)
                        q = q2T[rows, g, c * P:(c + 1) * P]
                        k = k2T[rows, g, :].rearrange("p (r w) -> p r w", w=GRID)[:, :, KEY_COL[c]:KEY_COL[c] + KC]
                        mm(buf("sc", n)[:, hh, 0:256], q, k, start=True, stop=True)
                        last = mm(buf("sc", n)[:, hh, 256:512], q, ckT[rows, g, :], start=True, stop=True)
                    fill(last, "sc", n)
                elif name == "fourier":
                    n = turn["sc", "fourier", m]
                    claim(pe, "sc", n)
                    if m < 4:
                        w = chunk2("dft", n=FREQ)
                        if m == 0:
                            drained(pe, "mm", turn["mm", "u", TT - 2])
                            drained(pe, "mm", turn["mm", "u", TT - 1])
                        for a in range(2):
                            for t in range(TT):
                                last = mm(buf("sc", n)[:, a, 0:FREQ], u[:, t, m * P:(m + 1) * P], w[:, 4 * a + t, :],
                                          start=(t == 0), stop=(t == TT - 1))
                    elif m < 6:
                        if m == 4:
                            drained(pe, "sc", turn["sc", "fourier", 2])
                            drained(pe, "sc", turn["sc", "fourier", 3])
                        for b in range(2):
                            for a in range(2):
                                last = mm(buf("sc", n)[:, b, :], chan[:, a, :], seqT[:, 2 * (m - 4) + b, a, :],
                                          start=(a == 0), stop=(a == 1))
                    else:
                        w = chunk2("w_four", 4)
                        if m == 6:
                            drained(pe, "sc", turn["sc", "fourier", 4])
                            drained(pe, "sc", turn["sc", "fourier", 5])
                        for b in range(2):
                            f = 2 * (m - 6) + b
                            for k in range(4):
                                last = mm(buf("sc", n)[:, b, :], w[:, k, f * P:(f + 1) * P], yT[:, k, :],
                                          start=(k == 0), stop=(k == 3))
                    fill(last, "sc", n)
                elif name == "out_f":
                    if m == 0:
                        drained(pe, "sc", turn["sc", "fourier", 6])
                        drained(pe, "sc", turn["sc", "fourier", 7])
                    out_products(turn["sc", "out_f", m], m, 0)
                elif name == "pT":
                    drained(pe, "sc", turn["sc", "scores2", m])
                    for hh in range(2):
                        n = turn["tp", "pT2", 2 * m + hh]
                        claim(pe, "tp", n)
                        transposes(n, [s_buf[:, m % 2, hh, b * P:(b + 1) * P] for b in range(4)])
                elif name == "pv":
                    n = turn["mm", "o2", c]
                    if m == 0:
                        pe.wait_ge(v_win_loaded, 16 * 32)
                    if g == 0:
                        claim(pe, "mm", n)
                    for hh in range(2):
                        cols = slice((2 * g + hh) * DH, (2 * g + hh + 1) * DH)
                        drained(pe, "tp", turn["tp", "pT2", 2 * m + hh])
                        for b in range(4):
                            values = v_win[:, 2 * c + b, cols] if b < 2 else cv[:, b - 2, cols]
                            last = mm(buf("mm", n)[:, cols], pT[:, hh, b * P:(b + 1) * P], values,
                                      start=(b == 0), stop=(b == 3))
                    if g == 3:
                        fill(last, "mm", n)
                elif name == "oT":
                    n = turn["tp", "oT2", m]
                    drained(pe, "mm", turn["mm", "o2", m])
                    claim(pe, "tp", n)
                    transposes(n, [o_sb[:, b * P:(b + 1) * P] for b in range(4)])

        drained(pe, "tp", turn["tp", "oT2", TT - 1])
        for t in range(TT):
            out_products(turn["sc", "out", t], t, 4)

    @block.scalar
    def _(act):
        S = nc.scalar
        with nc.allow_non_contiguous_dma(reason="small vectors laid along partitions"):
            act.dma_start(gain1[:], A["norm_mix"][0].rearrange("(k p) -> p k", p=P)).then_inc(gain_loaded, 16)
            for n, name in enumerate(("da_q_norm", "da_k_norm")):
                for c in range(2):
                    act.dma_start(qk_gain[c * DH:(c + 1) * DH, n:n + 1],
                                  A[name].rearrange("a d -> d a")).then_inc(early_loaded, 16)

        for t in range(TT):
            act.wait_ge(x_loaded[t], 16)
            S.activation(xs[:, t, :], x[:, t, :], ACT.Square, accum_out=ssq[:, t:t + 1]).then_inc(ssq_ready, 1)
        with nc.allow_non_contiguous_dma(reason="small vectors laid along partitions"):
            act.dma_start(gain2[:], A["norm_ffn"][0].rearrange("(k p) -> p k", p=P)).then_inc(late_loaded, 16)
            act.dma_start(sub_gain[:], A["da_subln"].rearrange("a d -> d a")).then_inc(late_loaded, 16)
            for n, name in enumerate(("da_lambda_q1", "da_lambda_q2", "da_lambda_k1", "da_lambda_k2")):
                act.dma_start(lam_in[:, n, :], A[name].broadcast_to([P, DH])).then_inc(late_loaded, 16)
            act.dma_start(w_rt[:, :, 0:GROUPS], A["moe_w_group"][0].rearrange("(k p) g -> p k g", p=P)).then_inc(late_loaded, 16)
            act.dma_start(w_rt[:, :, GROUPS:20], A["moe_w_router"][0].rearrange("(k p) g -> p k g", p=P)).then_inc(late_loaded, 16)
            act.dma_start(b_rt[:, 0:GROUPS], A["moe_b_group"].broadcast_to([P, GROUPS])).then_inc(late_loaded, 16)
            act.dma_start(b_rt[:, GROUPS:20], A["moe_b_router"].broadcast_to([P, EXPERTS])).then_inc(late_loaded, 16)
            act.dma_start(b_ada[:], A["b_ada_2"][0].rearrange("(k p) -> p k", p=P)).then_inc(second_loaded, 16)
            act.dma_start(norm_g[:], A["norm_g_2"][0].rearrange("(k p) -> p k", p=P)).then_inc(second_loaded, 16)
            for n, name in enumerate(("q_norm_g_2", "k_norm_g_2")):
                for c in range(2):
                    act.dma_start(qk_gain2[c * DH:(c + 1) * DH, n:n + 1],
                                  A[name].rearrange("a d -> d a")).then_inc(second_loaded, 16)
            act.dma_start(cond[:, :, 0], A["c_2"][0].rearrange("(k p) -> p k", p=P)).then_inc(second_loaded, 16)
            act.dma_start(cond[:, :, 1], A["c_ctx_2"].rearrange("(k p) -> p k", p=P)).then_inc(second_loaded, 16)
            act.dma_start(mask[:], A["mask"]).then_inc(second_loaded, 16)
            act.dma_start(chan[:], A["chan"]).then_inc(second_loaded, 16)

        for i in range(6 * TT):
            c, t = divmod(i, TT)
            n = turn["mm", "proj", i]
            filled(act, "mm", n)
            if c < QK_CHUNKS:
                if i >= 2:
                    act.wait_ge(qk_ms_ready, i - 1)
                S.activation(pT[:, i % 2, :], buf("mm", n), ACT.Square).then_inc(sq_ready, 1)
            else:
                drain(S.copy(v[:, t, (c - QK_CHUNKS) * CH:(c - QK_CHUNKS + 1) * CH], buf("mm", n)), "mm", n)
            if 1 <= i <= QK_CHUNKS * TT:
                c, t = divmod(i - 1, TT)
                n = turn["tp", "qkT", i - 1]
                filled(act, "tp", n)
                if i == 1:
                    act.wait_ge(early_loaded, 4 * 16)
                    act.wait_ge(gains_scaled, 1)
                dst, g = (qT, 0) if c < 2 else (kT, 1)
                drain(S.activation(dst[:, 4 * (c % 2):4 * (c % 2) + 4, t * P:(t + 1) * P],
                                   buf("tp", n).rearrange("p (h n) -> p h n", h=4), ACT.Copy,
                                   scale=qk_gain[:, g:g + 1]), "tp", n)
            if i == 4:
                act.wait_ge(second_loaded, 10 * 16)
                S.activation(cond[:], cond[:], ACT.Silu).then_inc(cond_ready, 1)

        def norm2_squares(t):
            for c in range(2):
                drained(act, "mm", turn["mm", "w_out", 2 * t + c])
            S.activation(xs2[:, t, :], x[:, t, :], ACT.Square, accum_out=ssq[:, 4 + t:5 + t]).then_inc(ssq_ready, 1)

        act.wait_ge(lam_sum, 1)
        S.activation(lam[:, 2:4], lam[:, 0:2], ACT.Exp).then_inc(lam_exp, 1)
        for s in range(ATTENTION_STEPS):
            for name, m in attention_steps(s):
                t, h = divmod(m, HEADS)
                if name == "scores":
                    act.wait_ge(nmx_ready, m + 1)
                    for c in range(2):
                        sc = s_buf[:, m % 2, c, 0:(t + 1) * P]
                        last = S.activation(sc, sc, ACT.Exp, bias=nmx[:, m % 2, c:c + 1],
                                            accum_out=den[:, m % 2, c:c + 1])
                    last.then_inc(exp_ready, 1)
                elif name == "pdT":
                    n = turn["tp", "pdT", m]
                    filled(act, "tp", n)
                    drain(S.copy(pT[:, m % 2, 0:(t + 1) * P], buf("tp", n)[:, 0:(t + 1) * P]), "tp", n)
                elif name == "o_raw1":
                    drained(act, "mm", turn["mm", "o", 2 * m + 1])
                    S.activation(oT[:, :, m * P:(m + 1) * P], o_sb[:].rearrange("p (h e) -> p h e", h=HEADS),
                                 ACT.Square).then_inc(o_sq_ready, 1)
                elif name == "oT":
                    t = m
                    act.wait_ge(gains_scaled, 2)
                    for b in range(2):
                        n = turn["tp", "oT", 2 * t + b]
                        filled(act, "tp", n)
                        drain(S.activation(oT[:, 4 * b:4 * b + 4, t * P:(t + 1) * P],
                                           buf("tp", n).rearrange("p (h n) -> p h n", h=4), ACT.Copy,
                                           scale=sub_gain[:, 0:1]), "tp", n)
                elif name == "norm2":
                    for t in range(TT - 1):
                        norm2_squares(t)
                elif name == "xT2":
                    n = turn["tp", "xT2", 2 * m]
                    filled(act, "tp", n)
                    drain(S.copy(xT2[:, 2 * m, 0:LAST], buf("tp", n)[:, 0:LAST]), "tp", n)

        norm2_squares(TT - 1)
        n = turn["tp", "xT2_last", 0]
        filled(act, "tp", n)
        drain(S.copy(xT2[:, 0:4, LAST:SEQ], buf("tp", n).rearrange("p (k n) -> p k n", k=4)), "tp", n)
        n = turn["mm", "router_T"]
        filled(act, "mm", n)
        drain(S.copy(logit_T, buf("mm", n)[0:20, :]), "mm", n)
        act.wait_ge(ge_in, 1)
        S.activation(g_exp[:], g_exp[:], ACT.Exp).then_inc(ge_out, 1)
        act.wait_ge(ge_in, 2)
        S.activation(in_group[:], in_group[:], ACT.Exp).then_inc(ge_out, 1)
        for c in range(2):
            n = turn["mm", "g_x", c]
            filled(act, "mm", n)
            drain(S.copy(g_x[:, c * 512:(c + 1) * 512], buf("mm", n)), "mm", n)

        def silu(b, n, n_hid, more=0, more_hid=0):
            filled(act, "sc", n, more)
            if n_hid is not None:
                filled(act, "tp", n_hid, more_hid)
            S.activation(sg[:, b, :], buf("sc", n)[:, 0, :], ACT.Silu).then_inc(sg_ready, 1)

        def hid_copy(b, n, more=0):
            filled(act, "tp", n, more)
            drain(S.copy(hidT[:, b, :], buf("tp", n)), "tp", n)

        def y_copy(b, n, e, stored, more=0):
            filled(act, "sc", n, more)
            if stored is not None:
                act.wait_ge(y_stored[b], stored)
            drain(S.copy(y_sb[:, b, :].rearrange("p (m n) -> p m n", m=2), buf("sc", n)), "sc", n)
            drained(act, "sc", n, more)
            dst = y_d[e * P:(e + 1) * P, :] if isinstance(e, int) else y_d[bass.ds(e * P, P), :]
            act.dma_start(dst, y_sb[:, b, :]).then_inc(y_stored[b], 16)

        silu(0, turn_gu(0), None)
        hid_copy(0, turn_hid(0))
        silu(1, turn_gu(1), None)
        y_copy(0, turn_dn(0), 0, None)
        hid_copy(1, turn_hid(1))
        silu(0, turn_gu(2), turn_hid(0))
        y_copy(1, turn_dn(1), 1, None)
        hid_copy(0, turn_hid(2))
        with act.Fori(0, (EXPERTS - 4) // 2) as j:
            for e in (3, 4):
                silu(e % 2, turn_gu(e), turn_hid(e - 2), 2 * j, 3 * j)
                y_copy((e - 1) % 2, turn_dn(e - 1), 2 * j + (e - 1), 16 * j + 16 * ((e - 1) // 2), 2 * j)
                hid_copy(e % 2, turn_hid(e), 3 * j)
        for t in range(CT):
            act.wait_ge(ctx_loaded[t], 16)
            S.activation(buf_d[:, 2048 + t * D:2048 + (t + 1) * D], cx[:, t, :], ACT.Square,
                         accum_out=cssq[:, 0, t:t + 1]).then_inc(c_ssq_ready, 1)
        e = EXPERTS - 1
        silu(1, turn_gu(e), turn_hid(e - 2))
        act.wait_ge(mod_ready, 1)
        for k in range(0, KD, 2):
            n = turn["tp", "cxT", k]
            filled(act, "tp", n)
            for kk in range(2):
                last = S.activation(cxT[:, k + kk, :], buf("tp", n)[:, kk * CTX:(kk + 1) * CTX], ACT.Identity,
                                    bias=mod_sh[:, 1, k + kk:k + kk + 1], scale=mod_g[:, 1, k + kk:k + kk + 1])
            drain(last, "tp", n)
        y_copy(0, turn_dn(e - 1), e - 1, 16 * ((e - 1) // 2))
        hid_copy(1, turn_hid(e))
        y_copy(1, turn_dn(e), e, 16 * (e // 2))

        spills = spill_count(act)
        with act.If(spills > 0):
            act.wait_ge(y_stored[0], 16 * EXPERTS // 2)
            act.sem_inc(spill_y, 16)
            act.sem_inc(spill_act, 1)
            with act.Fori(0, SPILL) as o:
                with act.If(spills > o):
                    act.wait_ge(spill_pe, 4 * o + 3)
                    S.activation(sg[:, 0, :], SC[0][:, 0, :], ACT.Silu).then_inc(spill_act, 1)
                    act.wait_ge(spill_pe, 4 * o + 4)
                    S.copy(hidT[:, 0, :], TP[0]).then_inc(spill_act, 1)
                    act.wait_ge(spill_pe, 4 * o + 5)
                    act.wait_ge(spill_y, 16 * o + 16)
                    S.copy(y_sb[:, 0, :].rearrange("p (m n) -> p m n", m=2), SC[1]).then_inc(spill_act, 1)
                    act.wait_ge(spill_act, 3 * o + 4)
                    act.dma_start(y_d[bass.ds(o * P + EXPERTS * P, P), :], y_sb[:, 0, :]).then_inc(spill_y, 16)

        act.sem_inc(spills_done, 1)

        qk_from = QK_CHUNKS * TT

        def qk_squares(j):
            n = turn["mm", *QK2[j]]
            filled(act, "mm", n)
            if j >= 2:
                act.wait_ge(qk_ms_ready, qk_from + j - 1)
            S.activation(pT[:, j % 2, :], buf("mm", n), ACT.Square).then_inc(sq_ready, 1)

        for i, (what, t) in enumerate(PROJ2):
            n = turn["mm", what, t]
            if (what, t) == ("ck", 0):
                for tt in range(TT):
                    act.wait_ge(x2_ready, tt + 1)
                    if tt >= 2:
                        act.wait_ge(ssq_ready, 8 + tt - 1)
                    S.activation(s_buf[:, tt % 2].rearrange("p a n -> p (a n)"), x[:, tt, :], ACT.Square,
                                 accum_out=ssq[:, tt:tt + 1]).then_inc(ssq_ready, 1)
            if (what, t) == ("k", 0):
                for k in range(0, KD, 2):
                    nk = turn["tp", "x3T", k]
                    filled(act, "tp", nk)
                    drain(S.activation(x3T[:, k, :], buf("tp", nk), ACT.Identity, bias=mod_sh[:, 0, k:k + 1],
                                       scale=mod_g[:, 0, k:k + 1]), "tp", nk)
            if (what, t) in QK2:
                qk_squares(QK2.index((what, t)))
            else:
                filled(act, "mm", n)
                if what == "cv":
                    drain(S.copy(cv[:, t, :], buf("mm", n)), "mm", n)
                elif what == "v":
                    if t >= 2:
                        act.wait_ge(v_stored[t % 2], 16)
                    drain(S.copy(o_sb[:, (t % 2) * 512:(t % 2 + 1) * 512], buf("mm", n)), "mm", n)
                    drained(act, "mm", n)
                    act.dma_start(v_d[t * P:(t + 1) * P, :], o_sb[:, (t % 2) * 512:(t % 2 + 1) * 512]).then_inc(v_stored[t % 2], 16)
                elif what == "u":
                    drain(S.copy(u[:, t, :], buf("mm", n)), "mm", n)
                else:
                    dst = ngT if what == "ng" else fgT
                    drain(S.activation(dst[:, t, :], buf("mm", n), ACT.Silu), "mm", n)
            if i >= 1 and PROJ2[i - 1] in QK2:
                j = QK2.index(PROJ2[i - 1])
                what, t = QK2[j]
                n = turn["tp", "qkT2", j]
                filled(act, "tp", n)
                if what == "q":
                    for r in range(2):
                        dst = q2T.rearrange("p g (c r w) -> p g c r w", c=TT, r=ROWS_G)[:, :, :, 2 * t + r, :]
                        src = buf("tp", n).rearrange("p (g r c w) -> p g r c w", g=4, r=2, c=TT)[:, :, r, :, ::-1]
                        last = S.activation(dst, src, ACT.Copy, scale=qk_gain2[:, 0:1])
                    drain(last, "tp", n)
                else:
                    dst = ckT if what == "ck" else k2T
                    drain(S.activation(dst[:, :, t * P:(t + 1) * P], buf("tp", n).rearrange("p (g n) -> p g n", g=4),
                                       ACT.Copy, scale=qk_gain2[:, 1:2]), "tp", n)

        for s in range(MIXER_STEPS):
            for name, m in mixer_steps(s):
                if name == "scores":
                    n = turn["sc", "scores2", m]
                    act.wait_ge(neg_max, m + 1)
                    if m >= 2:
                        filled(act, "tp", turn["tp", "pT2", 2 * (m - 2) + 1])
                    for hh in range(2):
                        last = S.activation(s_buf[:, m % 2, hh, :], buf("sc", n)[:, hh, :], ACT.Exp,
                                            bias=nmx[:, m % 2, hh:hh + 1],
                                            accum_out=rden[:, (m // 4) % 2, 2 * (m % 4) + hh:2 * (m % 4) + hh + 1])
                    drain(last, "sc", n)
                elif name == "fourier" and m < 6:
                    n = turn["sc", "fourier", m]
                    filled(act, "sc", n)
                    if m == 0:
                        act.wait_ge(bias_ready, 3)
                    if m < 4:
                        S.copy(seqT[:, m, :, 0:FREQ], buf("sc", n)[:, :, 0:FREQ])
                        S.copy(seqT[:, m, 0, FREQ:SEQ], buf("sc", n)[:, 0, 1:FREQ - 1][:, ::-1])
                        drain(S.activation(seqT[:, m, 1, FREQ:SEQ], buf("sc", n)[:, 1, 1:FREQ - 1][:, ::-1], ACT.Copy,
                                           scale=-1.0), "sc", n)
                    else:
                        drain(S.copy(yT[:, 2 * (m - 4):2 * (m - 4) + 2, :], buf("sc", n)), "sc", n)
                elif name == "pT":
                    for hh in range(2):
                        n = turn["tp", "pT2", 2 * m + hh]
                        filled(act, "tp", n)
                        drain(S.copy(pT[:, hh, :], buf("tp", n)), "tp", n)

    @block.vector
    def _(dve):
        V = nc.vector
        links = [0]

        def link(ins):
            links[0] += 1
            ins.then_inc(dve_done, 1)
            dve.wait_ge(dve_done, links[0])

        def norm1(t):
            dve.wait_ge(ssq_ready, t + 1)
            V.tensor_scalar(ms[:, t:t + 1], ssq[:, t:t + 1], 1.0 / D, EPS, ALU.mult, ALU.add).then_inc(ms_ready, 1)
            dve.wait_ge(rstd_ready, t + 1)
            V.tensor_scalar(xs[:, t, :], x[:, t, :], rstd[:, t:t + 1], None, ALU.mult).then_inc(xs_ready, 1)

        def h_copies(t):
            for b in range(2):
                n = turn["tp", "hT", 2 * t + b]
                filled(dve, "tp", n)
                drain(V.tensor_tensor(hT[:, 4 * b:4 * b + 4, t * P:(t + 1) * P],
                                      buf("tp", n).rearrange("p (k n) -> p k n", k=4),
                                      gain1[:, 4 * b:4 * b + 4].unsqueeze(2).to_broadcast([P, 4, P]), ALU.mult), "tp", n)

        norm1(0)
        dve.wait_ge(gain_loaded, 16)
        h_copies(0)
        dve.wait_ge(early_loaded, 4 * 16)
        V.tensor_scalar(qk_gain[:, 0:1], qk_gain[:, 0:1], DH ** -0.5, None, ALU.mult).then_inc(gains_scaled, 1)
        for t in range(1, TT):
            norm1(t)

        def ada_sums(c, steps):
            for step in steps:
                k, b = divmod(step, 2) if c < 4 else (step, step % 2)
                if step == 0:
                    dve.wait_ge(cond_ready, 1)
                    dve.wait_ge(ada_landed[c % 2], 16 * (c // 2 + 1))
                w = ring[:, c % 2, k * 512:(k + 1) * 512]
                scale = cond[:, k, b:b + 1] if c < 4 else cond[:, k, 0:1]
                if step < 2:
                    ins = V.tensor_scalar(ada_acc[:, b, :], w, scale, None, ALU.mult)
                else:
                    dve.wait_ge(ada_step, (ADA_OPS[c - 1] if c > 0 else 0) + step - 1)
                    ins = V.scalar_tensor_tensor(out=ada_acc[:, b, :], in0=w, scalar=scale, in1=ada_acc[:, b, :],
                                                 op0=ALU.mult, op1=ALU.add)
                ins.then_inc(ada_step, 1)

        def ada_out(c):
            n = turn["tp", "ada", c]
            filled(dve, "tp", n)
            cols = slice(4 * (c % 2), 4 * (c % 2) + 4)
            added = b_ada[:, 4 * c:4 * c + 4]
            if c < 4:
                dst = (mod_sh if c < 2 else mod_g)[:, :, cols]
                drain(V.tensor_tensor(dst, buf("tp", n)[:, 0:8].rearrange("p (b k) -> p b k", b=2),
                                      added.unsqueeze(1).to_broadcast([P, 2, 4]), ALU.add), "tp", n)
            else:
                drain(V.tensor_tensor(gate_col[:, cols], buf("tp", n)[:, 0:4], added, ALU.add), "tp", n)

        for i in range(QK_CHUNKS * TT):
            b = i % 2
            if i < TT - 1:
                h_copies(i + 1)
            if i in (10, 14):
                ada_out((i - 10) // 4)
            dve.wait_ge(sq_ready, i + 1)
            link(V.tensor_reduce(qk_st[:, b, 0, :], pT[:, b, :].rearrange("p (g d) -> p g d", d=DH), AX.X, ALU.add))
            V.tensor_scalar(qk_st[:, b, 1, :], qk_st[:, b, 0, :], 1.0 / DH, EPS, ALU.mult, ALU.add).then_inc(qk_ms_ready, 1)
            dve.wait_ge(qk_rstd_ready, i + 1)
            n = turn["mm", "proj", i]
            filled(dve, "mm", n)
            if i >= 2:
                filled(dve, "tp", turn["tp", "qkT", i - 2])
            drain(V.tensor_tensor(pd[:, b, :].rearrange("p (g d) -> p g d", d=DH),
                                  buf("mm", n).rearrange("p (g d) -> p g d", d=DH),
                                  qk_st[:, b, 2, :].unsqueeze(2).to_broadcast([P, 8, DH]), ALU.mult), "mm", n)
            if 6 <= i < 9 or 10 <= i < 13:
                first = 6 * ((i - 6) % 4)
                ada_sums((i - 6) // 4, range(first, min(first + 6, 16)))
            elif i in (14, 15):
                ada_sums(2, range(8 * (i - 14), 8 * (i - 13)))

        ada_out(2)
        for c in range(3, ADA_CHUNKS):
            ada_sums(c, range(ADA_OPS[c] - ADA_OPS[c - 1]))
            ada_out(c)
        drained(dve, "tp", turn["tp", "ada", 3])
        V.scalar_tensor_tensor(out=mod_g[:], in0=mod_g[:], scalar=1.0, in1=norm_g[:].unsqueeze(1).to_broadcast([P, 2, KD]),
                               op0=ALU.add, op1=ALU.mult).then_inc(mod_ready, 1)
        V.tensor_scalar(qk_gain2[:, 0:1], qk_gain2[:, 0:1], DH ** -0.5, None, ALU.mult)

        dve.wait_ge(late_loaded, 10 * 16)
        V.tensor_scalar(sub_gain[:], sub_gain[:], 1.0 - LAMBDA_INIT, None, ALU.mult).then_inc(gains_scaled, 1)
        link(V.tensor_tensor(lam_pr[:], lam_in[:, 0:2, :], lam_in[:, 2:4, :], ALU.mult))
        V.tensor_reduce(lam[:, 0:2], lam_pr[:], AX.X, ALU.add).then_inc(lam_sum, 1)
        V.tensor_tensor(w_rt[:], w_rt[:], gain2[:].unsqueeze(2).to_broadcast([P, KD, 20]), ALU.mult).then_inc(w_rt_ready, 1)
        dve.wait_ge(lam_exp, 1)
        link(V.tensor_tensor(lam[:, 0:1], lam[:, 3:4], lam[:, 2:3], ALU.subtract))
        link(V.tensor_scalar(lam[:, 1:2], lam[:, 0:1], LAMBDA_INIT, None, ALU.subtract))
        neg_lambda = lam[:, 1:2]
        dve.wait_ge(pool_consts, 2)
        dve.wait_ge(ids_zeroed, 16)
        dve.wait_ge(y_zeroed, 16)

        def norm2(tiles):
            for t in tiles:
                dve.wait_ge(ssq_ready, 4 + t + 1)
                V.tensor_scalar(ms[:, 4 + t:5 + t], ssq[:, 4 + t:5 + t], 1.0 / D, EPS, ALU.mult, ALU.add).then_inc(ms_ready, 1)
            for t in tiles:
                dve.wait_ge(rstd_ready, 4 + t + 1)
                V.tensor_scalar(xs2[:, t, :], x[:, t, :], rstd[:, 4 + t:5 + t], None, ALU.mult).then_inc(xs2_ready, 1)

        for s in range(ATTENTION_STEPS):
            for name, m in attention_steps(s):
                t, h = divmod(m, HEADS)
                b = m % 2
                w = (t + 1) * P
                if name == "scores":
                    n = turn["sc", "scores", m]
                    filled(dve, "sc", n)
                    if m >= 2:
                        dve.wait_ge(pd_ready, m - 1)
                    drain(V.scalar_tensor_tensor(out=s_buf[:, b, :, 0:w],
                                                 in0=dist[:, 512 - w:512].unsqueeze(1).to_broadcast([P, 2, w]),
                                                 scalar=2.0 ** -(h + 1), in1=buf("sc", n)[:, :, 0:w],
                                                 op0=ALU.mult, op1=ALU.add), "sc", n)
                    drained(dve, "sc", n)
                    V.tensor_reduce(nmx[:, b, :], s_buf[:, b, :, 0:w], AX.X, ALU.max, negate=True).then_inc(nmx_ready, 1)
                elif name == "pd":
                    dve.wait_ge(exp_ready, m + 1)
                    V.reciprocal(rden[:, t % 2, h:h + 1], den[:, b, 0:1])
                    link(V.reciprocal(ratio[:, b, 0:1], den[:, b, 1:2]))
                    link(V.scalar_tensor_tensor(out=ratio[:, b, 1:2], in0=den[:, b, 0:1], scalar=neg_lambda,
                                                in1=ratio[:, b, 0:1], op0=ALU.mult, op1=ALU.mult))
                    if m >= 2:
                        filled(dve, "tp", turn["tp", "pdT", m - 2])
                    V.scalar_tensor_tensor(out=pd[:, b, 0:w], in0=s_buf[:, b, 1, 0:w], scalar=ratio[:, b, 1:2],
                                           in1=s_buf[:, b, 0, 0:w], op0=ALU.mult, op1=ALU.add).then_inc(pd_ready, 1)
                elif name in ("o_raw0", "o_raw1"):
                    t, g = m, int(name[-1])
                    if t > 0 and g == 0:
                        filled(dve, "tp", turn["tp", "oT", 2 * t - 1])
                    n = turn["mm", "o", 2 * t + g]
                    filled(dve, "mm", n)
                    drain(V.tensor_tensor(o_sb[:, g * 512:(g + 1) * 512].rearrange("p (h e) -> p h e", h=4),
                                          buf("mm", n).rearrange("p (h e) -> p h e", h=4),
                                          rden[:, t % 2, 4 * g:4 * g + 4].unsqueeze(2).to_broadcast([P, 4, P]),
                                          ALU.mult), "mm", n)
                elif name == "o_mean":
                    dve.wait_ge(o_sq_ready, m + 1)
                    link(V.tensor_reduce(o_st[:, 0, :], oT[:, :, m * P:(m + 1) * P], AX.X, ALU.add))
                    V.tensor_scalar(o_st[:, 1, :], o_st[:, 0, :], 1.0 / P, EPS, ALU.mult, ALU.add).then_inc(o_ms_ready, 1)
                elif name == "o_norm":
                    dve.wait_ge(o_rstd_ready, m + 1)
                    o3 = o_sb[:].rearrange("p (h e) -> p h e", h=HEADS)
                    V.tensor_tensor(o3, o3, o_st[:, 2, :].unsqueeze(2).to_broadcast([P, HEADS, P]),
                                    ALU.mult).then_inc(o_norm_ready, 1)
                elif name in ("x_add0", "x_add1"):
                    c = int(name[-1])
                    n = turn["mm", "w_out", 2 * m + c]
                    filled(dve, "mm", n)
                    xt = x[:, m, c * CH:(c + 1) * CH]
                    drain(V.tensor_tensor(xt, xt, buf("mm", n), ALU.add), "mm", n)
                elif name == "norm2":
                    norm2(range(TT - 1))
                    filled(dve, "tp", turn["tp", "oT", 2 * TT - 1])
                    drained(dve, "tp", turn["tp", "ada", 5])
                    V.tensor_tensor(gate_diag, ident[:].unsqueeze(1).to_broadcast([P, KD, P]),
                                    gate_col[:].unsqueeze(2).to_broadcast([P, KD, P]), ALU.mult).then_inc(gate_ready, 1)
                elif name == "xT2":
                    n = turn["tp", "xT2", 2 * m + 1]
                    filled(dve, "tp", n)
                    drain(V.tensor_copy(xT2[:, 2 * m + 1, 0:LAST], buf("tp", n)[:, 0:LAST]), "tp", n)

        norm2([TT - 1])
        n = turn["tp", "xT2_last", 1]
        filled(dve, "tp", n)
        drain(V.tensor_copy(xT2[:, 4:8, LAST:SEQ], buf("tp", n).rearrange("p (k n) -> p k n", k=4)), "tp", n)

        def wide(ap, k):
            return ap.unsqueeze(2).to_broadcast([P, TT, k])

        n = turn["mm", "router"]
        filled(dve, "mm", n)
        drain(V.tensor_tensor(logit[:], buf("mm", n)[:, 0:TT * 20].rearrange("p (t e) -> p t e", t=TT),
                              b_rt[:].unsqueeze(1).to_broadcast([P, TT, 20]), ALU.add), "mm", n)
        drained(dve, "mm", n)
        dve.wait_ge(pool_consts, 3)

        def first_of_max(out_ap, values, top, k=4):
            link(V.tensor_tensor(r_b[:], values, wide(top, k), ALU.is_equal))
            link(V.tensor_tensor(r_c[:], r_b[:], prio[:].unsqueeze(1).to_broadcast([P, TT, k]), ALU.mult))
            link(V.tensor_reduce(r_m[:, 5, :], r_c[:], AX.X, ALU.max))
            link(V.tensor_tensor(out_ap, r_c[:], wide(r_m[:, 5, :], k), ALU.is_equal))

        groups = logit[:, :, 0:GROUPS]
        link(V.tensor_reduce(r_m[:, 0, :], groups, AX.X, ALU.max))
        V.tensor_tensor(g_exp[:], groups, wide(r_m[:, 0, :], GROUPS), ALU.subtract).then_inc(ge_in, 1)
        first_of_max(g_pick[:], groups, r_m[:, 0, :])
        link(V.tensor_tensor(r_a[:].rearrange("p t (g e) -> p t g e", g=GROUPS),
                             logit[:, :, GROUPS:20].rearrange("p t (g e) -> p t g e", g=GROUPS),
                             g_pick[:].unsqueeze(3).to_broadcast([P, TT, GROUPS, PER_GROUP]), ALU.mult))
        link(V.tensor_reduce(in_group[:], r_a[:].rearrange("p t (g e) -> p t e g", g=GROUPS), AX.X, ALU.add))
        link(V.tensor_reduce(r_m[:, 1, :], in_group[:], AX.X, ALU.max))
        V.tensor_tensor(in_group[:], in_group[:], wide(r_m[:, 1, :], PER_GROUP), ALU.subtract).then_inc(ge_in, 1)
        dve.wait_ge(ge_out, 2)
        link(V.tensor_reduce(r_m[:, 1, :], in_group[:], AX.X, ALU.max))
        first_of_max(e_pick[:, 0], in_group[:], r_m[:, 1, :])
        link(V.scalar_tensor_tensor(out=in_group[:], in0=e_pick[:, 0], scalar=-4.0, in1=in_group[:],
                                    op0=ALU.mult, op1=ALU.add))
        link(V.tensor_reduce(r_m[:, 2, :], in_group[:], AX.X, ALU.max))
        first_of_max(e_pick[:, 1], in_group[:], r_m[:, 2, :])
        for c in range(2):
            last = V.tensor_tensor(picks[:, c].rearrange("p t (g e) -> p t g e", g=GROUPS),
                                   g_pick[:].unsqueeze(3).to_broadcast([P, TT, GROUPS, PER_GROUP]),
                                   e_pick[:, c].unsqueeze(2).to_broadcast([P, TT, GROUPS, PER_GROUP]), ALU.mult)
        link(last)
        V.tensor_tensor(sel[:], picks[:, 0], picks[:, 1], ALU.add).then_inc(sel_ready, 1)
        link(V.tensor_reduce(r_m[:, 3, :], g_exp[:], AX.X, ALU.add))
        link(V.tensor_tensor(r_m[:, 4, :], r_m[:, 1, :], r_m[:, 2, :], ALU.add))
        link(V.tensor_tensor(r_m[:, 3, :], r_m[:, 3, :], r_m[:, 4, :], ALU.mult))
        link(V.reciprocal(r_m[:, 4, :], r_m[:, 3, :]))
        V.tensor_tensor(weight[:, 0, :], r_m[:, 1, :], r_m[:, 4, :], ALU.mult)
        V.tensor_tensor(weight[:, 1, :], r_m[:, 2, :], r_m[:, 4, :], ALU.mult)
        n = turn["mm", "places"]
        filled(dve, "mm", n)
        drain(V.tensor_copy(place[:], buf("mm", n)[:, 0:(TT + 1) * 16].rearrange("p (t e) -> p t e", e=16)), "mm", n)
        drained(dve, "mm", n)
        at_place = r_a[:]
        for c in range(2):
            link(V.tensor_tensor(at_place, picks[:, c], place[:, 0:TT, :], ALU.mult))
            link(V.tensor_reduce(place_f[:, c, :], at_place, AX.X, ALU.add))
        dve.wait_ge(iota_ready, 1)
        for i in range(2 * TT):
            c, t = divmod(i, TT)
            V.tensor_scalar(slot_pick[:, i, :], slots_iota, place_f[:, c, t:t + 1], tok_f[:, t:t + 1],
                            ALU.is_equal, ALU.mult).then_inc(pick_ready, 1)
        n = turn["mm", "ids"]
        filled(dve, "mm", n)
        drain(V.tensor_copy(idx[:, 0:EXPERTS], buf("mm", n)[:, 0:EXPERTS]), "mm", n)
        length = place[:, TT, :]
        tiles, upto = full_tiles[:, 0, :], full_tiles[:, 1, :]
        link(V.tensor_scalar(tiles, length, float(P), None, ALU.is_gt))
        for q in (2, 3):
            link(V.scalar_tensor_tensor(out=tiles, in0=length, scalar=float(q * P), in1=tiles, op0=ALU.is_gt, op1=ALU.add))
        link(V.tensor_tensor_scan(upto, ones[:, 0:16], tiles, 0.0, ALU.mult, ALU.add))
        before = s_buf[:, 0, 0, 0:SPILL * EXPERTS].rearrange("p (o e) -> p o e", o=SPILL)
        spill_f = s_buf[:, 0, 1, 0:SPILL + 1]
        link(V.tensor_tensor(before, upto.unsqueeze(1).to_broadcast([P, SPILL, EXPERTS]),
                             iota16[:, 0:SPILL].unsqueeze(2).to_broadcast([P, SPILL, EXPERTS]), ALU.is_le))
        V.tensor_reduce(spill_f[:, 0:SPILL], before, AX.X, ALU.add)
        link(V.tensor_copy(spill_f[:, SPILL:SPILL + 1], upto[:, EXPERTS - 1:EXPERTS]))
        link(V.tensor_scalar(spill_f, spill_f, float(EXPERTS - 1), None, ALU.min))
        V.tensor_copy(spill_i[:], spill_f).then_inc(spill_ready, 1)
        spill_base, step_back = full_tiles[:, 2, :], full_tiles[:, 3, :]
        link(V.tensor_tensor(spill_base, upto, tiles, ALU.subtract))
        link(V.tensor_scalar(spill_base, spill_base, float(P), float((EXPERTS - 1) * P), ALU.mult, ALU.add))
        link(V.scalar_tensor_tensor(out=step_back, in0=iota16[:], scalar=float(P), in1=spill_base,
                                    op0=ALU.mult, op1=ALU.subtract))
        link(V.tensor_scalar(r_a[:], place[:, 0:TT, :], float(P), None, ALU.is_lt))
        link(V.tensor_tensor(r_a[:], r_a[:], step_back.unsqueeze(1).to_broadcast([P, TT, EXPERTS]), ALU.mult))
        link(V.tensor_tensor(r_a[:], r_a[:], spill_base.unsqueeze(1).to_broadcast([P, TT, EXPERTS]), ALU.add))
        link(V.tensor_tensor(r_a[:], r_a[:], place[:, 0:TT, :], ALU.add))
        for c in range(2):
            link(V.tensor_tensor(picks[:, c], picks[:, c], r_a[:], ALU.mult))
            link(V.tensor_reduce(row_f[:, c, :], picks[:, c], AX.X, ALU.add))
        V.tensor_copy(row_i[:], row_f[:]).then_inc(rows_ready, 1)

        def x_copy(b, n, more=0):
            for half_row in range(2):
                filled(dve, "tp", n + half_row, more)
                drain(V.tensor_tensor(xgT[:, b, 4 * half_row:4 * half_row + 4, :],
                                      buf("tp", n + half_row).rearrange("p (k n) -> p k n", k=4),
                                      gain2[:, 4 * half_row:4 * half_row + 4].unsqueeze(2).to_broadcast([P, 4, P]),
                                      ALU.mult), "tp", n + half_row)

        def hidden(b, n, n_sg, more=0):
            dve.wait_ge(sg_ready, n_sg)
            filled(dve, "sc", n, more)
            drain(V.tensor_tensor(sg[:, b, :], sg[:, b, :], buf("sc", n)[:, 1, :], ALU.mult), "sc", n)

        x_copy(0, turn_x(0))
        hidden(0, turn_gu(0), 1)
        x_copy(1, turn_x(1))
        with dve.Fori(0, EXPERTS // 2 - 1) as j:
            for e in (1, 2):
                hidden(e % 2, turn_gu(e), 2 * j + (e + 1), 2 * j)
                x_copy((e + 1) % 2, turn_x(e + 1), 3 * j)
        for t in range(CT):
            dve.wait_ge(c_ssq_ready, t + 1)
            V.tensor_scalar(cssq[:, 1, t:t + 1], cssq[:, 0, t:t + 1], 1.0 / D, EPS, ALU.mult, ALU.add).then_inc(c_ms_ready, 1)
            dve.wait_ge(c_rstd_ready, t + 1)
            V.tensor_scalar(cx[:, t, :], cx[:, t, :], cssq[:, 2, t:t + 1], None, ALU.mult).then_inc(cx_ready, 1)
        e = EXPERTS - 1
        hidden(1, turn_gu(e), e + 1)

        spills = spill_count(dve)
        with dve.If(spills > 0):
            with dve.Fori(0, SPILL) as o:
                with dve.If(spills > o):
                    dve.wait_ge(spill_pe, 4 * o + 2)
                    for half_row in range(2):
                        last = V.tensor_tensor(xgT[:, 0, 4 * half_row:4 * half_row + 4, :],
                                               TP[half_row].rearrange("p (k n) -> p k n", k=4),
                                               gain2[:, 4 * half_row:4 * half_row + 4].unsqueeze(2).to_broadcast([P, 4, P]),
                                               ALU.mult)
                    last.then_inc(spill_dve, 1)
                    dve.wait_ge(spill_act, 3 * o + 2)
                    V.tensor_tensor(sg[:, 0, :], sg[:, 0, :], SC[0][:, 1, :], ALU.mult).then_inc(spill_dve, 1)

        def add_rows(t):
            for c in range(2):
                dve.wait_ge(yg_ready[(2 * t + c) % 4], 16 * ((2 * t + c) // 4 + 1))
                ins = V.scalar_tensor_tensor(out=x[:, t, :], in0=yg[:, (2 * t + c) % 4, :], scalar=weight[:, c, t:t + 1],
                                             in1=x[:, t, :], op0=ALU.mult, op1=ALU.add)
                if c == 0:
                    link(ins)
            ins.then_inc(x2_ready, 1)

        qk_from = QK_CHUNKS * TT
        for t in range(TT):
            add_rows(t)
        for t in range(TT):
            dve.wait_ge(ssq_ready, 8 + t + 1)
            V.tensor_scalar(ms[:, t:t + 1], ssq[:, t:t + 1], 1.0 / D, EPS, ALU.mult, ALU.add).then_inc(ms_ready, 1)
        for j, item in enumerate(QK2):
            if item == ("ck", 1):
                for t in range(TT):
                    dve.wait_ge(rstd_ready, 8 + t + 1)
                    V.tensor_scalar(xs3[:, t, :], x[:, t, :], rstd[:, t:t + 1], None, ALU.mult).then_inc(xs3_ready, 1)
                for k in range(1, KD, 2):
                    n = turn["tp", "x3T", k]
                    filled(dve, "tp", n)
                    drain(V.tensor_scalar(x3T[:, k, :], buf("tp", n), mod_g[:, 0, k:k + 1], mod_sh[:, 0, k:k + 1],
                                          ALU.mult, ALU.add), "tp", n)
            b = j % 2
            dve.wait_ge(sq_ready, qk_from + j + 1)
            link(V.tensor_reduce(qk_st[:, b, 0, :], pT[:, b, :].rearrange("p (g d) -> p g d", d=DH), AX.X, ALU.add))
            V.tensor_scalar(qk_st[:, b, 1, :], qk_st[:, b, 0, :], 1.0 / DH, EPS, ALU.mult, ALU.add).then_inc(qk_ms_ready, 1)
            dve.wait_ge(qk_rstd_ready, qk_from + j + 1)
            n = turn["mm", *item]
            filled(dve, "mm", n)
            if j >= 2:
                filled(dve, "tp", turn["tp", "qkT2", j - 2])
            drain(V.tensor_tensor(pd[:, b, :].rearrange("p (g d) -> p g d", d=DH),
                                  buf("mm", n).rearrange("p (g d) -> p g d", d=DH),
                                  qk_st[:, b, 2, :].unsqueeze(2).to_broadcast([P, 8, DH]), ALU.mult), "mm", n)

        def gate_and_add(n, t, gated, signal):
            filled(dve, "sc", n)
            drain(V.tensor_tensor(gated.rearrange("p (a n) -> p a n", a=2), buf("sc", n),
                                  g_x[:].rearrange("p (a n) -> p a n", a=2), ALU.mult), "sc", n)
            drained(dve, "sc", n)
            V.tensor_tensor(x[:, t, :], x[:, t, :], gated, ALU.add).then_inc(signal, 1)

        for s in range(MIXER_STEPS):
            for name, m in mixer_steps(s):
                c, g = divmod(m, 4)
                if name == "scores":
                    n = turn["sc", "scores2", m]
                    filled(dve, "sc", n)
                    dve.wait_ge(bias_ready, MASK[c] + 1)
                    local = buf("sc", n)[:, :, 0:256]
                    link(V.tensor_tensor(local, local, bias[MASK[c]].rearrange("p (h n) -> p h n", h=H2)[:, 2 * g:2 * g + 2, :],
                                         ALU.add))
                    V.tensor_reduce(nmx[:, m % 2, :], buf("sc", n), AX.X, ALU.max, negate=True).then_inc(neg_max, 1)
                elif name == "fourier" and m >= 6:
                    n = turn["sc", "fourier", m]
                    filled(dve, "sc", n)
                    drain(V.tensor_tensor(mixT[:, 2 * (m - 6):2 * (m - 6) + 2, :], buf("sc", n),
                                          fgT[:, 2 * (m - 6):2 * (m - 6) + 2, :], ALU.mult), "sc", n)
                elif name == "out_f":
                    if m > 0:
                        dve.wait_ge(out_f_added, m)
                    gate_and_add(turn["sc", "out_f", m], m, pd[:, :, :].rearrange("p a n -> p (a n)"), out_f_added)
                elif name == "pv" and g == 3:
                    n = turn["mm", "o2", c]
                    drained(dve, "sc", turn["sc", "scores2", m])
                    link(V.reciprocal(rden[:, c % 2, :], rden[:, c % 2, :]))
                    filled(dve, "mm", n)
                    if c > 0:
                        filled(dve, "tp", turn["tp", "oT2", c - 1])
                    drain(V.tensor_tensor(o_sb[:, 0:512].rearrange("p (h d) -> p h d", h=H2),
                                          buf("mm", n).rearrange("p (h d) -> p h d", h=H2),
                                          rden[:, c % 2, :].unsqueeze(2).to_broadcast([P, H2, DH]), ALU.mult), "mm", n)
                elif name == "oT":
                    n = turn["tp", "oT2", m]
                    filled(dve, "tp", n)
                    cols = slice(m * QC, (m + 1) * QC)
                    grid = lambda ap: ap.rearrange("p f (r w) -> p f r w", w=GRID)[:, :, :, cols]
                    drain(V.tensor_tensor(grid(mixT[:, 4:8, :]), buf("tp", n).rearrange("p (f r w) -> p f r w", f=4, r=ROWS_G)[:, :, :, ::-1],
                                          grid(ngT[:, :, :]), ALU.mult), "tp", n)

        dve.wait_ge(out_f_added, TT)
        for t in range(TT):
            if t >= 2:
                dve.wait_ge(out_ready, t - 1)
            gate_and_add(turn["sc", "out", t], t, o_sb[:] if t % 2 == 0 else pd[:, :, :].rearrange("p a n -> p (a n)"),
                         out_ready)

    @block.gpsimd
    def _(pool):
        G = nc.gpsimd
        links = [0]

        def link(ins):
            links[0] += 1
            ins.then_inc(pool_done, 1)
            pool.wait_ge(pool_done, links[0])

        link(G.memset(half[:], -0.5))
        link(G.memset(ones[:], 1.0))
        G.affine_select(out=ident[:], in_=ones[:], compare_op=ALU.is_equal, fill=0.0, base=0,
                        pattern=[[1, P]], channel_multiplier=-1).then_inc(pool_consts, 1)

        def power(dst, src, width, signal):
            G.tensor_tensor(dst, src, half[:, 0:width], ALU.pow).then_inc(signal, 1)

        for t in range(TT):
            pool.wait_ge(ms_ready, t + 1)
            power(rstd[:, t:t + 1], ms[:, t:t + 1], 1, rstd_ready)
        link(G.iota(dist, pattern=[[1, 512]], base=P - 512, channel_multiplier=-1,
                    allow_small_or_imprecise_dtypes=True))
        G.affine_select(out=dist, in_=dist, compare_op=ALU.is_ge, fill=-BIG, base=512 - P,
                        pattern=[[-1, 512]], channel_multiplier=1).then_inc(pool_consts, 1)
        G.affine_select(out=tri[:], in_=ones[:], compare_op=ALU.is_gt, fill=0.0, base=0,
                        pattern=[[1, P]], channel_multiplier=-1)
        G.iota(iota16[:], pattern=[[1, 16]], base=0, channel_multiplier=0, allow_small_or_imprecise_dtypes=True)
        G.iota(prio[:], pattern=[[-1, 4]], base=4, channel_multiplier=0, allow_small_or_imprecise_dtypes=True)
        link(G.memset(zeros[:], 0.0))
        G.memset(sel_pad[:], 0.0)
        G.iota(tok_f[:], pattern=[[P, TT]], base=0, channel_multiplier=1, allow_small_or_imprecise_dtypes=True)
        G.iota(tok_i[:], pattern=[[P, TT]], base=0, channel_multiplier=1).then_inc(pool_consts, 1)
        pool.wait_ge(pool_consts, 3)
        pool.dma_start(ids_d.rearrange("(p c) a -> p (c a)", p=P), zeros[:, 0:ROWS // P].bitcast(I32)).then_inc(ids_zeroed, 16)
        pool.dma_start(y_d[EXPERTS * P:ROWS, :].rearrange("(p s) (c n) -> p (s c) n", p=P, n=P),
                       zeros[:].unsqueeze(1).to_broadcast([P, SPILL * KD, P])).then_inc(y_zeroed, 16)
        for i in range(QK_CHUNKS * TT):
            pool.wait_ge(qk_ms_ready, i + 1)
            power(qk_st[:, i % 2, 2, :], qk_st[:, i % 2, 1, :], 8, qk_rstd_ready)
        for t in range(TT):
            pool.wait_ge(o_ms_ready, t + 1)
            power(o_st[:, 2, :], o_st[:, 1, :], 8, o_rstd_ready)
        for tiles in (range(TT - 1), [TT - 1]):
            for t in tiles:
                pool.wait_ge(ms_ready, TT + t + 1)
                power(rstd[:, 4 + t:5 + t], ms[:, 4 + t:5 + t], 1, rstd_ready)
            if len(tiles) > 1:
                G.iota(slots_iota, pattern=[[1, P]], base=0, channel_multiplier=0,
                       allow_small_or_imprecise_dtypes=True).then_inc(iota_ready, 1)
            for t in tiles:
                pool.wait_ge(xs2_ready, t + 1)
                pool.dma_start(xn_d[t * P:(t + 1) * P, :], xs2[:, t, :]).then_inc(xn_stored, 16)
        pool.wait_ge(xn_stored, TT * 16)
        drained(pool, "mm", turn["mm", "ids"])

        for e in range(EXPERTS):
            b = e % 2
            if e >= 2:
                filled(pool, "tp", turn_x(e - 2) + 1)
            pool.indirect_dma_start(out=xg[:, b, :], out_offset=None, in_=xn_d,
                                    in_offset=bass.IndirectOffsetOnAxis(ap=idx[:, e:e + 1], axis=0)
                                    ).then_inc(xg_ready[b], 16)
            if e == 3:
                for t in range(CT):
                    pool.dma_start(cx[:, t, :], A["ctx_2"][0, t * P:(t + 1) * P, :]).then_inc(ctx_loaded[t], 16)
        for t in range(CT):
            pool.wait_ge(c_ms_ready, t + 1)
            power(cssq[:, 2, t:t + 1], cssq[:, 1, t:t + 1], 1, c_rstd_ready)
        pool.wait_ge(rows_ready, 1)
        pool.wait_ge(ids_zeroed, 16)
        spills = spill_count(pool)
        with pool.If(spills > 0):
            for c in range(2):
                for t in range(TT):
                    pool.indirect_dma_start(out=ids_d, out_offset=bass.IndirectOffsetOnAxis(ap=row_i[:, c, t:t + 1], axis=0),
                                            in_=tok_i[:, t:t + 1], in_offset=None).then_inc(ids_stored, 16)
            pool.wait_ge(ids_stored, 8 * 16)
        for o in range(SPILL):
            with pool.If(spills > o):
                pool.wait_ge(spill_pe, 4 * o + 1)
                pool.dma_start(idx[:, EXPERTS:EXPERTS + 1], ids_d[(EXPERTS + o) * P:(EXPERTS + o + 1) * P, :]).then_inc(spill_idx, 16)
                pool.wait_ge(spill_idx, 16 * (o + 1))
                pool.indirect_dma_start(out=xg[:, 0, :], out_offset=None, in_=xn_d,
                                        in_offset=bass.IndirectOffsetOnAxis(ap=idx[:, EXPERTS:EXPERTS + 1], axis=0)
                                        ).then_inc(spill_x, 16)
                pool.wait_ge(spill_y, 16 * (o + 2))
        pool.wait_ge(y_zeroed, 16)
        pool.wait_ge(y_stored[0], 16 * EXPERTS // 2)
        pool.wait_ge(y_stored[1], 16 * EXPERTS // 2)
        for i in range(2 * TT):
            t, c = divmod(i, 2)
            if i >= 4:
                pool.wait_ge(x2_ready, (i - 4) // 2 + 1)
            pool.indirect_dma_start(out=yg[:, i % 4, :], out_offset=None, in_=y_d,
                                    in_offset=bass.IndirectOffsetOnAxis(ap=row_i[:, c, t:t + 1], axis=0)
                                    ).then_inc(yg_ready[i % 4], 16)
        for t in range(TT):
            pool.wait_ge(ms_ready, 8 + t + 1)
            power(rstd[:, t:t + 1], ms[:, t:t + 1], 1, rstd_ready)
        for j in range(CT):
            pool.wait_ge(qk_ms_ready, QK_CHUNKS * TT + j + 1)
            power(qk_st[:, j % 2, 2, :], qk_st[:, j % 2, 1, :], 8, qk_rstd_ready)

        def bias_table(i):
            shift = (16, 8, 0)[i]
            G.tensor_tensor(bias[i].rearrange("p (h r n) -> p r h n", h=H2, r=ROWS_G), rel[:, :, :, shift:shift + KC],
                            mask[:, i, :].unsqueeze(1).unsqueeze(1).to_broadcast([P, ROWS_G, H2, KC]),
                            ALU.add).then_inc(bias_ready, 1)

        for j in range(CT, len(QK2)):
            pool.wait_ge(qk_ms_ready, QK_CHUNKS * TT + j + 1)
            power(qk_st[:, j % 2, 2, :], qk_st[:, j % 2, 1, :], 8, qk_rstd_ready)
            if j == len(QK2) - 1:
                pool.wait_ge(rel_loaded, 16 * ROWS_G)
                bias_table(0)
                bias_table(1)
                filled(pool, "mm", turn["mm", "ng", TT - 1])
                bias_table(2)


_NAMES = ["x", "norm_mix", "norm_ffn", "da_w_in", "da_q_norm", "da_k_norm", "da_lambda_q1", "da_lambda_k1",
          "da_lambda_q2", "da_lambda_k2", "da_subln", "da_w_out", "moe_w_group", "moe_b_group", "moe_w_router",
          "moe_b_router", "moe_w_gate", "moe_w_up", "moe_w_down", "c_2", "ctx_2", "c_ctx_2", "norm_g_2",
          "w_ada_2", "b_ada_2", "w_in_2", "w_four_2", "q_norm_g_2", "k_norm_g_2", "w_out_2"]


def _shape_constants():
    n = np.arange(SEQ)
    angle = 2 * np.pi * ((n[:, None] * n[None, :]) % SEQ) / SEQ
    dft = np.stack([np.cos(angle), np.sin(angle)])[:, :, 0:FREQ].astype(np.float32)
    m = np.arange(P)
    angle = 2 * np.pi * ((m[:, None] * m[None, :]) % P) / P
    scale = (SEQ * P) ** -0.5
    chan = np.stack([np.cos(angle) * scale, -np.sin(angle) * scale], axis=1).astype(np.float32)
    mask = np.zeros((P, 3, KC), np.float32)
    for tile in (0, 1, 3):
        q = tile * QC + QC - 1 - np.arange(P) % QC
        first = np.clip(q - QC // 2, 0, GRID - QC)[:, None]
        key = KEY_COL[tile] + np.arange(KC)[None, :]
        mask[:, MASK[tile], :] = np.where((key >= first) & (key < first + QC), 0.0, -BIG)
    return {"dft": dft, "chan": chan, "mask": mask}


def kernel(**inputs):
    import numpy as _np
    import concourse.bacc as _bacc
    from concourse import mybir as _mybir
    from concourse.bass_utils import run_bass_kernel_spmd as _run

    nc = _bacc.Bacc("TRN2", target_bir_lowering=False, num_devices=1)
    arrays, A = {}, {}
    for name in _NAMES:
        a = _np.ascontiguousarray(inputs[name])
        arrays[f"in_{name}"] = a
        A[name] = nc.dram_tensor(f"in_{name}", a.shape, _mybir.dt.from_np(a.dtype), kind="ExternalInput").ap()
    rel = _np.ascontiguousarray(inputs["rel_bias_2"])[0]
    rel_pad = _np.zeros((rel.shape[1], H2, REL_W), rel.dtype)
    rel_pad[:, :, 16:16 + rel.shape[2]] = rel.transpose(1, 0, 2)
    for name, a in {"rel_pad": rel_pad, **_shape_constants()}.items():
        arrays[f"in_{name}"] = a
        A[name] = nc.dram_tensor(f"in_{name}", a.shape, _mybir.dt.from_np(a.dtype), kind="ExternalInput").ap()
    out = nc.dram_tensor("out_0", (1, SEQ, D), F32, kind="ExternalOutput").ap()
    kernel_program(nc, A, out)
    r = _run(nc, [arrays], core_ids=[0])
    return r.results[0]["out_0"]
```
